# Optimizing a Trainium2 kernel written in Bass

```python
import math
import jax, jax.numpy as jnp
from jax import lax
import numpy as np

D_MODEL = 2048
BATCH = 1
SEQ = 256
DEPTH = 2

GRID_W = 64
N_MIXERS = 2
BLOCK_Q = 128
CHUNK = 128
ROPE_THETA = 10000.0
RMS_EPS = 1e-6
LN_EPS = 1e-5

A_HEADS = 16
A_KV_HEADS = 4
A_HEAD_DIM = D_MODEL // A_HEADS
A_GROUP = A_HEADS // A_KV_HEADS
A_WIDTH = A_HEADS * A_HEAD_DIM
A_KV_WIDTH = A_KV_HEADS * A_HEAD_DIM
A_IN = 2 * A_WIDTH + 2 * A_KV_WIDTH

R_HEADS = 8
R_QK_DIM = D_MODEL // R_HEADS
R_V_DIM = 2 * R_QK_DIM
R_QK_WIDTH = R_HEADS * R_QK_DIM
R_V_WIDTH = R_HEADS * R_V_DIM
R_IN = 2 * R_QK_WIDTH + 2 * R_V_WIDTH
R_DECAY_BASE = 5.0

N_A_LAYERS = (DEPTH + 1) // N_MIXERS
N_R_LAYERS = DEPTH // N_MIXERS
ALPHA = (2.0 * DEPTH) ** 0.25
BETA = (8.0 * DEPTH) ** -0.25


def axial_rope_tables(seq_len, head_dim):
    rows_n = seq_len // GRID_W
    row = jnp.repeat(jnp.arange(rows_n, dtype=jnp.float32), GRID_W)
    col = jnp.tile(jnp.arange(GRID_W, dtype=jnp.float32), rows_n)
    half = head_dim // 2
    inv_freq = ROPE_THETA ** (-jnp.arange(0, half, 2, dtype=jnp.float32) / half)
    ang_r = row[:, None] * inv_freq
    ang_c = col[:, None] * inv_freq
    ang = jnp.concatenate([ang_r, ang_r, ang_c, ang_c], axis=-1)
    return jnp.cos(ang), jnp.sin(ang)

def apply_rope(x, cos, sin):
    x32 = x.astype(jnp.float32)
    a, b, c, d = jnp.split(x32, 4, axis=-1)
    rot = jnp.concatenate([-b, a, -d, c], axis=-1)
    out = x32 * cos[None, :, None, :] + rot * sin[None, :, None, :]
    return out.astype(x.dtype)

def rms_norm(x, gain):
    x32 = x.astype(jnp.float32)
    y = x32 * lax.rsqrt(jnp.mean(x32 * x32, axis=-1, keepdims=True) + RMS_EPS)
    return (y * gain.astype(jnp.float32)).astype(x.dtype)

def layer_norm(x, gain, bias):
    x32 = x.astype(jnp.float32)
    mu = jnp.mean(x32, axis=-1, keepdims=True)
    var = jnp.mean(jnp.square(x32 - mu), axis=-1, keepdims=True)
    y = (x32 - mu) * lax.rsqrt(var + LN_EPS)
    return (y * gain.astype(jnp.float32) + bias.astype(jnp.float32)).astype(x.dtype)

def head_group_norm(x):
    x32 = x.astype(jnp.float32)
    mu = jnp.mean(x32, axis=-1, keepdims=True)
    var = jnp.mean(jnp.square(x32 - mu), axis=-1, keepdims=True)
    return ((x32 - mu) * lax.rsqrt(var + LN_EPS)).astype(x.dtype)

def attention_mixer(h, w_in, q_gain, k_gain, w_out, cos, sin):
    B, S, _ = h.shape
    proj = h @ w_in
    q, k, v, g = jnp.split(proj, [A_WIDTH, A_WIDTH + A_KV_WIDTH, A_WIDTH + 2 * A_KV_WIDTH], axis=-1)
    q = q.reshape(B, S, A_HEADS, A_HEAD_DIM)
    k = k.reshape(B, S, A_KV_HEADS, A_HEAD_DIM)
    v = v.reshape(B, S, A_KV_HEADS, A_HEAD_DIM)
    q = apply_rope(rms_norm(q, q_gain), cos, sin) * (A_HEAD_DIM ** -0.5)
    k = apply_rope(rms_norm(k, k_gain), cos, sin)
    n_blocks = S // BLOCK_Q
    qb_all = q.reshape(B, n_blocks, BLOCK_Q, A_KV_HEADS, A_GROUP, A_HEAD_DIM).transpose(1, 0, 3, 4, 2, 5)

    def block(qb):
        s = jnp.einsum('bkgqd,bskd->bkgqs', qb, k).astype(jnp.float32)
        p = jax.nn.softmax(s, axis=-1).astype(v.dtype)
        return jnp.einsum('bkgqs,bskd->bkgqd', p, v)

    o = lax.map(block, qb_all)
    o = o.transpose(1, 0, 4, 2, 3, 5).reshape(B, S, A_WIDTH)
    return (o * jax.nn.silu(g)) @ w_out

def chunk_retention(q, k, v, log_g, strict):
    B, S, H, dk = q.shape
    dv = v.shape[-1]
    nc = S // CHUNK

    def to_chunks(t):
        return t.reshape(B, nc, CHUNK, H, t.shape[-1]).transpose(1, 0, 3, 2, 4)

    qc, kc, vc = to_chunks(q), to_chunks(k), to_chunks(v)
    log_g = log_g.astype(jnp.float32)
    pos = jnp.arange(CHUNK, dtype=jnp.float32)
    diff = pos[:, None] - pos[None, :]
    mask = (diff > 0) if strict else (diff >= 0)
    intra_decay = jnp.where(mask[None], jnp.exp(log_g[:, None, None] * jnp.maximum(diff, 0.0)[None]), 0.0)
    q_decay = jnp.exp(log_g[:, None] * (pos + 1.0))[..., None]
    k_decay = jnp.exp(log_g[:, None] * (CHUNK - 1.0 - pos))[..., None]
    chunk_decay = jnp.exp(log_g * CHUNK)[:, None, None]

    def step(state, xs):
        qb, kb, vb = xs
        q32, k32, v32 = qb.astype(jnp.float32), kb.astype(jnp.float32), vb.astype(jnp.float32)
        s = jnp.einsum('bhqd,bhkd->bhqk', q32, k32) * intra_decay
        inner = jnp.einsum('bhqk,bhkv->bhqv', s, v32)
        cross = jnp.einsum('bhqd,bhdv->bhqv', q32, state) * q_decay
        new_state = state * chunk_decay + jnp.einsum('bhkd,bhkv->bhdv', k32 * k_decay, v32)
        return new_state, (inner + cross).astype(vb.dtype)

    state0 = jnp.zeros((B, H, dk, dv), jnp.float32)
    _, out = lax.scan(step, state0, (qc, kc, vc))
    return out.transpose(1, 0, 3, 2, 4).reshape(B, S, H, dv)

def retention_mixer(h, w_in, decay_exp, w_out, cos, sin):
    B, S, _ = h.shape
    proj = h @ w_in
    q, k, v, g = jnp.split(proj, [R_QK_WIDTH, 2 * R_QK_WIDTH, 2 * R_QK_WIDTH + R_V_WIDTH], axis=-1)
    q = apply_rope(q.reshape(B, S, R_HEADS, R_QK_DIM), cos, sin)
    k = apply_rope(k.reshape(B, S, R_HEADS, R_QK_DIM), cos, sin) * (R_QK_DIM ** -0.5)
    v = v.reshape(B, S, R_HEADS, R_V_DIM)
    log_g = jnp.log1p(-jnp.exp2(-decay_exp.astype(jnp.float32)))
    fwd = chunk_retention(q, k, v, log_g[0], strict=False)
    bwd = jnp.flip(chunk_retention(jnp.flip(q, 1), jnp.flip(k, 1), jnp.flip(v, 1), log_g[1], strict=True), 1)
    o = head_group_norm(fwd + bwd).reshape(B, S, R_V_WIDTH)
    return (o * jax.nn.silu(g)) @ w_out

def first_inputs(seed: int = 0) -> dict:
    key = jax.random.key(seed)
    ks = jax.random.split(key, 12)
    f32 = jnp.float32
    x = jax.random.normal(ks[0], (BATCH, SEQ, D_MODEL), f32)

    a_col_scale = jnp.concatenate([jnp.ones((A_WIDTH + A_KV_WIDTH,), f32),
                                   jnp.full((A_KV_WIDTH,), BETA, f32),
                                   jnp.ones((A_WIDTH,), f32)])
    attn_w_in = jax.random.normal(ks[1], (N_A_LAYERS, D_MODEL, A_IN), f32) * (D_MODEL ** -0.5) * a_col_scale
    attn_q_gain = 1.0 + 0.02 * jax.random.normal(ks[2], (N_A_LAYERS, A_HEAD_DIM), f32)
    attn_k_gain = 1.0 + 0.02 * jax.random.normal(ks[3], (N_A_LAYERS, A_HEAD_DIM), f32)
    attn_w_out = jax.random.normal(ks[4], (N_A_LAYERS, A_WIDTH, D_MODEL), f32) * (A_WIDTH ** -0.5) * BETA

    r_col_scale = jnp.concatenate([jnp.ones((2 * R_QK_WIDTH,), f32),
                                   jnp.full((R_V_WIDTH,), BETA, f32),
                                   jnp.ones((R_V_WIDTH,), f32)])
    ret_w_in = jax.random.normal(ks[5], (N_R_LAYERS, D_MODEL, R_IN), f32) * (D_MODEL ** -0.5) * r_col_scale
    base = R_DECAY_BASE + jnp.arange(R_HEADS, dtype=f32)
    base2 = jnp.stack([base, base[::-1]], axis=0)
    ret_decay_exp = base2[None] + 0.1 * jax.random.normal(ks[6], (N_R_LAYERS, 2, R_HEADS), f32)
    ret_w_out = jax.random.normal(ks[7], (N_R_LAYERS, R_V_WIDTH, D_MODEL), f32) * (R_V_WIDTH ** -0.5) * BETA

    ln_gain = 1.0 + 0.02 * jax.random.normal(ks[8], (DEPTH, D_MODEL), f32)
    ln_bias = 0.02 * jax.random.normal(ks[9], (DEPTH, D_MODEL), f32)
    return {"x": x, "attn_w_in": attn_w_in, "attn_q_gain": attn_q_gain, "attn_k_gain": attn_k_gain,
            "attn_w_out": attn_w_out, "ret_w_in": ret_w_in, "ret_decay_exp": ret_decay_exp,
            "ret_w_out": ret_w_out, "ln_gain": ln_gain, "ln_bias": ln_bias}

def first_block(x, attn_w_in, attn_q_gain, attn_k_gain, attn_w_out, ret_w_in, ret_decay_exp,
              ret_w_out, ln_gain, ln_bias):
    S = x.shape[1]
    cos_a, sin_a = axial_rope_tables(S, A_HEAD_DIM)
    cos_r, sin_r = axial_rope_tables(S, R_QK_DIM)
    for i in range(DEPTH):
        j = i // N_MIXERS
        if i % N_MIXERS == 0:
            y = attention_mixer(x, attn_w_in[j], attn_q_gain[j], attn_k_gain[j], attn_w_out[j], cos_a, sin_a)
        else:
            y = retention_mixer(x, ret_w_in[j], ret_decay_exp[j], ret_w_out[j], cos_r, sin_r)
        x = layer_norm(ALPHA * x + y, ln_gain[i], ln_bias[i])
    return x


DEPTH_2 = 1

HEAD_DIM = 64
A_KV_HEADS_2 = 2
WINDOW = 128
BLOCK = 128
B_HEADS = 16
KV_RANK = 256
IDX_HEADS = 16
IDX_DIM = 64
TOPK_MAX = 256
NUM_BUCKETS = 32
MAX_DISTANCE = 128
D_FF = 5632
CONV_WIDTH = 3
EPS = 1e-6
NEG_INF = -1e30
IDX_SCALE = IDX_DIM ** -0.5 * IDX_HEADS ** -0.5
MIX_WIDTH = (A_HEADS + B_HEADS) * HEAD_DIM

A_Q = A_HEADS * HEAD_DIM
A_KV = A_KV_HEADS_2 * HEAD_DIM
B_Q = B_HEADS * HEAD_DIM
I_Q = IDX_HEADS * IDX_DIM
IN_WIDTH = A_Q + 2 * A_KV + B_Q + KV_RANK + I_Q + IDX_DIM + IDX_HEADS
SPLIT_POINTS = (
    A_Q,
    A_Q + A_KV,
    A_Q + 2 * A_KV,
    A_Q + 2 * A_KV + B_Q,
    A_Q + 2 * A_KV + B_Q + KV_RANK,
    A_Q + 2 * A_KV + B_Q + KV_RANK + I_Q,
    A_Q + 2 * A_KV + B_Q + KV_RANK + I_Q + IDX_DIM,
)


def rms_norm_2(x, g):
    xf = x.astype(jnp.float32)
    y = xf * lax.rsqrt(jnp.mean(xf * xf, axis=-1, keepdims=True) + EPS)
    return (y * g.astype(jnp.float32)).astype(x.dtype)

def rel_bucket(dist):
    n = jnp.maximum(dist, 0)
    max_exact = NUM_BUCKETS // 2
    nf = jnp.maximum(n, 1).astype(jnp.float32)
    large = max_exact + (jnp.log(nf / max_exact) / math.log(MAX_DISTANCE / max_exact)
                         * (NUM_BUCKETS - max_exact)).astype(jnp.int32)
    large = jnp.minimum(large, NUM_BUCKETS - 1)
    return jnp.where(n < max_exact, n, large)

def swa_attention(q, k, v, sinks, rel_table):
    Bsz, T, H, D = q.shape
    nblk = T // BLOCK
    G = H // A_KV_HEADS_2
    qb = q.reshape(Bsz, nblk, BLOCK, A_KV_HEADS_2, G, D)
    pad = ((0, 0), (BLOCK, 0), (0, 0), (0, 0))
    kp = jnp.pad(k, pad).reshape(Bsz, nblk + 1, BLOCK, A_KV_HEADS_2, D)
    vp = jnp.pad(v, pad).reshape(Bsz, nblk + 1, BLOCK, A_KV_HEADS_2, D)
    kb = jnp.concatenate([kp[:, :-1], kp[:, 1:]], axis=2)
    vb = jnp.concatenate([vp[:, :-1], vp[:, 1:]], axis=2)
    s = jnp.einsum('bnqkgd,bnskd->bnkgqs', qb, kb).astype(jnp.float32) * (D ** -0.5)
    i = jnp.arange(BLOCK, dtype=jnp.int32)[:, None]
    j = jnp.arange(2 * BLOCK, dtype=jnp.int32)[None, :]
    dist = i + BLOCK - j
    in_window = (dist >= 0) & (dist < WINDOW)
    key_pos = jnp.arange(nblk, dtype=jnp.int32)[:, None, None] * BLOCK - BLOCK + j[None]
    valid = in_window[None] & (key_pos >= 0)
    bias = jnp.transpose(rel_table[rel_bucket(dist)], (2, 0, 1))
    bias = bias.reshape(A_KV_HEADS_2, G, BLOCK, 2 * BLOCK).astype(jnp.float32)
    s = jnp.where(valid[None, :, None, None], s + bias[None, None], NEG_INF)
    sink = sinks.astype(jnp.float32).reshape(A_KV_HEADS_2, G)[None, None, :, :, None, None]
    m = jnp.maximum(jnp.max(s, axis=-1, keepdims=True), sink)
    e = jnp.exp(s - m)
    p = e / (jnp.sum(e, axis=-1, keepdims=True) + jnp.exp(sink - m))
    o = jnp.einsum('bnkgqs,bnskd->bnqkgd', p.astype(v.dtype), vb)
    return o.reshape(Bsz, T, H * D)

def dsa_attention(q, c_kv, w_uk, w_uv, q_idx, k_idx, w_idx, rel_table):
    Bsz, T, H, D = q.shape
    nblk = T // BLOCK
    topk = min(TOPK_MAX, T // 4)
    scale = D ** -0.5
    key_pos = jnp.arange(T, dtype=jnp.int32)

    def one_block(blk):
        start = blk * BLOCK
        qpos = start + jnp.arange(BLOCK, dtype=jnp.int32)
        qi = lax.dynamic_slice_in_dim(q_idx, start, BLOCK, axis=1)
        wi = lax.dynamic_slice_in_dim(w_idx, start, BLOCK, axis=1)
        qb = lax.dynamic_slice_in_dim(q, start, BLOCK, axis=1)
        dots = jnp.einsum('bqhd,bsd->bqhs', qi, k_idx).astype(jnp.float32)
        index_score = jnp.einsum('bqh,bqhs->bqs', wi.astype(jnp.float32),
                                 jax.nn.relu(dots)) * IDX_SCALE
        causal = key_pos[None, :] <= qpos[:, None]
        index_score = jnp.where(causal[None], index_score, NEG_INF)
        _, sel = lax.top_k(index_score, topk)
        c_sel = jax.vmap(lambda ck, ix: ck[ix])(c_kv, sel)
        q_lat = jnp.einsum('bqhd,hrd->bqhr', qb, w_uk)
        s = jnp.einsum('bqhr,bqkr->bqhk', q_lat, c_sel).astype(jnp.float32) * scale
        dist = qpos[None, :, None] - sel
        bias = jnp.moveaxis(rel_table[rel_bucket(dist)], -1, 2).astype(jnp.float32)
        s = jnp.where((dist >= 0)[:, :, None, :], s + bias, NEG_INF)
        p = jax.nn.softmax(s, axis=-1).astype(c_sel.dtype)
        o_lat = jnp.einsum('bqhk,bqkr->bqhr', p, c_sel)
        o = jnp.einsum('bqhr,hrd->bqhd', o_lat, w_uv)
        return o.reshape(Bsz, BLOCK, H * D)

    out = lax.map(one_block, jnp.arange(nblk, dtype=jnp.int32))
    return jnp.transpose(out, (1, 0, 2, 3)).reshape(Bsz, T, H * D)

def conv_ffn(h, w_up, conv_w, conv_b, w_down):
    u, g = jnp.split(h @ w_up, 2, axis=-1)
    u = lax.conv_general_dilated(
        u, conv_w[:, None, :], window_strides=(1,), padding=((CONV_WIDTH - 1, 0),),
        dimension_numbers=('NWC', 'WIO', 'NWC'), feature_group_count=D_FF) + conv_b
    return (jax.nn.silu(u) * g) @ w_down

def second_inputs(seed: int = 0) -> dict:
    key = jax.random.key(seed)
    ks = jax.random.split(key, 20)
    f32 = jnp.float32
    nrm = lambda k, shape, s: jax.random.normal(k, shape, f32) * s
    return {
        "x": nrm(ks[0], (BATCH, SEQ, D_MODEL), 1.0),
        "c": nrm(ks[1], (BATCH, D_MODEL), 1.0),
        "w_mod": nrm(ks[2], (DEPTH_2, D_MODEL, 6 * D_MODEL), D_MODEL ** -0.5),
        "b_mod": nrm(ks[3], (DEPTH_2, 6 * D_MODEL), 0.02),
        "norm_attn": 1.0 + nrm(ks[4], (DEPTH_2, D_MODEL), 0.02),
        "w_in": nrm(ks[5], (DEPTH_2, D_MODEL, IN_WIDTH), D_MODEL ** -0.5),
        "attn_sinks": nrm(ks[6], (DEPTH_2, A_HEADS), 0.5),
        "kv_norm": 1.0 + nrm(ks[7], (DEPTH_2, KV_RANK), 0.02),
        "w_uk": nrm(ks[8], (DEPTH_2, B_HEADS, KV_RANK, HEAD_DIM), KV_RANK ** -0.5),
        "w_uv": nrm(ks[9], (DEPTH_2, B_HEADS, KV_RANK, HEAD_DIM), KV_RANK ** -0.5),
        "rel_bias": nrm(ks[10], (NUM_BUCKETS, A_HEADS + B_HEADS), 0.3),
        "w_out": nrm(ks[11], (DEPTH_2, MIX_WIDTH, D_MODEL), MIX_WIDTH ** -0.5),
        "norm_ffn": 1.0 + nrm(ks[12], (DEPTH_2, D_MODEL), 0.02),
        "w_up": nrm(ks[13], (DEPTH_2, D_MODEL, 2 * D_FF), D_MODEL ** -0.5),
        "conv_w": nrm(ks[14], (DEPTH_2, CONV_WIDTH, D_FF), CONV_WIDTH ** -0.5),
        "conv_b": nrm(ks[15], (DEPTH_2, D_FF), 0.02),
        "w_down": nrm(ks[16], (DEPTH_2, D_FF, D_MODEL), D_FF ** -0.5),
        "norm_final": 1.0 + nrm(ks[17], (D_MODEL,), 0.02),
    }

def second_block(x, c, w_mod, b_mod, norm_attn, w_in, attn_sinks, kv_norm, w_uk, w_uv,
              rel_bias, w_out, norm_ffn, w_up, conv_w, conv_b, w_down, norm_final):
    Bsz, T, _ = x.shape
    rel_a = rel_bias[:, :A_HEADS]
    rel_b = rel_bias[:, A_HEADS:]
    c_act = jax.nn.silu(c)
    for l in range(DEPTH_2):
        mod = c_act @ w_mod[l] + b_mod[l]
        sh1, sc1, g1, sh2, sc2, g2 = [m[:, None, :] for m in jnp.split(mod, 6, axis=-1)]

        h = rms_norm_2(x, norm_attn[l]) * (1.0 + sc1) + sh1
        qa, ka, va, qb, ckv, qi, ki, wi = jnp.split(h @ w_in[l], SPLIT_POINTS, axis=-1)
        qa = qa.reshape(Bsz, T, A_HEADS, HEAD_DIM)
        ka = ka.reshape(Bsz, T, A_KV_HEADS_2, HEAD_DIM)
        va = va.reshape(Bsz, T, A_KV_HEADS_2, HEAD_DIM)
        qb = qb.reshape(Bsz, T, B_HEADS, HEAD_DIM)
        ckv = rms_norm_2(ckv, kv_norm[l])
        qi = qi.reshape(Bsz, T, IDX_HEADS, IDX_DIM)
        out_a = swa_attention(qa, ka, va, attn_sinks[l], rel_a)
        out_b = dsa_attention(qb, ckv, w_uk[l], w_uv[l], qi, ki, wi, rel_b)
        mix = jnp.concatenate([out_a, out_b], axis=-1) @ w_out[l]
        x = x + g1 * mix

        h = rms_norm_2(x, norm_ffn[l]) * (1.0 + sc2) + sh2
        x = x + g2 * conv_ffn(h, w_up[l], conv_w[l], conv_b[l], w_down[l])
    return rms_norm_2(x, norm_final)


def setup_inputs(seed=0):
    out = dict(first_inputs(seed))
    for name, value in second_inputs(seed + 1).items():
        if name != "x":
            out[name + "_2"] = value
    return out


def reference(
    x, attn_w_in, attn_q_gain, attn_k_gain, attn_w_out, ret_w_in, ret_decay_exp, ret_w_out,
    ln_gain, ln_bias, c_2, w_mod_2, b_mod_2, norm_attn_2, w_in_2, attn_sinks_2, kv_norm_2,
    w_uk_2, w_uv_2, rel_bias_2, w_out_2, norm_ffn_2, w_up_2, conv_w_2, conv_b_2, w_down_2,
    norm_final_2,
):
    x = first_block(
        x, attn_w_in, attn_q_gain, attn_k_gain, attn_w_out, ret_w_in, ret_decay_exp, ret_w_out,
        ln_gain, ln_bias,
    )
    return second_block(
        x, c_2, w_mod_2, b_mod_2, norm_attn_2, w_in_2, attn_sinks_2, kv_norm_2, w_uk_2, w_uv_2,
        rel_bias_2, w_out_2, norm_ffn_2, w_up_2, conv_w_2, conv_b_2, w_down_2, norm_final_2,
    )


_drawn_inputs = setup_inputs


def setup_inputs(seed=0):
    import zlib

    import numpy as np

    out = dict(_drawn_inputs(seed))
    spreads = {}
    factors = {'attn_q_gain': 8.0,
     'attn_k_gain': 8.0,
     'attn_w_out': 3.661,
     'norm_attn_2': 3.926,
     'attn_sinks_2': 20.37,
     'kv_norm_2': 8.0,
     'norm_ffn_2': 3.913,
     'conv_b_2': 7.16,
     'norm_final_2': 7.725}
    for name, (base, spread) in spreads.items():
        noise = np.random.default_rng([zlib.crc32(name.encode()), seed]).standard_normal(out[name].shape)
        drawn = base * np.exp(spread * noise) if base else spread * noise
        out[name] = __import__('jax').numpy.asarray(drawn.astype(out[name].dtype))
    for name, factor in factors.items():
        out[name] = (out[name] * factor).astype(out[name].dtype)
    return out
```

```python
from contextlib import ExitStack

import numpy as np
import concourse.bass as bass
from concourse import mybir

F32 = mybir.dt.float32
F32R = mybir.dt.float32r
ALU = mybir.AluOpType
ACT = mybir.ActivationFunctionType
AX = mybir.AxisListType.X

P = 128
D = 2048
T = 256
NT = T // P
KC = D // P
CB = 512
CH = 4
NEG = -1e30

A_HD, A_KV = 128, 4
R_HEADS, R_DK, R_DV = 8, 256, 512
W_HD, W_HEADS = 64, 16
RANK, TOPK, WINDOW = 256, 64, 128
FF = 5632
FG = FF // CB
ALPHA = 4.0 ** 0.25
LN_EPS, RMS_EPS = 1e-5, 1e-6
MOD_BLOCKS = 6 * D // CB
TOEP = 384
VEC_A, VEC_R, VEC_F = 45, 37, 16

INDEX_HEADS = {1: range(0, 4), 2: range(4, 9), 3: range(9, 16)}
A_B0 = 0
R_B0 = A_B0 + 4 * A_KV
B_B0 = R_B0 + 4 * R_HEADS
F_B0 = B_B0 + 12


def rope_tables(head_dim):
    pos = np.arange(T)
    row, col = (pos // 64).astype(np.float32), (pos % 64).astype(np.float32)
    half = head_dim // 2
    inv = (np.float32(10000.0) ** (-np.arange(0, half, 2, dtype=np.float32) / np.float32(half))).astype(np.float32)
    ar, ac = row[:, None] * inv, col[:, None] * inv
    ang = np.concatenate([ar, ar, ac, ac], axis=-1)
    sign = np.repeat(np.array([-1, 1, -1, 1], np.float32), head_dim // 4)
    return np.cos(ang).astype(np.float32), (np.sin(ang) * sign).astype(np.float32)


def shape_constants():
    cos_a, sin_a = rope_tables(A_HD)
    cos_r, sin_r = rope_tables(R_DK)
    s, t = np.arange(T)[:, None], np.arange(T)[None, :]
    ahead = np.maximum(t - s, 0).astype(np.float32)
    behind = np.maximum(s - t, 0).astype(np.float32)
    dist = 255 - np.arange(TOEP)
    n = np.maximum(dist, 0)
    nf = np.maximum(n, 1).astype(np.float32)
    large = 16 + (np.log(nf / np.float32(16)) / np.float32(np.log(128 / 16)) * np.float32(16)).astype(np.int32)
    bucket = np.where(n < 16, n, np.minimum(large, 31))
    onehot = (np.arange(32)[:, None] == bucket[None, :]).astype(np.float32)
    ok = np.stack([(dist >= 0) & (dist < WINDOW)] * W_HEADS + [dist >= 0] * W_HEADS)
    onehot *= (dist >= 0)[None, :]
    mask = np.where(ok, 0.0, NEG).astype(np.float32)
    i = np.arange(P)[:, None]
    causal = np.concatenate([np.where(np.arange(P)[None, :] <= i, 0.0, NEG),
                             np.where(np.arange(T)[None, :] <= i + P, 0.0, NEG)], axis=1).astype(np.float32)
    return {"ident": np.eye(P, dtype=np.float32), "cos_a": cos_a, "sin_a": sin_a, "cos_r": cos_r,
            "sin_r": sin_r, "ahead": ahead, "behind": behind, "onehot": onehot, "mask": mask,
            "causal": causal}


class Count:

    def __init__(self):
        self.n, self.reg = 0, None

    def one(self):
        self.n += 1
        return 1

    def now(self):
        return self.n if self.reg is None else self.n + self.reg

    def enter(self, index, first, per):
        self.start, self.per, self.reg = self.n, per, per * (index - first)

    def leave(self, trips):
        assert self.n - self.start == self.per, (self.n - self.start, self.per)
        self.n, self.reg = self.start + self.per * trips, None


def build(nc, x, attn_w_in, attn_q_gain, attn_k_gain, attn_w_out, ret_w_in, ret_decay_exp,
          ret_w_out, ln_gain, ln_bias, c_2, w_mod_2, b_mod_2, norm_attn_2, w_in_2, attn_sinks_2,
          kv_norm_2, w_uk_2, w_uv_2, rel_bias_2, w_out_2, norm_ffn_2, w_up_2, conv_w_2, conv_b_2,
          w_down_2, norm_final_2, ident_c, cos_a_c, sin_a_c, cos_r_c, sin_r_c, ahead_c, behind_c,
          onehot_c, mask_c, causal_c, out):
    ctx = ExitStack()
    with ctx:
        at = {"byte": 16512}

        def take(name, shape, dtype=F32):
            t = nc.alloc_sbuf_tensor_at(name, [P, *shape], dtype, offset=at["byte"])
            at["byte"] += -(-4 * int(np.prod(shape)) // 32) * 32
            return t

        def over(name, base, shape, dtype):
            return nc.alloc_sbuf_tensor_at(name, [P, *shape], dtype, offset=base)

        raw_at = at["byte"]
        raw = take("raw", [CH, CH, CB])
        w_lo = over("w_lo", raw_at, [CH, CH, CB], F32R)
        w_hi = take("w_hi", [CH, CH, CB], F32R)
        x_hi = take("x_hi", [KC, T], F32R)
        x_lo_at = at["byte"]
        x_lo = take("x_lo", [KC, T], F32R)
        b_tmp = over("b_tmp", x_lo_at, [NT, CB], F32)
        x_mid = over("x_mid", x_lo_at, [KC, T], F32)
        z = take("z", [NT, D])
        rows = take("rows", [2, D])
        ident = take("ident", [P])
        ones = take("ones", [P])
        par = take("par", [82])
        bmod = take("bmod", [6 * KC])
        modc = take("modc", [6 * KC])
        csilu = take("csilu", [KC])
        aff = take("aff", [KC])
        stats = take("stats", [NT, 4, 6])
        mv = take("mv", [NT, 2])
        rstd = take("rstd", [NT])
        var = take("var", [NT])
        spare = take("spare", [1])
        minus_half = take("minus_half", [8])
        nmr = take("nmr", [NT])
        ssq = take("ssq", [NT, 4])
        diag = take("diag", [NT, P])
        conv = take("conv", [FF // P, 4])
        arena = at["byte"]

        cos_q, sin_q = take("cos_q", [NT, A_HD]), take("sin_q", [NT, A_HD])
        cos_k, sin_k = take("cos_k", [NT, A_HD]), take("sin_k", [NT, A_HD])
        ropet = take("ropet", [CB])
        a_sq = take("a_sq", [NT, CB])
        a_ss, a_rs = take("a_ss", [2, NT, 4]), take("a_rs", [2, NT, 4])
        a_q, a_k = take("a_q", [NT, CB]), take("a_k", [NT, A_HD])
        a_v = take("a_v", [NT, A_HD])
        a_qT, a_kT = take("a_qT", [4, T]), take("a_kT", [T])
        a_p_at = at["byte"]
        a_p = take("a_p", [4, NT, T])
        a_pT = take("a_pT", [2, NT, T])
        a_nmax, a_sum, a_rinv = take("a_nmax", [4, NT]), take("a_sum", [4, NT]), take("a_rinv", [4, NT])
        a_sg, a_og = take("a_sg", [NT, CB]), take("a_og", [NT, CB])
        a_oh, a_ol = take("a_oh", [4, T], F32R), take("a_ol", [4, T], F32R)
        a_end = at["byte"]

        at["byte"] = arena
        cos_r, sin_r = take("cos_r", [NT, R_DK]), take("sin_r", [NT, R_DK])
        r_decay = take("r_decay", [R_HEADS, NT, T])
        r_t = take("r_t", [CB])
        r_qk, r_v = take("r_qk", [NT, CB]), take("r_v", [NT, R_DV])
        r_sg, r_og = take("r_sg", [NT, R_DV]), take("r_og", [NT, R_DV])
        r_qT, r_kT, r_s = take("r_qT", [2, T]), take("r_kT", [2, T]), take("r_s", [NT, T])
        r_oh, r_ol = take("r_oh", [4, T], F32R), take("r_ol", [4, T], F32R)
        r_st, r_mv, r_rs = take("r_st", [NT, 6]), take("r_mv", [NT, 2]), take("r_rs", [NT])
        r_var = take("r_var", [NT])
        r_end = at["byte"]
        at["byte"] = arena
        _ = take("skip0", [4 * R_DK + R_HEADS * NT * T])
        r_pos = take("r_pos", [2, NT, T])
        r_e, r_u = take("r_e", [16]), take("r_u", [16])
        r_lg, r_m, r_n = take("r_lg", [16]), take("r_m", [16]), take("r_n", [16])
        at["byte"] = max(a_end, r_end)

        mod_at = at["byte"]
        m_raw = take("m_raw", [2, CH, CB])
        m_acc = take("m_acc", [2, CB])
        top = at["byte"]
        assert top <= 229344, top

        at["byte"] = arena
        b_kBT = take("b_kBT", [8, T])
        b_vB = take("b_vB", [NT, W_HEADS * W_HD])
        b_kaT = take("b_kaT", [2, T])
        b_va = take("b_va", [NT, P])
        b_bias = take("b_bias", [8, 384])
        b_q = take("b_q", [NT, CB])
        b_qT = take("b_qT", [4, T])
        b_s_at = at["byte"]
        b_s = take("b_s", [4, 384])
        junk2_at = at["byte"]
        b_pT = take("b_pT", [2, 384])
        b_o = take("b_o", [NT, CB])
        b_ckvT = take("b_ckvT", [2, T])
        b_idx, b_sel = take("b_idx", [384]), take("b_sel", [384])
        b_max8 = take("b_max8", [NT, 8])
        b_w = take("b_w", [NT, 16])
        b_sink, b_nsink = take("b_sink", [16]), take("b_nsink", [16])
        b_nm, b_sum, b_es, b_ri = (take(n, [8, NT]) for n in ("b_nm", "b_sum", "b_es", "b_ri"))
        oT_at = at["byte"]
        b_oh, b_ol = take("b_oh", [2, 4, T], F32R), take("b_ol", [2, 4, T], F32R)
        b_end = at["byte"]
        assert b_end <= 229344, b_end
        b_wuk = over("b_wuk", oT_at, [2, W_HEADS * W_HD], F32)
        b_wuv = over("b_wuv", oT_at + 8192, [2, W_HEADS * W_HD], F32)
        at["byte"] = arena
        i_qT = take("i_qT", [8, T])
        i_kdup, i_kT = take("i_kdup", [NT, P]), take("i_kT", [T])
        i_relu = take("i_relu", [2, 384])
        i_end = at["byte"]
        assert i_end <= arena + 16384
        at["byte"] = arena + 16384 + 2048 + 1024
        i_q = take("i_q", [NT, CB])
        b_kvc = take("b_kvc", [NT, CB])
        b_kadup = take("b_kadup", [NT, 2, P])

        b_cvar, b_crs = take("b_cvar", [NT]), take("b_crs", [NT])
        junk = over("junk", arena, [D], F32)
        junk2 = over("junk2", junk2_at, [T], F32)
        gate_diag = over("gate_diag", b_s_at, [2, 4, P], F32)

        at["byte"] = arena
        f_u, f_g = take("f_u", [NT, CB]), take("f_g", [NT, CB])
        f_c, f_h = take("f_c", [4, T]), take("f_h", [4, T])
        f_par = take("f_par", [4, 4])
        f_hh, f_hl = take("f_hh", [4, T], F32R), take("f_hl", [4, T], F32R)
        f_y = take("f_y", [NT, CB])
        par_rows, bmod_rows = over("par_rows", a_p_at, [P], F32), over("bmod_rows", a_p_at + 512, [P], F32)
        conv_rows = over("conv_rows", a_p_at + 1024, [2, P], F32)
        at["byte"] = mod_at
        t_hot = nc.alloc_sbuf_tensor_at("t_hot", [32, TOEP], F32, offset=mod_at + 16384)
        t_mask = nc.alloc_sbuf_tensor_at("t_mask", [32, TOEP], F32, offset=mod_at + 16384 + 1536)
        t_rel = nc.alloc_sbuf_tensor_at("t_rel", [32, 32], F32, offset=a_end - 4096)
        t_out = nc.alloc_sbuf_tensor_at("t_out", [32, TOEP], F32, offset=a_end - 8192)

        toep = nc.dram_tensor("toeplitz_rows", (32, P, TOEP), F32, kind="Internal").ap()

        def bank(name):
            return ctx.enter_context(nc.psum_tensor(name, [P, CB], F32))

        pair = [[bank("pair0_t0"), bank("pair0_t1")], [bank("pair1_t0"), bank("pair1_t1")]]
        turn = [bank("turn0"), bank("turn1")]
        sc = [bank("sc0"), bank("sc1")]

        S = {}

        def sem(name):
            if name not in S:
                S[name] = ctx.enter_context(nc.semaphore(name))
            return S[name]

        def gview(ap, n):
            return ap.rearrange("p (n w) -> p n w", n=n)

        def swapped(ap, groups, width, part):
            v = ap.rearrange("p (g h s w) -> p g h s w", g=groups, h=2, s=2, w=width)
            return v[:, :, :, part, :]

        def cast(ap, groups):
            w = ap.shape[-1]
            return ap.unsqueeze(1).to_broadcast([P, groups, w])

        w_attn = attn_w_in[0].rearrange("(k p) n -> p k n", p=P)
        w_attn_out = attn_w_out[0].rearrange("(k p) n -> p k n", p=P)
        w_ret = ret_w_in[0].rearrange("(k p) n -> p k n", p=P)
        w_ret_out = ret_w_out[0].rearrange("(k p) n -> p k n", p=P)
        w_b = w_in_2[0].rearrange("(k p) n -> p k n", p=P)
        w_b_out = w_out_2[0].rearrange("(k p) n -> p k n", p=P)
        w_f = w_up_2[0].rearrange("(k p) n -> p k n", p=P)
        w_f_out = w_down_2[0].rearrange("(k p) n -> p k n", p=P)
        w_m = w_mod_2[0].rearrange("(k p) n -> p k n", p=P)

        def cols(w, first, width=CB):
            return lambda c: w[:, CH * c:CH * c + CH, bass.ds(first, width)]

        def two(w, lo, hi, step, first, width):
            v = w[:, :, lo:hi].rearrange("p k (s n) -> p k s n", n=step)
            return lambda c: v[:, CH * c:CH * c + CH, :, bass.ds(first, width)]

        def out_rows(w, g):
            return lambda c: w[:, bass.ds(CH * g, CH), c * CB:(c + 1) * CB]

        a_blocks = [lambda g: cols(w_attn, g * CB),
                    lambda g: two(w_attn, D, D + 2 * CB, CB, g * A_HD, A_HD),
                    lambda g: cols(w_attn, D + 2 * CB + g * CB)]
        r_blocks = [lambda g: two(w_ret, 0, 2 * D, D, g * R_DK, R_DK),
                    lambda g: cols(w_ret, 2 * D + g * CB),
                    lambda g: cols(w_ret, 4 * D + g * CB)]
        f_blocks = [lambda g: cols(w_f, g * CB), lambda g: cols(w_f, FF + g * CB)]
        b_blocks = [cols(w_b, 2560), cols(w_b, 3072), cols(w_b, 3584, 80),
                    two(w_b, 1024, 3584, 1280, 0, 256), cols(w_b, 0), cols(w_b, 512),
                    cols(w_b, 1280), cols(w_b, 1792), *(out_rows(w_b_out, g) for g in range(4))]
        b_width = [CB, CB, 80] + [CB] * 9

        def chunk(t, c, width=CB):
            return t[:, c, :, 0:width]

        def load(sp, b, source, width=CB, halves=False):
            for c in range(CH):
                if not isinstance(b, int) or b > 0:
                    sp.wait_ge(sem("products"), CH * b + c - CH + 1)
                for h in range(2):
                    if halves:
                        to = raw[:, c, :, h * width // 2:(h + 1) * width // 2]
                        src = source(c)[:, :, h, :]
                    else:
                        to = raw[:, c, 2 * h:2 * h + 2, 0:width]
                        src = source(c)[:, 2 * h:2 * h + 2, :]
                    sp.dma_start(to, src).then_inc(sem(f"chunk_in{c}"), 16)

        def round_hi(act, b, c, width=CB):
            act.wait_ge(sem(f"chunk_in{c}"), 32 * (b + 1))
            act.activation(chunk(w_hi, c, width), chunk(raw, c, width), ACT.Copy).then_inc(sem("hi"), 1)

        def split_lo(v, b, c, width=CB):
            v.wait_ge(sem("hi"), CH * b + c + 1)
            v.tensor_tensor(chunk(w_lo, c, width), chunk(raw, c, width),
                            chunk(w_hi, c, width).bitcast(F32), ALU.subtract).then_inc(sem("lo"), 1)

        def product(pe, to, xh, xl, c, k, width, start, stop):
            wh, wl = w_hi[:, c, k, 0:width], w_lo[:, c, k, 0:width]
            pe.matmul(to, xh, wh, start=start, stop=False)
            pe.matmul(to, xh, wl, start=False, stop=False)
            return pe.matmul(to, xl, wh, start=False, stop=stop)

        def project(pe, b, banks, width=CB, before=None, after=None):
            for c in range(CH):
                if before:
                    before(c)
                pe.wait_ge(sem("lo"), CH * b + c + 1)
                for k in range(CH):
                    kk = CH * c + k
                    for t in range(NT):
                        mm = product(pe, banks[t][:, 0:width], x_hi[:, kk, t * P:(t + 1) * P],
                                     x_lo[:, kk, t * P:(t + 1) * P], c, k, width,
                                     kk == 0, kk == KC - 1)
                mm.then_inc(sem("products"), 1)
                if after:
                    after(c)

        def output(pe, b, oh, ol, order, before, after=None):
            for c in range(CH):
                before(c)
                pe.wait_ge(sem("lo"), CH * b + c + 1)
                for t in range(NT):
                    for k in range(CH):
                        mm = product(pe, pair[order[c]][t][:, :], oh[:, k, t * P:(t + 1) * P],
                                     ol[:, k, t * P:(t + 1) * P], c, k, CB, k == 0, k == CH - 1)
                mm.then_inc(sem("products"), 1)
                if after:
                    after(c)

        turn_bank = [turn[0], turn[1], sc[0], sc[1], pair[1][0], pair[1][1]]

        def turn_groups(pe, n, ready, scaled):
            for j in range(KC // 2):
                ready(j)
                if j >= 6 and n == 0:
                    pe.wait_ge(sem("turn_lo"), j - 6 + 1)
                elif j >= 6:
                    pe.wait_ge(sem("turn_mid"), 8 * (n - 1) + j - 6 + 1)
                for k in range(2):
                    for t in range(NT):
                        to = turn_bank[j % 6][:, k * T + t * P:k * T + (t + 1) * P]
                        src = z[:, t, (2 * j + k) * P:(2 * j + k + 1) * P]
                        if scaled:
                            mm = pe.matmul(to, src, diag[:, t, :], start=True, stop=True)
                        else:
                            mm = pe.transpose(to, src, ident[:, :])
                mm.then_inc(sem("turned"), 1)

        def turn_hi(act, n, plain):
            for j in range(KC // 2):
                if plain:
                    act.wait_ge(sem("turned"), 8 * n + j + 1)
                    src = gview(turn_bank[j % 6][:, :], 2)
                else:
                    act.wait_ge(sem("turn_mid"), 8 * (n - 1) + j + 1)
                    src = x_mid[:, 2 * j:2 * j + 2, :]
                act.activation(x_hi[:, 2 * j:2 * j + 2, :], src, ACT.Copy).then_inc(sem("turn_hi"), 1)

        def turn_lo(v, n, gain=None, bias=None):
            def low(j, src):
                v.wait_ge(sem("turn_hi"), 8 * n + j + 1)
                ins = v.tensor_tensor(x_lo[:, 2 * j:2 * j + 2, :], src,
                                      x_hi[:, 2 * j:2 * j + 2, :].bitcast(F32), ALU.subtract)
                ins.then_inc(sem("turn_lo"), 1)
            if gain is None:
                for j in range(KC // 2):
                    v.wait_ge(sem("turned"), 8 * n + j + 1)
                    low(j, gview(turn_bank[j % 6][:, :], 2))
                return
            for j in range(KC // 2 + 2):
                if j < KC // 2:
                    v.wait_ge(sem("turned"), 8 * n + j + 1)
                    for k in range(2):
                        kk = 2 * j + k
                        ins = v.tensor_scalar(x_mid[:, kk, :], turn_bank[j % 6][:, k * T:(k + 1) * T],
                                              gain[:, kk:kk + 1], bias[:, kk:kk + 1], ALU.mult, ALU.add)
                    ins.then_inc(sem("turn_mid"), 1)
                if j >= 2:
                    low(j - 2, x_mid[:, 2 * (j - 2):2 * (j - 2) + 2, :])

        def pe_transposes(pe, to, src, tiles):
            for m in tiles:
                for t in range(NT):
                    i = (m - tiles[0]) * NT + t
                    mm = pe.transpose(to[:, i * P:(i + 1) * P], src[:, t, m * P:(m + 1) * P], ident[:, :])
            return mm

        def pe_mod(pe, step):
            pe.wait_ge(sem("mod_used"), 8 * step + 8)
            for m in range(2):
                for q in range(4):
                    mm = pe.matmul(turn[0][:, 4 * m + q:4 * m + q + 1], m_acc[:, m, q * P:(q + 1) * P],
                                   ones[:, 0:1], start=True, stop=True)
            mm.then_inc(sem("mod_cols"), 1)

        def a_block(i, j):
            return A_B0 + 4 * i - 1 + j if not isinstance(i, int) or i > 0 else A_B0 + j

        def pe_a_output(pe, i):
            def before(c):
                if c == 0:
                    pe.wait_ge(sem("a_ol"), 2 * i)
                    if not (isinstance(i, int) and i == A_KV):
                        pe.wait_ge(sem("a_krot"), i + 1)
                elif c == 1:
                    pe.wait_ge(sem("a_sg"), i if isinstance(i, int) and i == A_KV else i + 1)
                else:
                    pe.wait_ge(sem("a_sum_z"), 1 + 4 * (i - 1) + c - 1)
            output(pe, a_block(i, 3) if not (isinstance(i, int) and i == A_KV) else a_block(i, 0),
                   a_oh, a_ol, [1, 0, 1, 0], before)

        def pe_a_turn(pe, i):
            pe.wait_ge(sem("a_og"), i)
            pe.wait_ge(sem("mod_read"), i)
            for b in range(2):
                pe_transposes(pe, turn[b], a_og, [2 * b, 2 * b + 1]).then_inc(sem("a_turned"), 1)

        def pe_attention(pe, i):
            first = isinstance(i, int) and i == 0

            def arrived(c):
                if first:
                    pe.wait_ge(sem("turn_lo"), 2 * (c + 1))
                elif c == 0:
                    pe.wait_ge(sem("a_sg"), i)
                    pe.wait_ge(sem("a_sum_z"), 1 + 4 * (i - 1))
            project(pe, a_block(i, 0), pair[0], before=arrived)
            if first:
                pe_params(pe)
            else:
                pe_a_turn(pe, i)

            def kv_free(c):
                if c == 0 and not first:
                    pe.wait_ge(sem("a_krot"), i)
            project(pe, a_block(i, 1), pair[1], width=2 * A_HD, before=kv_free)

            def q_read(c):
                if c == 0:
                    pe.wait_ge(sem("a_qrot"), i + 1)
            project(pe, a_block(i, 2), pair[0], before=q_read)
            if not first:
                pe.wait_ge(sem("a_ol"), 2 * i)
            else:
                pe.wait_ge(sem("par_read"), 2)
            pe_transposes(pe, turn[0], a_q, [0, 1]).then_inc(sem("a_qk_turned"), 1)
            pe_transposes(pe, turn[1], a_q, [2, 3]).then_inc(sem("a_qk_turned"), 1)
            pe.wait_ge(sem("a_krot"), i + 1)
            if not first:
                pe.wait_ge(sem("a_og"), i)
            pe_transposes(pe, sc[0], a_k, [0]).then_inc(sem("a_qk_turned"), 1)
            pe.wait_ge(sem("a_qT_act"), i + 1)
            pe.wait_ge(sem("a_qkT_dve"), i + 1)
            for h in range(4):
                if h >= 2:
                    pe.wait_ge(sem("a_prob"), 4 * i + h - 1)
                for t in range(NT):
                    mm = pe.matmul(sc[(h + 1) % 2][:, t * T:(t + 1) * T], a_qT[:, h, t * P:(t + 1) * P],
                                   a_kT[:, :], start=True, stop=True)
                mm.then_inc(sem("a_score"), 1)
            if not first:
                pe_a_output(pe, i)

            def turn_probs(h):
                pe.wait_ge(sem("a_prob"), 4 * i + h + 1)
                if h >= 2:
                    pe.wait_ge(sem(f"a_pT{h % 2}"), 2 * i + 1)
                for k in range(NT):
                    for t in range(NT):
                        mm = pe.transpose(turn[h % 2][:, k * T + t * P:k * T + (t + 1) * P],
                                          a_p[:, h, t, k * P:(k + 1) * P], ident[:, :])
                mm.then_inc(sem("a_p_turned"), 1)

            def values(h):
                pe.wait_ge(sem(f"a_pT{h % 2}"), 2 * i + h // 2 + 1)
                for t in range(NT):
                    for k in range(NT):
                        mm = pe.matmul(sc[t][:, h * A_HD:(h + 1) * A_HD], a_pT[:, h % 2, k, t * P:(t + 1) * P],
                                       a_v[:, k, :], start=k == 0, stop=k == NT - 1)
                mm.then_inc(sem("a_pv"), 1)

            turn_probs(0)
            turn_probs(1)
            pe.wait_ge(sem("a_prob"), 4 * i + 4)
            values(0)
            turn_probs(2)
            values(1)
            turn_probs(3)
            values(2)
            values(3)
            pe_mod(pe, i)

        def pe_params(pe):
            pe.wait_ge(sem("par_in"), 16 * 13)
            pe.transpose(sc[0][:, 0:82], par_rows[0:82, :], ident[0:82, 0:82])
            pe.transpose(sc[0][:, 128:224], bmod_rows[0:96, :], ident[0:96, 0:96])
            for m in range(2):
                mm = pe.transpose(sc[0][:, 256 + 128 * m:344 + 128 * m], conv_rows[0:88, m, :],
                                  ident[0:88, 0:88])
            mm.then_inc(sem("par_turned"), 1)
            pe.matmul(sc[1][0:32, 0:TOEP], t_rel[:, :], t_hot[:, :], start=True, stop=True)\
                .then_inc(sem("par_turned"), 1)

        def r_block(i, j):
            return R_B0 + 4 * i - 1 + j if not isinstance(i, int) or i > 0 else R_B0 + j

        def pe_r_output(pe, i):
            last = isinstance(i, int) and i == R_HEADS

            def before(c):
                if c == 0:
                    pe.wait_ge(sem("r_ol"), 2 * i)
                    if not last:
                        pe.wait_ge(sem("r_v"), i + 1)
                elif c == 1:
                    pe.wait_ge(sem("r_sg"), i if last else i + 1)
                else:
                    pe.wait_ge(sem("r_sum_z"), 1 + 4 * (i - 1) + c - 1)
            output(pe, r_block(i, 0) if last else r_block(i, 3), r_oh, r_ol, [1, 0, 1, 0], before)

        def pe_r_turn(pe, i):
            pe.wait_ge(sem("r_og"), i)
            pe.wait_ge(sem("mod_read"), A_KV + i)
            for b in range(2):
                pe_transposes(pe, turn[b], r_og, [2 * b, 2 * b + 1]).then_inc(sem("r_turned"), 1)

        def pe_retention(pe, i):
            first = isinstance(i, int) and i == 0

            def arrived(c):
                if first:
                    pe.wait_ge(sem("turn_lo"), 8 + 2 * (c + 1))
                elif c == 0:
                    pe.wait_ge(sem("r_sg"), i)
                    pe.wait_ge(sem("r_sum_z"), 1 + 4 * (i - 1))
            project(pe, r_block(i, 0), pair[0], before=arrived)
            if not first:
                pe_r_turn(pe, i)

            def v_free(c):
                if c == 0 and not first:
                    pe.wait_ge(sem("r_v"), i)
            project(pe, r_block(i, 1), pair[1], before=v_free)

            def qk_read(c):
                if c == 0:
                    pe.wait_ge(sem("r_rot"), i + 1)
            project(pe, r_block(i, 2), pair[0], before=qk_read)
            if not first:
                pe.wait_ge(sem("r_ol"), 2 * i)
            pe_transposes(pe, turn[0], r_qk, [0, 1]).then_inc(sem("r_qk_turned"), 1)
            pe_transposes(pe, turn[1], r_qk, [2, 3]).then_inc(sem("r_qk_turned"), 1)
            pe.wait_ge(sem("r_qT"), i + 1)
            pe.wait_ge(sem("r_kT"), i + 1)
            if not first:
                pe.wait_ge(sem("r_og"), i)
            for s in range(NT):
                for k in range(2):
                    mm = pe.matmul(sc[0][:, s * T:(s + 1) * T], r_kT[:, k, s * P:(s + 1) * P], r_qT[:, k, :],
                                   start=k == 0, stop=k == 1)
            mm.then_inc(sem("r_score"), 1)
            if not first:
                pe_r_output(pe, i)
            pe.wait_ge(sem("r_s"), i + 1)
            pe.wait_ge(sem("r_v"), i + 1)
            for t in range(NT):
                for s in range(NT):
                    mm = pe.matmul(sc[t][:, :], r_s[:, s, t * P:(t + 1) * P], r_v[:, s, :],
                                   start=s == 0, stop=s == NT - 1)
            mm.then_inc(sem("r_o"), 1)
            pe_mod(pe, A_KV + i)

        def pe_first_block(pe):
            pe.wait_ge(sem("ident_in"), 16)
            pe.wait_ge(sem("x_in"), 16)
            turn_groups(pe, 0, lambda j: None, False)
            pe_attention(pe, 0)
            with pe.Fori(1, A_KV) as i:
                pe_attention(pe, i)
            pe_a_turn(pe, A_KV)
            pe_a_output(pe, A_KV)
            def normalized(j):
                if j % 4 == 0:
                    pe.wait_ge(sem("z_norm"), j // 4 + 1)
                    pe.wait_ge(sem("z_norm1"), j // 4 + 1)
            turn_groups(pe, 1, normalized, False)
            pe_retention(pe, 0)
            with pe.Fori(1, R_HEADS) as i:
                pe_retention(pe, i)
            pe_r_turn(pe, R_HEADS)
            pe_r_output(pe, R_HEADS)

        def act_attention(act, i, n, rest):
            first = isinstance(i, int) and i == 0
            H = lambda j, c: round_hi(act, a_block(i, j), c, 2 * A_HD if j == 1 else CB)
            H(0, 3)
            for c in range(3):
                H(1, c)
            act.wait_ge(sem("products"), CH * a_block(i, 0) + 4)
            for t in range(NT):
                act.activation(a_sq[:, t, :], pair[0][t][:, :], ACT.Square).then_inc(sem("a_square"), 1)
            if not first:
                act_a_turn(act, i)
            else:
                act_params(act)
            H(1, 3)
            H(2, 0)
            H(2, 1)
            H(2, 2)
            act.wait_ge(sem("products"), CH * a_block(i, 1) + 4)
            if not first:
                act.wait_ge(sem("a_pv"), 4 * i)
            for t in range(NT):
                act.activation(a_v[:, t, :], pair[1][t][:, A_HD:2 * A_HD], ACT.Copy).then_inc(sem("a_v"), 1)
            act.wait_ge(sem("a_qrot"), i + 1)
            for t in range(NT):
                act.activation(a_sq[:, t, 0:A_HD], pair[1][t][:, 0:A_HD], ACT.Square).then_inc(sem("a_square"), 1)
            H(2, 3)
            round_hi(act, n, 0)
            act.wait_ge(sem("a_qk_turned"), 3 * i + 1)
            act.activation(a_qT[:, 0:2, :], gview(turn[0][:, :], 2), ACT.Copy).then_inc(sem("a_qT_act"), 1)
            round_hi(act, n, 1)
            round_hi(act, n, 2)
            act.wait_ge(sem("products"), CH * a_block(i, 2) + 4)
            if not first:
                act.wait_ge(sem("a_og"), i)
            for t in range(NT):
                ins = act.activation(a_sg[:, t, :], pair[0][t][:, :], ACT.Silu)
            ins.then_inc(sem("a_sg"), 1)

            def probs(h):
                act.wait_ge(sem("a_max"), 4 * i + h + 1)
                for t in range(NT):
                    ins = act.activation(a_p[:, h, t, :], sc[(h + 1) % 2][:, t * T:(t + 1) * T], ACT.Exp,
                                         bias=a_nmax[:, h, t:t + 1], accum_out=a_sum[:, h, t:t + 1])
                ins.then_inc(sem("a_prob"), 1)
            probs(0)
            probs(1)
            if rest:
                rest[0](3)
            probs(2)
            probs(3)
            if rest:
                for c in range(3):
                    rest[1](c)
            for h in (0, 2):
                act.wait_ge(sem("a_p_turned"), 4 * i + h + 1)
                act.activation(a_pT[:, 0, :, :], gview(turn[0][:, :], 2), ACT.Copy).then_inc(sem("a_pT0"), 1)

        def act_a_turn(act, i):
            for b in range(2):
                act.wait_ge(sem("a_turned"), 2 * (i - 1) + b + 1)
                if b == 0 and not (isinstance(i, int) and i == 1):
                    act.wait_ge(sem("a_sum_z"), 1 + 4 * (i - 1))
                act.activation(a_oh[:, 2 * b:2 * b + 2, :], gview(turn[b][:, :], 2), ACT.Copy)\
                    .then_inc(sem("a_oh"), 1)

        def act_params(act):
            act.wait_ge(sem("par_read"), 1)
            act.activation(csilu[:, :], par[:, 32:48], ACT.Silu).then_inc(sem("csilu"), 1)

        def act_retention(act, i, n, rest):
            first = isinstance(i, int) and i == 0
            H = lambda j, c: round_hi(act, r_block(i, j), c)
            H(0, 3)
            for c in range(3):
                H(1, c)
            if not first:
                act_r_turn(act, i)
            H(1, 3)
            H(2, 0)
            H(2, 1)
            H(2, 2)
            act.wait_ge(sem("products"), CH * r_block(i, 1) + 4)
            if not first:
                act.wait_ge(sem("r_o"), i)
            for t in range(NT):
                ins = act.activation(r_v[:, t, :], pair[1][t][:, :], ACT.Copy)
            ins.then_inc(sem("r_v"), 1)
            H(2, 3)
            round_hi(act, n, 0)
            act.wait_ge(sem("r_qk_turned"), 2 * i + 1)
            act.activation(r_qT[:, :, :], gview(turn[0][:, :], 2), ACT.Copy).then_inc(sem("r_qT"), 1)
            round_hi(act, n, 1)
            round_hi(act, n, 2)
            act.wait_ge(sem("products"), CH * r_block(i, 2) + 4)
            if not first:
                act.wait_ge(sem("r_og"), i)
            for t in range(NT):
                ins = act.activation(r_sg[:, t, :], pair[0][t][:, :], ACT.Silu)
            ins.then_inc(sem("r_sg"), 1)
            if rest:
                rest[0](3)
                for c in range(3):
                    rest[1](c)

        def act_r_turn(act, i):
            for b in range(2):
                act.wait_ge(sem("r_turned"), 2 * (i - 1) + b + 1)
                if b == 0 and not (isinstance(i, int) and i == 1):
                    act.wait_ge(sem("r_sum_z"), 1 + 4 * (i - 1))
                act.activation(r_oh[:, 2 * b:2 * b + 2, :], gview(turn[b][:, :], 2), ACT.Copy)\
                    .then_inc(sem("r_oh"), 1)

        def act_normalize(act, n, value):
            act.wait_ge(sem("norm_stats"), n)
            for h in range(2):
                act.activation(z[:, 0, h * 1024:(h + 1) * 1024], z[:, 0, h * 1024:(h + 1) * 1024],
                               ACT.Identity, bias=nmr[:, 0:1], scale=rstd[:, 0:1]).then_inc(sem("z_norm"), 1)

        def act_first_block(act):
            act.dma_start(ident[:, :], ident_c).then_inc(sem("ident_in"), 16)
            turn_hi(act, 0, True)
            for c in range(3):
                round_hi(act, 0, c)
            act_attention(act, 0, a_block(1, 0), None)
            with act.Fori(1, A_KV) as i:
                act_attention(act, i, a_block(i, 3),
                              [lambda c: round_hi(act, a_block(i, 3), c),
                               lambda c: round_hi(act, a_block(i + 1, 0), c)])
            round_hi(act, R_B0 - 1, 3)
            act_a_turn(act, A_KV)
            act_decay(act)
            for c in range(3):
                round_hi(act, R_B0, c)
            act_normalize(act, 1, 1)
            turn_hi(act, 1, False)
            act_retention(act, 0, r_block(1, 0), None)
            act.wait_ge(sem("rows_used"), 1)
            act_rows(act, 1)
            with act.Fori(1, R_HEADS) as i:
                act_retention(act, i, r_block(i, 3),
                              [lambda c: round_hi(act, r_block(i, 3), c),
                               lambda c: round_hi(act, r_block(i + 1, 0), c)])
            round_hi(act, B_B0 - 1, 3)
            act_r_turn(act, R_HEADS)
            for c in range(3):
                round_hi(act, B_B0, c)
            act_normalize(act, 2, 1)

        def act_rows(act, layer):
            act.dma_start(rows[:, 0, :], broadcast_row(ln_gain, layer * D, D)).then_inc(sem("rows1_in"), 16)
            act.dma_start(rows[:, 1, :], broadcast_row(ln_bias, layer * D, D)).then_inc(sem("rows1_in"), 16)

        def act_decay(act):
            act.wait_ge(sem("decay_in"), 16 * 5)
            act.activation(r_e[:, :], r_e[:, :], ACT.Exp, scale=-float(np.log(2.0))).then_inc(sem("decay_e"), 1)
            act.wait_ge(sem("decay_u"), 1)
            act.activation(r_lg[:, :], r_u[:, :], ACT.Ln).then_inc(sem("decay_e"), 1)
            for h in range(R_HEADS):
                act.wait_ge(sem("decay_x"), h + 1)
                act.activation(r_decay[:, h, :, :], r_decay[:, h, :, :], ACT.Exp).then_inc(sem("decay"), 1)

        vs = Count()

        def vec(ins):
            ins.then_inc(sem("vec"), vs.one())

        def vec_wait(v):
            v.wait_ge(sem("vec"), vs.now())

        def mod_quarter(v, step, m, c):
            n = 8 * step + 4 * m + c
            if c == 0 and not (isinstance(step, int) and step == 0):
                v.wait_ge(sem("mod_cols"), step)
            v.wait_ge(sem(f"mod_in{c % 2}"), 16 * (4 * step + 2 * m + c // 2 + 1))
            for k in range(CH):
                w, cc = m_raw[:, c % 2, k, :], csilu[:, CH * c + k:CH * c + k + 1]
                if c == 0 and k == 0:
                    ins = v.tensor_scalar(m_acc[:, m, :], w, cc, None, ALU.mult)
                else:
                    if k == 0:
                        v.wait_ge(sem("mod_used"), n)
                    else:
                        vec_wait(v)
                    ins = v.scalar_tensor_tensor(out=m_acc[:, m, :], in0=w, scalar=cc,
                                                 in1=m_acc[:, m, :], op0=ALU.mult, op1=ALU.add)
                if k < CH - 1:
                    vec(ins)
            ins.then_inc(sem("mod_used"), 1)

        def mod_read(v, step):
            v.wait_ge(sem("mod_cols"), step + 1)
            v.tensor_tensor(modc[:, bass.ds(8 * step, 8)], turn[0][:, 0:8],
                            bmod[:, bass.ds(8 * step, 8)], ALU.add).then_inc(sem("mod_read"), 1)

        def rotate(v, to, src, tmp, cos, sin, groups, width):
            vec(v.tensor_tensor(gview(to, groups), gview(src, groups), cast(cos, groups), ALU.mult))
            for part in range(2):
                sn = gview(sin, 2)[:, :, part * width:(part + 1) * width]
                vec(v.tensor_tensor(swapped(tmp, groups, width, part), swapped(src, groups, width, 1 - part),
                                    sn.unsqueeze(1).to_broadcast([P, groups, 2, width]), ALU.mult))
            vec_wait(v)
            return v.tensor_tensor(to, to, tmp, ALU.add)

        def vec_params(v):
            v.wait_ge(sem("par_turned"), 1)
            v.tensor_copy(par[:, :], sc[0][:, 0:82]).then_inc(sem("par_read"), 1)
            v.tensor_copy(bmod[:, :], sc[0][:, 128:224])
            for m in range(2):
                v.tensor_copy(conv.rearrange("p f j -> p j f")[:, 2 * m:2 * m + 2, :],
                              gview(sc[0][:, 256 + 128 * m:344 + 128 * m], 2))
            v.wait_ge(sem("par_in"), 16 * 13)
            v.wait_ge(sem("par_turned"), 2)
            v.tensor_tensor(t_out[:, :], sc[1][0:32, 0:TOEP], t_mask[:, :], ALU.add)\
                .then_inc(sem("par_read"), 1)

        def vec_rope_gains(v):
            v.wait_ge(sem("rope_in"), 16 * 6)
            vec(v.tensor_scalar(ropet[:, P:2 * P], ropet[:, P:2 * P], float(A_HD) ** 0.5, None, ALU.mult))
            vec_wait(v)
            q = A_HD // 4
            for m, (cos, sin) in enumerate(((cos_q, sin_q), (cos_k, sin_k))):
                gain = ropet[:, m * P:(m + 1) * P]
                v.tensor_tensor(cos[:, :, :], cos[:, :, :], cast(gain, NT), ALU.mult)
                for part in range(2):
                    sv = sin.rearrange("p t (h s w) -> p t h s w", h=2, s=2)[:, :, :, part, :]
                    gs = gain.rearrange("p (h s w) -> p h s w", h=2, s=2)[:, :, 1 - part, :]
                    vec(v.tensor_tensor(sv, sv, gs.unsqueeze(1).to_broadcast([P, NT, 2, q]), ALU.mult))
            vec_wait(v)

        def vec_attention(v, i, n, rest):
            first = isinstance(i, int) and i == 0
            todo = [(m, c) for m in range(2) for c in range(CH)]

            def M(count=1):
                for _ in range(count):
                    mod_quarter(v, i, *todo.pop(0))
            S_ = lambda j, c: split_lo(v, a_block(i, j), c, 2 * A_HD if j == 1 else CB)
            S_(0, 3)
            for c in range(3):
                S_(1, c)
                if not first:
                    M()
            for kind in range(2):
                w = CB if kind == 0 else A_HD
                cos, sin, to = (cos_q, sin_q, a_q) if kind == 0 else (cos_k, sin_k, a_k)
                heads = w // A_HD
                ss, rs = a_ss[:, kind, :, 0:heads], a_rs[:, kind, :, 0:heads]
                for t in range(NT):
                    v.wait_ge(sem("a_square"), 4 * i + 2 * kind + t + 1)
                    vec(v.tensor_reduce(ss[:, t, :], gview(a_sq[:, t, 0:w], heads), AX, ALU.add))
                vec_wait(v)
                v.tensor_scalar(ss, ss, RMS_EPS * A_HD, None, ALU.add).then_inc(sem("a_var"), 1)
                for t in range(NT):
                    vec(rotate(v, to[:, t, :], pair[kind][t][:, 0:w], ropet[:, 0:w], cos[:, t, :], sin[:, t, :],
                               heads, A_HD // 4))
                    vec_wait(v)
                v.wait_ge(sem("a_rsqrt"), 2 * i + kind + 1)
                for t in range(NT):
                    ins = v.tensor_tensor(gview(to[:, t, :], heads), gview(to[:, t, :], heads),
                                          rs[:, t, :].unsqueeze(2).to_broadcast([P, heads, A_HD]), ALU.mult)
                ins.then_inc(sem("a_qrot" if kind == 0 else "a_krot"), 1)
                if kind == 0:
                    if first:
                        vec_params(v)
                    else:
                        vec_a_turn(v, i)
                    S_(1, 3)
                    for c in range(3):
                        S_(2, c)
                        if c == 2 and first:
                            v.wait_ge(sem("csilu"), 1)
                            v.wait_ge(sem("par_read"), 2)
                            M(4)
                        elif c and not first:
                            M()
            S_(2, 3)
            split_lo(v, n, 0)
            v.wait_ge(sem("a_qk_turned"), 3 * i + 2)
            v.tensor_copy(a_qT[:, 2:4, :], gview(turn[1][:, :], 2))
            v.wait_ge(sem("a_qk_turned"), 3 * i + 3)
            v.tensor_copy(a_kT[:, :], sc[0][:, 0:T]).then_inc(sem("a_qkT_dve"), 1)
            split_lo(v, n, 1)
            split_lo(v, n, 2)
            for h in range(4):
                v.wait_ge(sem("a_score"), 4 * i + h + 1)
                v.tensor_reduce(a_nmax[:, h, :], gview(sc[(h + 1) % 2][:, :], NT), AX, ALU.max,
                                negate=True).then_inc(sem("a_max"), 1)
                if h == 2 and rest:
                    rest[0](3)
            if rest:
                for c in range(CH):
                    if c < 3:
                        rest[1](c)
                    vec_sum(v, "a", 1 + 4 * (i - 1) + c, CH * a_block(i, 3) + c + 1, c)
                    if c < 3:
                        M()
            else:
                M(4)
            assert not todo
            for h in (1, 3):
                v.wait_ge(sem("a_p_turned"), 4 * i + h + 1)
                v.tensor_copy(a_pT[:, 1, :, :], gview(turn[1][:, :], 2)).then_inc(sem("a_pT1"), 1)
            v.wait_ge(sem("a_prob"), 4 * i + 4)
            vec(v.reciprocal(a_rinv[:, :, :], a_sum[:, :, :]))
            vec_wait(v)
            v.wait_ge(sem("a_pv"), 4 * i + 4)
            v.wait_ge(sem("a_sg"), i + 1)
            for t in range(NT):
                for h in range(4):
                    w = slice(h * A_HD, (h + 1) * A_HD)
                    ins = v.scalar_tensor_tensor(out=a_og[:, t, w], in0=sc[t][:, w], scalar=a_rinv[:, h, t:t + 1],
                                                 in1=a_sg[:, t, w], op0=ALU.mult, op1=ALU.mult)
            ins.then_inc(sem("a_og"), 1)
            mod_read(v, i)

        def vec_sum(v, which, before, done, c, order=(1, 0, 1, 0), stat=False):
            v.wait_ge(sem("products"), done)
            v.wait_ge(sem(which + "_sum_z"), before)
            for t in range(NT):
                ins = v.tensor_tensor(z[:, t, c * CB:(c + 1) * CB], z[:, t, c * CB:(c + 1) * CB],
                                      pair[order[c]][t][:, :], ALU.add)
            ins.then_inc(sem(which + "_sum_z"), 1)

        def vec_a_turn(v, i):
            for b in range(2):
                v.wait_ge(sem("a_oh"), 2 * (i - 1) + b + 1)
                v.tensor_tensor(a_ol[:, 2 * b:2 * b + 2, :], gview(turn[b][:, :], 2),
                                a_oh[:, 2 * b:2 * b + 2, :].bitcast(F32), ALU.subtract).then_inc(sem("a_ol"), 1)

        def vec_r_turn(v, i):
            for b in range(2):
                v.wait_ge(sem("r_oh"), 2 * (i - 1) + b + 1)
                v.tensor_tensor(r_ol[:, 2 * b:2 * b + 2, :], gview(turn[b][:, :], 2),
                                r_oh[:, 2 * b:2 * b + 2, :].bitcast(F32), ALU.subtract).then_inc(sem("r_ol"), 1)

        def vec_retention(v, i, n, rest, between=None):
            todo = [(m, c) for m in range(2) for c in range(CH)]

            def M():
                mod_quarter(v, A_KV + i, *todo.pop(0))
            first = isinstance(i, int) and i == 0
            S_ = lambda j, c: split_lo(v, r_block(i, j), c)
            S_(0, 3)
            for c in range(3):
                S_(1, c)
                M()
            v.wait_ge(sem("products"), CH * r_block(i, 0) + 4)
            for t in range(NT):
                ins = rotate(v, r_qk[:, t, :], pair[0][t][:, :], r_t[:, :], cos_r[:, t, :], sin_r[:, t, :],
                             2, R_DK // 4)
                if t == 0:
                    vec(ins)
                    vec_wait(v)
            ins.then_inc(sem("r_rot"), 1)
            if not first:
                vec_r_turn(v, i)
            S_(1, 3)
            for c in range(3):
                S_(2, c)
                if c:
                    M()
            if between:
                between()
            S_(2, 3)
            split_lo(v, n, 0)
            v.wait_ge(sem("r_qk_turned"), 2 * i + 2)
            v.tensor_copy(r_kT[:, :, :], gview(turn[1][:, :], 2)).then_inc(sem("r_kT"), 1)
            split_lo(v, n, 1)
            split_lo(v, n, 2)
            v.wait_ge(sem("r_score"), i + 1)
            v.tensor_tensor(r_s[:, :, :], gview(sc[0][:, :], 2),
                            r_decay[:, bass.ds(i, 1), :, :].rearrange("p o t n -> p (o t) n"),
                            ALU.mult).then_inc(sem("r_s"), 1)
            if rest:
                rest[0](3)
                for c in range(CH):
                    if c < 3:
                        rest[1](c)
                    vec_sum(v, "r", 1 + 4 * (i - 1) + c, CH * r_block(i, 3) + c + 1, c)
                    if c < 3:
                        M()
            else:
                for _ in range(3):
                    M()
            assert not todo
            v.wait_ge(sem("r_o"), i + 1)
            v.wait_ge(sem("r_sg"), i + 1)
            for t in range(NT):
                vec(v.bn_stats(r_st[:, t, :], sc[t][:, :]))
            vec_wait(v)
            v.memset(spare[:, :], 0.0)
            for t in range(NT):
                vec(v.bn_aggr(r_mv[:, t, :], r_st[:, t, :]))
            vec_wait(v)
            v.tensor_scalar(r_var[:, :], r_mv[:, :, 1], LN_EPS, None, ALU.add).then_inc(sem("r_var"), 1)
            v.wait_ge(sem("r_rsqrt"), i + 1)
            for t in range(NT):
                vec(v.tensor_scalar(r_og[:, t, :], sc[t][:, :], r_mv[:, t, 0:1], r_rs[:, t:t + 1],
                                    ALU.subtract, ALU.mult))
            vec_wait(v)
            ins = v.tensor_tensor(r_og[:, :, :], r_og[:, :, :], r_sg[:, :, :], ALU.mult)
            ins.then_inc(sem("r_og"), 1)
            mod_read(v, A_KV + i)

        def vec_layer_end(v, which, b, i, n):
            split_lo(v, b, 3)
            (vec_a_turn if which == "a" else vec_r_turn)(v, i)
            for c in range(CH):
                if c < 3:
                    split_lo(v, b + 1, c)
                vec_sum(v, which, 1 + 4 * (i - 1) + c, CH * b + c + 1, c)
                v.wait_ge(sem(which + "_sum_z"), 1 + 4 * (i - 1) + c + 1)
                for t in range(NT):
                    ins = v.bn_stats(stats[:, t, c, :], z[:, t, c * CB:(c + 1) * CB])
                vec(ins)
            vec_wait(v)
            for t in range(NT):
                vec(v.bn_aggr(mv[:, t, :], stats[:, t, :, :]))
            vec_wait(v)
            v.tensor_scalar(var[:, :], mv[:, :, 1], LN_EPS, None, ALU.add).then_inc(sem("var"), 1)
            v.wait_ge(sem("rsqrt"), n)
            v.scalar_tensor_tensor(out=nmr[:, :], in0=mv[:, :, 0], scalar=-1.0, in1=rstd[:, :],
                                   op0=ALU.mult, op1=ALU.mult).then_inc(sem("norm_stats"), 1)
            for h in range(2):
                zz = z[:, 1, h * 1024:(h + 1) * 1024]
                v.tensor_scalar(zz, zz, mv[:, 1, 0:1], rstd[:, 1:2], ALU.subtract, ALU.mult)\
                    .then_inc(sem("z_norm1"), 1)

        def vec_affine(v, which, scale):
            for t in range(NT):
                vec(v.scalar_tensor_tensor(out=z[:, t, :], in0=z[:, t, :], scalar=scale, in1=rows[:, 0, :],
                                           op0=ALU.mult, op1=ALU.mult))
                vec_wait(v)
                ins = v.scalar_tensor_tensor(out=z[:, t, :], in0=rows[:, 1, :], scalar=scale, in1=z[:, t, :],
                                             op0=ALU.mult, op1=ALU.add)
                if t == 0:
                    ins.then_inc(sem("affine"), 1)
            return ins

        def vec_decay(v):
            v.wait_ge(sem("decay_e"), 1)
            v.tensor_scalar(r_u[:, :], r_e[:, :], -1.0, 1.0, ALU.mult, ALU.add).then_inc(sem("decay_u"), 1)
            terms = 14
            vec(v.tensor_scalar(r_m[:, :], r_e[:, :], 1.0 / terms, 1.0 / (terms - 1), ALU.mult, ALU.add))
            for k in range(terms - 2, 0, -1):
                vec_wait(v)
                vec(v.tensor_tensor(r_m[:, :], r_m[:, :], r_e[:, :], ALU.mult))
                vec_wait(v)
                vec(v.tensor_scalar(r_m[:, :], r_m[:, :], 1.0 / k, None, ALU.add))
            vec_wait(v)
            vec(v.scalar_tensor_tensor(out=r_m[:, :], in0=r_m[:, :], scalar=-1.0, in1=r_e[:, :],
                                       op0=ALU.mult, op1=ALU.mult))
            v.wait_ge(sem("decay_u"), 1)
            v.wait_ge(sem("decay_e"), 2)
            vec(v.tensor_scalar(r_u[:, :], r_u[:, :], -1.0, 1.0, ALU.mult, ALU.add))
            vec_wait(v)
            vec(v.tensor_scalar(r_u[:, :], r_u[:, :], 1e-7, None, ALU.max))
            vec_wait(v)
            vec(v.reciprocal(r_u[:, :], r_u[:, :]))
            vec_wait(v)
            vec(v.tensor_tensor(r_lg[:, :], r_lg[:, :], r_u[:, :], ALU.mult))
            vec_wait(v)
            vec(v.tensor_tensor(r_lg[:, :], r_lg[:, :], r_e[:, :], ALU.mult))
            vec(v.tensor_scalar(r_n[:, :], r_e[:, :], 0.25, None, ALU.is_lt))
            vec_wait(v)
            vec(v.tensor_tensor(r_m[:, :], r_m[:, :], r_n[:, :], ALU.mult))
            vec(v.tensor_scalar(r_n[:, :], r_n[:, :], -1.0, 1.0, ALU.mult, ALU.add))
            vec_wait(v)
            vec(v.tensor_tensor(r_lg[:, :], r_lg[:, :], r_n[:, :], ALU.mult))
            vec_wait(v)
            vec(v.tensor_tensor(r_lg[:, :], r_lg[:, :], r_m[:, :], ALU.add))
            vec_wait(v)
            for h in range(R_HEADS):
                vec(v.tensor_scalar(r_decay[:, h, :, :], r_pos[:, 0, :, :], r_lg[:, h:h + 1], None, ALU.mult))
                vec_wait(v)
                v.scalar_tensor_tensor(out=r_decay[:, h, :, :], in0=r_pos[:, 1, :, :],
                                       scalar=r_lg[:, R_HEADS + h:R_HEADS + h + 1],
                                       in1=r_decay[:, h, :, :], op0=ALU.mult, op1=ALU.add)\
                    .then_inc(sem("decay_x"), 1)

        def vec_first_block(v):
            vec(v.memset(ones[:, :], 1.0))
            turn_lo(v, 0)
            v.wait_ge(sem("x_in"), 16)
            v.wait_ge(sem("turned"), 8)
            v.tensor_scalar(z[:, :, :], z[:, :, :], ALPHA, None, ALU.mult).then_inc(sem("a_sum_z"), 1)
            for c in range(3):
                split_lo(v, 0, c)
            vec_rope_gains(v)
            vec_attention(v, 0, a_block(1, 0), None)
            with v.Fori(1, A_KV) as i:
                vs.enter(i, 1, VEC_A)
                vec_attention(v, i, a_block(i, 3),
                              [lambda c: split_lo(v, a_block(i, 3), c),
                               lambda c: split_lo(v, a_block(i + 1, 0), c)])
            vs.leave(A_KV - 1)
            vec_decay(v)
            vec_layer_end(v, "a", R_B0 - 1, A_KV, 1)
            turn_lo(v, 1, par[:, 0:KC], par[:, KC:2 * KC])
            v.wait_ge(sem("decay"), R_HEADS)
            vec(v.tensor_scalar(r_decay[:, :, :, :], r_decay[:, :, :, :], float(R_DK) ** -0.5, None, ALU.mult))

            def affine():
                v.wait_ge(sem("rows_in"), 32)
                v.wait_ge(sem("z_norm"), 2)
                v.wait_ge(sem("z_norm1"), 2)
                vec_affine(v, "r", ALPHA).then_inc(sem("r_sum_z"), 1)
                v.wait_ge(sem("r_sum_z"), 1)
                v.sem_inc(sem("rows_used"), 1)
            vec_retention(v, 0, r_block(1, 0), None, affine)
            with v.Fori(1, R_HEADS) as i:
                vs.enter(i, 1, VEC_R)
                vec_retention(v, i, r_block(i, 3),
                              [lambda c: split_lo(v, r_block(i, 3), c),
                               lambda c: split_lo(v, r_block(i + 1, 0), c)])
            vs.leave(R_HEADS - 1)
            vec_layer_end(v, "r", B_B0 - 1, R_HEADS, 2)

        def broadcast_row(ap, first, n):
            return bass.AP(tensor=ap.tensor, offset=ap.offset + first, ap=[[0, P], [1, n]])

        def by_row(ap, first, n):
            return bass.AP(tensor=ap.tensor, offset=ap.offset + first, ap=[[P, n], [1, P]])

        def by_token(ap):
            return ap.rearrange("(t p) d -> p t d", p=P)

        def sync_first_block(sp):
            sp.dma_start(z[:, :, :], by_token(x[0])).then_inc(sem("x_in"), 16)
            widths = (CB, 2 * A_HD, CB)
            for j in range(3):
                load(sp, a_block(0, j), a_blocks[j](0), widths[j], halves=j == 1)
            with sp.Fori(1, A_KV) as i:
                for j in range(3):
                    load(sp, a_block(i, j), a_blocks[j](i), widths[j], halves=j == 1)
                load(sp, a_block(i, 3), out_rows(w_attn_out, i - 1))
            load(sp, R_B0 - 1, out_rows(w_attn_out, A_KV - 1))
            for j in range(3):
                load(sp, r_block(0, j), r_blocks[j](0), halves=j == 0)
            with sp.Fori(1, R_HEADS) as i:
                for j in range(3):
                    load(sp, r_block(i, j), r_blocks[j](i), halves=j == 0)
                load(sp, r_block(i, 3), out_rows(w_ret_out, i - 1))
            load(sp, B_B0 - 1, out_rows(w_ret_out, R_HEADS - 1))

        def pool_first_block(g):
            def get(to, src, name):
                g.dma_start(to, src).then_inc(sem(name), 16)
            for m in range(2):
                gain = (attn_q_gain, attn_k_gain)[m]
                get(ropet[:, m * P:(m + 1) * P], broadcast_row(gain, 0, P), "rope_in")
                get((cos_q, cos_k)[m][:, :, :], by_token(cos_a_c), "rope_in")
                get((sin_q, sin_k)[m][:, :, :], by_token(sin_a_c), "rope_in")
            get(par_rows[0:16, :], by_row(ln_gain, 0, 16), "par_in")
            get(par_rows[16:32, :], by_row(ln_bias, 0, 16), "par_in")
            get(par_rows[32:48, :], by_row(c_2, 0, 16), "par_in")
            get(par_rows[48:64, :], by_row(norm_attn_2, 0, 16), "par_in")
            get(par_rows[64:80, :], by_row(norm_ffn_2, 0, 16), "par_in")
            get(par_rows[80:82, :], by_row(kv_norm_2, 0, 2), "par_in")
            get(bmod_rows[0:96, :], by_row(b_mod_2, 0, 96), "par_in")
            get(conv_rows[0:88, 0, :], by_row(conv_w_2, 0, 88), "par_in")
            get(conv_rows[0:44, 1, :], by_row(conv_w_2, 2 * FF, 44), "par_in")
            get(conv_rows[44:88, 1, :], by_row(conv_b_2, 0, 44), "par_in")
            get(t_rel[:, :], rel_bias_2, "par_in")
            get(t_hot[:, :], onehot_c, "par_in")
            get(t_mask[:, :], mask_c, "par_in")
            get(rows[:, 0, :], broadcast_row(ln_gain, 0, D), "rows_in")
            get(rows[:, 1, :], broadcast_row(ln_bias, 0, D), "rows_in")

            def mod_load(step, m, c):
                n = 8 * step + 4 * m + c
                if not isinstance(n, int) or n >= 2:
                    g.wait_ge(sem("mod_used"), n - 1)
                g.dma_start(m_raw[:, c % 2, :, :],
                            w_m[:, CH * c:CH * c + CH, bass.ds((2 * step + m) * CB, CB)])\
                    .then_inc(sem(f"mod_in{c % 2}"), 16)

            def loads(step, first, last):
                for n in range(first, last):
                    mod_load(step, n // CH, n % CH)

            def power(to, src, ready, value, done):
                g.wait_ge(sem(ready), value)
                shape = list(src.shape)
                half = minus_half[:, 0:int(np.prod(shape[1:]))]
                if len(shape) == 3:
                    half = half.rearrange("p (a b) -> p a b", a=shape[1])
                g.tensor_tensor(to, src, half, ALU.pow).then_inc(sem(done), 1)

            def a_power(i, kind):
                h = 4 if kind == 0 else 1
                power(a_rs[:, kind, :, 0:h], a_ss[:, kind, :, 0:h], "a_var", 2 * i + kind + 1, "a_rsqrt")

            g.memset(minus_half[:, :], -0.5).then_inc(sem("half_set"), 1)
            g.wait_ge(sem("half_set"), 1)
            loads(0, 0, 2)
            a_power(0, 0)
            g.wait_ge(sem("par_read"), 2)
            get(toep, t_out[:, :].unsqueeze(1).to_broadcast([32, P, TOEP]), "toep")
            g.wait_ge(sem("toep"), 16)
            loads(0, 2, 6)
            a_power(0, 1)
            loads(0, 6, 8)
            loads(1, 0, 2)
            with g.Fori(1, A_KV) as i:
                loads(i, 2, 5)
                a_power(i, 0)
                loads(i, 5, 7)
                a_power(i, 1)
                loads(i, 7, 8)
                loads(i + 1, 0, 2)
            g.wait_ge(sem("a_og"), A_KV)
            g.wait_ge(sem("a_turned"), 2 * A_KV)
            get(cos_r[:, :, :], by_token(cos_r_c), "decay_in")
            get(sin_r[:, :, :], by_token(sin_r_c), "decay_in")
            get(r_e[:, :], broadcast_row(ret_decay_exp, 0, 16), "decay_in")
            get(r_pos[:, 0, :, :], by_token(ahead_c), "decay_in")
            get(r_pos[:, 1, :, :], by_token(behind_c), "decay_in")
            power(rstd[:, :], var[:, :], "var", 1, "rsqrt")

            def r_step(i, last):
                loads(A_KV + i, 2, 8)
                power(r_rs[:, :], r_var[:, :], "r_var", i + 1, "r_rsqrt")
                if not last:
                    loads(A_KV + i + 1, 0, 2)
            with g.Fori(0, R_HEADS - 1) as i:
                r_step(i, False)
            r_step(R_HEADS - 1, True)
            power(rstd[:, :], var[:, :], "var", 2, "rsqrt")

        B_STEPS = {1: ["s0", "s1", "s2"], 2: ["t0", "s3", "t1", "v0", "s4"],
                   3: ["t2", "v1", "s5", "t3", "v2", "s6", "t4", "v3", "s7", "t5", "v4", "t6", "v5", "t7",
                       "v6", "v7"]}
        HALF = W_HD

        def half(h):
            return slice((h % 2) * HALF, (h % 2 + 1) * HALF)

        def b_out(g):
            return b_q if g == 3 else b_o

        def three(to, fn):
            fn(to[:, 0:P], 0, P)
            return fn(to[:, P:P + T], 1, T)

        def pe_b_step(pe, g, what):
            kind, h = what[0], int(what[1])
            n = 8 * g + h
            if kind == "s":
                pe.wait_ge(sem("b_qT_v"), g + 1)
                pe.wait_ge(sem("b_qT_a"), g + 1)
                if n >= 2:
                    pe.wait_ge(sem("b_read"), n - 1)
                keys = (lambda w: b_kaT[half(h), g, 0:w]) if g < 2 else \
                       (lambda w: b_kBT[half(h), 4 * (g - 2) + h // 2, 0:w])
                mm = three(sc[h % 2], lambda to, t, w: pe.matmul(
                    to, b_qT[half(h), h // 2, t * P:(t + 1) * P], keys(w), start=True, stop=True))
                mm.then_inc(sem("b_score"), 1)
            elif kind == "t":
                pe.wait_ge(sem("b_prob"), n + 1)
                if h < 2 and g > 0:
                    pe.wait_ge(sem("b_ol"), 4 if g == 3 else 2 * g)
                if n >= 2:
                    pe.wait_ge(sem("b_pT"), n - 1)
                for m in range(3):
                    mm = pe.transpose(turn[h % 2][:, m * P:(m + 1) * P], b_s[:, h % 4, m * P:(m + 1) * P],
                                      ident[:, :])
                mm.then_inc(sem("b_p_turned"), 1)
            else:
                pe.wait_ge(sem("b_pT"), n + 1)
                if h == 0 and g > 0:
                    pe.wait_ge(sem("b_og"), g)
                val = (lambda k: b_va[:, k, g * HALF:(g + 1) * HALF]) if g < 2 else \
                      (lambda k: b_vB[:, k, (8 * (g - 2) + h) * HALF:(8 * (g - 2) + h + 1) * HALF])
                col = slice(h * HALF, (h + 1) * HALF)
                pe.matmul(pair[1][0][:, col], b_pT[:, h % 2, 0:P], val(0), start=True, stop=True)
                pe.matmul(pair[1][1][:, col], b_pT[:, h % 2, P:2 * P], val(0), start=True, stop=False)
                pe.matmul(pair[1][1][:, col], b_pT[:, h % 2, 2 * P:3 * P], val(1), start=False, stop=True)\
                    .then_inc(sem("b_pv"), 1)

        def pe_turn_pairs(pe, src, done):
            for b in range(2):
                pe_transposes(pe, turn[b], src, [2 * b, 2 * b + 1]).then_inc(sem(done), 1)

        def pe_b_outT(pe, g):
            pe.wait_ge(sem("b_og"), g + 1)
            if g < 2:
                pe.wait_ge(sem("b_qT_a"), g + 2)
                pe.wait_ge(sem("b_qT_v"), g + 2)
            elif g == 2:
                pe.wait_ge(sem("b_pT"), 32)
            else:
                pe.wait_ge(sem("b_ol"), 6)
            pe_turn_pairs(pe, b_out(g), "b_o_turned")

        def pe_second_attention(pe):
            pe.wait_ge(sem("diag"), 1)
            turn_groups(pe, 2, lambda j: None, True)

            def gates(c):
                for b in range(2):
                    n = 2 * c + b
                    pe.wait_ge(sem("gate_diag"), n + 1)
                    if n >= 2:
                        pe.wait_ge(sem("gate_row"), n - 1)
                    for m in range(4):
                        mm = pe.matmul(sc[b][:, m * P:(m + 1) * P], ones[:, :], gate_diag[:, b, m, :],
                                       start=True, stop=True)
                    mm.then_inc(sem("gate_mm"), 1)
            project(pe, B_B0, pair[0], after=gates,
                    before=lambda c: pe.wait_ge(sem("turn_lo"), 16 + 2 * (c + 1)))

            def turn_qi0(c):
                if c == 0:
                    pe.wait_ge(sem("i_q"), 1)
                    pe_turn_pairs(pe, i_q, "i_q_turned")
            project(pe, B_B0 + 1, pair[1], after=turn_qi0)
            project(pe, B_B0 + 2, pair[0], width=80)
            pe.wait_ge(sem("i_q"), 2)
            pe.wait_ge(sem("i_qT_a"), 1)
            pe.wait_ge(sem("i_qT_v"), 1)
            pe_turn_pairs(pe, i_q, "i_q_turned")

            def index(c):
                if c == 0:
                    pe.wait_ge(sem("i_kdup"), 1)
                    pe.wait_ge(sem("gate_row"), 8)
                    pe_transposes(pe, sc[0], i_kdup, [0]).then_inc(sem("i_k_turned"), 1)
                    return
                if c == 1:
                    pe.wait_ge(sem("i_kT"), 1)
                    pe.wait_ge(sem("i_qT_a"), 2)
                    pe.wait_ge(sem("i_qT_v"), 2)
                for h in INDEX_HEADS[c]:
                    if h >= 2:
                        pe.wait_ge(sem("i_relu"), h - 1)
                    three(sc[h % 2], lambda to, t, w: pe.matmul(
                        to, i_qT[half(h), h // 2, t * P:(t + 1) * P], i_kT[half(h), 0:w],
                        start=True, stop=True)).then_inc(sem("i_dot"), 1)
            project(pe, B_B0 + 3, pair[1], after=index)

            def build(c):
                if c == 0:
                    pe.wait_ge(sem("b_kadup"), 1)
                    for kv in range(2):
                        for t in range(NT):
                            mm = pe.transpose(turn[0][:, kv * T + t * P:kv * T + (t + 1) * P],
                                              b_kadup[:, t, kv, :], ident[:, :])
                    mm.then_inc(sem("b_kv_turned"), 1)
                    pe.wait_ge(sem("b_cdiag"), 1)
                    for r in range(2):
                        for t in range(NT):
                            mm = pe.matmul(turn[1][:, r * T + t * P:r * T + (t + 1) * P],
                                           b_kvc[:, t, (2 + r) * P:(3 + r) * P], diag[:, t, :],
                                           start=True, stop=True)
                    mm.then_inc(sem("b_kv_turned"), 1)
                elif c < 3:
                    pe.wait_ge(sem("b_kvT"), 1)
                    pe.wait_ge(sem("b_w_in"), 16 * 4)
                    if c == 2:
                        pe.wait_ge(sem("b_kB_a"), 1)
                        pe.wait_ge(sem("b_kB_v"), 1)
                    for b in range(2):
                        for m in range(2):
                            n = 4 * (c - 1) + 2 * b + m
                            for r in range(2):
                                mm = pe.matmul(turn[b][:, m * T:(m + 1) * T], b_wuk[:, r, n * P:(n + 1) * P],
                                               b_ckvT[:, r, :], start=r == 0, stop=r == 1)
                        mm.then_inc(sem("b_kB"), 1)
                else:
                    pe.wait_ge(sem("b_kB_a"), 2)
                    pe.wait_ge(sem("b_kB_v"), 2)
                    pe.wait_ge(sem("i_relu"), 16)
                    for m in range(4):
                        to = (turn[0], turn[1], sc[0], sc[1])[m]
                        for r in range(2):
                            mm = pe.matmul(to[:, :], b_ckvT[:, r, m // 2 * P:(m // 2 + 1) * P],
                                           b_wuv[:, r, m % 2 * CB:(m % 2 + 1) * CB], start=r == 0, stop=r == 1)
                        mm.then_inc(sem("b_vB_mm"), 1)
            project(pe, B_B0 + 4, pair[0], after=build)

            for g in range(4):
                def steps(c, g=g):
                    if c == 0:
                        pe.wait_ge(sem("b_q"), g + 1)
                        if g == 0:
                            pe.wait_ge(sem("b_vB_a"), 2)
                            pe.wait_ge(sem("b_vB_v"), 2)
                        else:
                            pe.wait_ge(sem("b_pT"), 8 * g)
                        pe_turn_pairs(pe, b_q, "b_q_turned")
                    if c == 1 and 1 <= g <= 2:
                        pe_b_outT(pe, g - 1)
                    for what in B_STEPS.get(c, []):
                        pe_b_step(pe, g, what)
                if g < 3:
                    def q_read(c, g=g):
                        if c == 0:
                            pe.wait_ge(sem("b_q"), g + 1)
                    project(pe, B_B0 + 5 + g, pair[0], before=q_read, after=steps)
                else:
                    def z_read(c):
                        if c == 0:
                            pe.wait_ge(sem("b_ol"), 4)
                            pe.wait_ge(sem("b_q"), 4)
                        else:
                            pe.wait_ge(sem("b_scaled"), c)
                    output(pe, B_B0 + 8, b_oh[:, 0], b_ol[:, 0], [0, 0, 0, 0], z_read, steps)
            for g in range(1, 4):
                def z_read(c, g=g):
                    if c == 0:
                        pe.wait_ge(sem("b_og"), 4)
                        pe.wait_ge(sem("b_ol"), 2 * g + 2)
                    pe.wait_ge(sem("b_scaled"), max(4, 4 * g + c - 1))

                def after(c, g=g):
                    if c == 0 and g < 3:
                        pe_b_outT(pe, g + 1)
                output(pe, B_B0 + 8 + g, b_oh[:, g % 2], b_ol[:, g % 2], [0, 1, 0, 1], z_read, after)

        def f_block(f, j):
            return F_B0 + j if isinstance(f, int) and f == 0 else F_B0 - 1 + 3 * f + j

        def pe_f_output(pe, f, after=None):
            last = isinstance(f, int) and f == FG

            def before(c):
                if c == 0:
                    pe.wait_ge(sem("f_hl"), f)
                    pe.wait_ge(sem("f_u"), f if last else f + 1)
                if c == 1:
                    pe.wait_ge(sem("f_g"), f if last else f + 1)
                if c >= 2:
                    pe.wait_ge(sem("f_scaled"), 1 + 4 * (f - 1) + c - 1)
            output(pe, f_block(f, 0) if last else f_block(f, 2), f_hh, f_hl, [0, 1, 0, 1], before, after)

        def pe_feed_forward(pe, f):
            first = isinstance(f, int) and f == 0

            def u_before(c):
                if first:
                    pe.wait_ge(sem("turn_lo"), 24 + 2 * (c + 1))
                elif c == 0:
                    pe.wait_ge(sem("f_u"), f)
                    pe.wait_ge(sem("f_scaled"), 1 + 4 * (f - 1))
            project(pe, f_block(f, 0), pair[0], before=u_before)

            def g_before(c):
                if c == 0 and not first:
                    pe.wait_ge(sem("f_g"), f)
                    pe.wait_ge(sem("f_scaled"), 1 + 4 * (f - 1))

            def turn_u(c):
                if c == 0:
                    pe.wait_ge(sem("f_u"), f + 1)
                    if not first:
                        pe.wait_ge(sem("f_conv"), f)
                    pe_turn_pairs(pe, f_u, "f_u_turned")
            project(pe, f_block(f, 1), pair[1], before=g_before, after=turn_u)

            def turn_g(c):
                if c == 0:
                    pe.wait_ge(sem("f_g"), f + 1)
                    if not first:
                        pe.wait_ge(sem("f_h"), f)
                    for b in range(2):
                        pe_transposes(pe, sc[b], f_g, [2 * b, 2 * b + 1]).then_inc(sem("f_g_turned"), 1)
            if first:
                turn_g(0)
            else:
                pe_f_output(pe, f, turn_g)

        def pe_second_block(pe):
            pe_second_attention(pe)
            pe.wait_ge(sem("diag"), 2)
            turn_groups(pe, 3, lambda j: None, True)
            pe_feed_forward(pe, 0)
            with pe.Fori(1, FG) as f:
                pe_feed_forward(pe, f)
            pe_f_output(pe, FG)

        def act_rms(act, n):
            for t in range(NT):
                act.wait_ge(sem("z_full"), NT * (n - 1) + t + 1)
                if t:
                    act.wait_ge(sem("ssq"), NT * (n - 1) + t)
                act.activation(junk[:, :], z[:, t, :], ACT.Square, accum_out=ssq[:, t, 0:1])\
                    .then_inc(sem("ssq"), 1)

        def act_blocks(act, b, slots):
            for c in range(CH):
                bb, cc = (b, 3) if c == 0 else (b + 1, c - 1)
                round_hi(act, bb, cc, b_width[bb - B_B0] if bb < F_B0 else CB)
                for task in slots.get(c, []):
                    task()

        def act_second_attention(act):
            act_rms(act, 1)
            turn_hi(act, 2, False)

            def done(b):
                act.wait_ge(sem("products"), CH * (B_B0 + b) + 4)

            def gates(c):
                for b in range(2):
                    n = 2 * c + b
                    act.wait_ge(sem("gate_mm"), n + 1)
                    act.activation(rows[:, n // 4, n % 4 * CB:(n % 4 + 1) * CB], sc[b][:, :], ACT.Copy)\
                        .then_inc(sem("gate_row"), 1)
            act_blocks(act, B_B0, {c: [lambda c=c: gates(c)] for c in range(CH)})

            def qi(n):
                done(n)
                if n == 1:
                    act.wait_ge(sem("i_q_turned"), 2)
                for t in range(NT):
                    ins = act.activation(i_q[:, t, :], pair[n][t][:, :], ACT.Copy)
                ins.then_inc(sem("i_q"), 1)

            def qiT(n):
                act.wait_ge(sem("i_q_turned"), 2 * n + 1)
                act.activation(i_qT[:, 4 * n:4 * n + 2, :], gview(turn[0][:, :], 2), ACT.Copy)\
                    .then_inc(sem("i_qT_a"), 1)
            act_blocks(act, B_B0 + 1, {0: [lambda: qi(0), lambda: qiT(0)]})
            act_blocks(act, B_B0 + 2, {0: [lambda: qi(1)]})

            def kiT():
                act.wait_ge(sem("i_k_turned"), 1)
                act.activation(i_kT[:, :], sc[0][:, 0:T], ACT.Copy).then_inc(sem("i_kT"), 1)

            def relu(heads):
                for h in heads:
                    act.wait_ge(sem("i_dot"), h + 1)
                    if h >= 2:
                        act.wait_ge(sem("i_added"), h - 1)
                    act.activation(i_relu[:, h % 2, :], sc[h % 2][:, 0:384], ACT.Relu).then_inc(sem("i_relu"), 1)
            act_blocks(act, B_B0 + 3, {0: [lambda: qiT(1), kiT], 1: [lambda: relu(INDEX_HEADS[1])],
                                       2: [lambda: relu(INDEX_HEADS[2])], 3: [lambda: relu(INDEX_HEADS[3])]})

            def kvc():
                done(3)
                for t in range(NT):
                    act.activation(b_kvc[:, t, :], pair[1][t][:, :], ACT.Copy).then_inc(sem("b_kvc"), 1)
                act.wait_ge(sem("b_kvc"), 2)
                for t in range(NT):
                    act.activation(junk2[:, :], b_kvc[:, t, T:2 * T], ACT.Square, accum_out=ssq[:, t, 1:2])\
                        .then_inc(sem("b_cssq"), 1)
                    act.wait_ge(sem("b_cssq"), t + 1)

            def kB(n):
                act.wait_ge(sem("b_kB"), 2 * n + 1)
                act.activation(b_kBT[:, 4 * n:4 * n + 2, :], gview(turn[0][:, :], 2), ACT.Copy)\
                    .then_inc(sem("b_kB_a"), 1)

            def vB():
                act.wait_ge(sem("i_added"), 16)
                for m in (0, 2):
                    act.wait_ge(sem("b_vB_mm"), m + 1)
                    act.activation(b_vB[:, m // 2, 0:CB], (turn[0], sc[0])[m // 2][:, :], ACT.Copy)\
                        .then_inc(sem("b_vB_a"), 1)
            act_blocks(act, B_B0 + 4, {0: [kvc], 1: [lambda: kB(0)], 2: [lambda: kB(1)], 3: [vB]})
            for g in range(4):
                def start(g=g):
                    done(4 + g)
                    if g == 0:
                        act.wait_ge(sem("b_kadup"), 1)
                        act.wait_ge(sem("b_kv_turned"), 2)
                    else:
                        act.wait_ge(sem("b_q_turned"), 2 * g)
                    for t in range(NT):
                        ins = act.activation(b_q[:, t, :], pair[0][t][:, :], ACT.Copy, scale=float(W_HD) ** -0.5)
                    ins.then_inc(sem("b_q"), 1)
                    act.wait_ge(sem("b_q_turned"), 2 * g + 1)
                    act.activation(b_qT[:, 0:2, :], gview(turn[0][:, :], 2), ACT.Copy).then_inc(sem("b_qT_a"), 1)

                def steps(c, g=g):
                    if c == 1 and 1 <= g <= 2:
                        act_b_outT(act, g - 1)
                    for what in B_STEPS.get(c, []):
                        kind, h = what[0], int(what[1])
                        n = 8 * g + h
                        if kind == "s":
                            act.wait_ge(sem("b_max"), n + 1)
                            for t, w in ((0, slice(0, P)), (1, slice(P, 384))):
                                ins = act.activation(b_s[:, h % 4, w], b_s[:, h % 4, w], ACT.Exp,
                                                     bias=b_nm[:, h, t:t + 1], accum_out=b_sum[:, h, t:t + 1])
                            ins.then_inc(sem("b_prob"), 1)
                        elif kind == "t":
                            act.wait_ge(sem("b_p_turned"), n + 1)
                            act.activation(b_pT[:, h % 2, :], turn[h % 2][:, 0:384], ACT.Copy)\
                                .then_inc(sem("b_pT"), 1)
                    if c == 3 and g < 2:
                        act.wait_ge(sem("b_esx"), g + 1)
                        act.activation(b_es[:, :, :], b_es[:, :, :], ACT.Exp).then_inc(sem("b_es"), 1)
                act_blocks(act, B_B0 + 5 + g, {0: [start], **{c: [lambda c=c, s=steps: s(c)] for c in (1, 2, 3)}})
            for g in range(1, 4):
                act_blocks(act, B_B0 + 8 + g, {0: [lambda g=g: act_b_outT(act, g + 1)]} if g < 3 else {})

        def act_b_outT(act, g):
            if g >= 2:
                act.wait_ge(sem("products"), CH * (B_B0 + 8 + g - 2) + 4)
            for b in range(2):
                act.wait_ge(sem("b_o_turned"), 2 * g + b + 1)
                act.activation(b_oh[:, g % 2, 2 * b:2 * b + 2, :], gview(turn[b][:, :], 2), ACT.Copy)\
                    .then_inc(sem("b_oh"), 1)

        def act_feed_forward(act, f):
            first = isinstance(f, int) and f == 0
            last = isinstance(f, int) and f == FG
            B = [f_block(f, 0), f_block(f, 1), f_block(f, 2)]
            nb = B[1] + 1 if first else B[2] + 1
            if last:
                round_hi(act, B[0], 3)
                act_f_hi(act, f)
                return
            ahead = [(B[0], 3), *((B[1], c) for c in range(4)), *([] if first else ((B[2], c) for c in range(4))),
                     (nb, 0), (nb, 1), (nb, 2)]

            def H(count):
                for _ in range(count):
                    round_hi(act, *ahead.pop(0))
            H(2)
            if not first:
                act_f_hi(act, f)
            H(2)
            act.wait_ge(sem("products"), CH * B[0] + 4)
            if not first:
                act.wait_ge(sem("f_u_turned"), 2 * f)
            for t in range(NT):
                ins = act.activation(f_u[:, t, :], pair[0][t][:, :], ACT.Copy)
            ins.then_inc(sem("f_u"), 1)
            H(2)
            act.wait_ge(sem("f_par"), f + 1)
            if not first:
                act.wait_ge(sem("f_h"), f)
            for k in range(4):
                if k % 2 == 0:
                    act.wait_ge(sem("f_u_turned"), 2 * f + k // 2 + 1)
                ins = act.activation(f_c[:, k, :], turn[k // 2][:, k % 2 * T:(k % 2 + 1) * T], ACT.Identity,
                                     bias=f_par[:, k, 3:4], scale=f_par[:, k, 2:3])
            ins.then_inc(sem("f_tap"), 1)
            H(2)
            act.wait_ge(sem("products"), CH * B[1] + 4)
            if not first:
                act.wait_ge(sem("f_g_turned"), 2 * f)
            for t in range(NT):
                ins = act.activation(f_g[:, t, :], pair[1][t][:, :], ACT.Copy)
            ins.then_inc(sem("f_g"), 1)
            act.wait_ge(sem("f_conv"), f + 1)
            act.activation(f_c[:, :, :], f_c[:, :, :], ACT.Silu).then_inc(sem("f_silu"), 1)
            H(len(ahead))

        def act_f_hi(act, f):
            act.wait_ge(sem("f_h"), f)
            if not (isinstance(f, int) and f == 1):
                act.wait_ge(sem("products"), CH * f_block(f, 0))
            act.activation(f_hh[:, :, :], f_h[:, :, :], ACT.Copy).then_inc(sem("f_hh"), 1)

        def act_second_block(act):
            act_second_attention(act)
            act.wait_ge(sem("b_scaled"), 16)
            act.dma_start(rows[:, 0, :], broadcast_row(norm_final_2, 0, D)).then_inc(sem("final_in"), 16)
            act_rms(act, 2)
            turn_hi(act, 3, False)
            act_feed_forward(act, 0)
            with act.Fori(1, FG) as f:
                act_feed_forward(act, f)
            act_feed_forward(act, FG)
            act_rms(act, 3)

        def vec_rms(v, n):
            v.wait_ge(sem("ssq"), NT * n)
            v.tensor_scalar(var[:, :], ssq[:, :, 0], 1.0 / D, RMS_EPS, ALU.mult, ALU.add).then_inc(sem("var"), 1)
            v.wait_ge(sem("rsqrt"), 2 + n)
            if n < 3:
                for t in range(NT):
                    ins = v.tensor_scalar(diag[:, t, :], ident[:, :], rstd[:, t:t + 1], None, ALU.mult)
                ins.then_inc(sem("diag"), 1)

        def vec_blocks(v, b, slots):
            for c in range(CH):
                bb, cc = (b, 3) if c == 0 else (b + 1, c - 1)
                split_lo(v, bb, cc, b_width[bb - B_B0] if bb < F_B0 else CB)
                for task in slots.get(c, []):
                    task()

        def vec_scaled_sum(v, which, n, done, c, banks, tmp, row):
            v.wait_ge(sem("products"), done)
            for t in range(NT):
                ins = v.tensor_tensor(tmp[:, t, :], banks[t][:, :], rows[:, row, c * CB:(c + 1) * CB], ALU.mult)
                if t == 0:
                    vec(ins)
            ins.then_inc(sem(which), 1)
            v.wait_ge(sem(which), n + 1)
            for t in range(NT):
                ins = v.tensor_tensor(z[:, t, c * CB:(c + 1) * CB], z[:, t, c * CB:(c + 1) * CB],
                                      tmp[:, t, :], ALU.add)
                vec(ins)
            vec_wait(v)

        def vec_second_attention(v):
            v.wait_ge(sem("rows1_in"), 32)
            v.wait_ge(sem("z_norm"), 4)
            v.wait_ge(sem("z_norm1"), 4)
            v.wait_ge(sem("turned"), 16)
            for t in range(NT):
                vec(v.tensor_tensor(z[:, t, :], z[:, t, :], rows[:, 0, :], ALU.mult))
                vec_wait(v)
                v.tensor_tensor(z[:, t, :], z[:, t, :], rows[:, 1, :], ALU.add).then_inc(sem("z_full"), 1)
            v.scalar_tensor_tensor(out=aff[:, :], in0=modc[:, KC:2 * KC], scalar=1.0, in1=par[:, 48:64],
                                   op0=ALU.add, op1=ALU.mult).then_inc(sem("aff"), 1)
            vec_rms(v, 1)
            v.wait_ge(sem("aff"), 1)
            turn_lo(v, 2, aff[:, :], modc[:, 0:KC])

            def gates(c):
                for b in range(2):
                    n = 2 * c + b
                    first = 2 * KC if n < 4 else 5 * KC
                    if n >= 2:
                        v.wait_ge(sem("gate_mm"), n - 1)
                    v.tensor_tensor(gate_diag[:, b, :, :], cast(ident[:, :], 4),
                                    modc[:, first + n % 4 * 4:first + n % 4 * 4 + 4].unsqueeze(2)
                                    .to_broadcast([P, 4, P]), ALU.mult).then_inc(sem("gate_diag"), 1)
            vec_blocks(v, B_B0, {c: [lambda c=c: gates(c)] for c in range(CH)})

            def qiT(n):
                v.wait_ge(sem("i_q_turned"), 2 * n + 2)
                v.tensor_copy(i_qT[:, 4 * n + 2:4 * n + 4, :], gview(turn[1][:, :], 2)).then_inc(sem("i_qT_v"), 1)
            vec_blocks(v, B_B0 + 1, {1: [lambda: qiT(0)]})
            vec_blocks(v, B_B0 + 2, {})

            def kiwi():
                v.wait_ge(sem("products"), CH * (B_B0 + 2) + 4)
                for t in range(NT):
                    v.tensor_copy(gview(i_kdup[:, t, :], 2), cast(pair[0][t][:, 0:HALF], 2))
                    ins = v.tensor_scalar(b_w[:, t, :], pair[0][t][:, HALF:HALF + 16],
                                          float(W_HD * W_HEADS) ** -0.5, None, ALU.mult)
                ins.then_inc(sem("i_kdup"), 1)

            def added(heads):
                v.wait_ge(sem("i_kdup"), 1)
                v.wait_ge(sem("causal_in"), 16)
                for h in heads:
                    v.wait_ge(sem("i_relu"), h + 1)
                    if h:
                        v.wait_ge(sem("i_added"), h)
                    for t, w in ((0, slice(0, P)), (1, slice(P, 384))):
                        ins = v.scalar_tensor_tensor(out=b_idx[:, w], in0=i_relu[:, h % 2, w],
                                                     scalar=b_w[:, t, h:h + 1], in1=b_idx[:, w],
                                                     op0=ALU.mult, op1=ALU.add)
                    ins.then_inc(sem("i_added"), 1)
            vec_blocks(v, B_B0 + 3, {0: [kiwi, lambda: qiT(1)], 1: [lambda: added(INDEX_HEADS[1])],
                                     2: [lambda: added(INDEX_HEADS[2])], 3: [lambda: added(INDEX_HEADS[3])]})

            def topk(rounds):
                v.wait_ge(sem("i_added"), 16)
                for _ in range(rounds):
                    for t, w in ((0, slice(0, P)), (1, slice(P, 384))):
                        vec(v.max(b_max8[:, t, :], b_idx[:, w]))
                    vec_wait(v)
                    for t, w in ((0, slice(0, P)), (1, slice(P, 384))):
                        vec(v.match_replace(b_idx[:, w], b_max8[:, t, :], b_idx[:, w], -3e38))
                    vec_wait(v)

            def select():
                v.tensor_scalar(b_sel[:, :], b_idx[:, :], -2e38, NEG, ALU.is_gt, ALU.mult).then_inc(sem("sel"), 1)

            def kadup():
                v.wait_ge(sem("b_kvc"), 2)
                for t in range(NT):
                    for kv in range(2):
                        v.tensor_copy(gview(b_kadup[:, t, kv, :], 2),
                                      cast(b_kvc[:, t, kv * HALF:(kv + 1) * HALF], 2))
                v.tensor_copy(b_va[:, :, :], b_kvc[:, :, P:2 * P]).then_inc(sem("b_kadup"), 1)
                v.wait_ge(sem("b_cssq"), 2)
                v.tensor_scalar(b_cvar[:, :], ssq[:, :, 1], 1.0 / RANK, RMS_EPS, ALU.mult, ALU.add)\
                    .then_inc(sem("b_cvar"), 1)
                v.wait_ge(sem("b_crsqrt"), 1)
                for t in range(NT):
                    ins = v.tensor_scalar(diag[:, t, :], ident[:, :], b_crs[:, t:t + 1], None, ALU.mult)
                ins.then_inc(sem("b_cdiag"), 1)

            def kvT():
                v.wait_ge(sem("b_kv_turned"), 2)
                v.tensor_copy(b_kaT[:, :, :], gview(turn[0][:, :], 2))
                for r in range(2):
                    ins = v.tensor_scalar(b_ckvT[:, r, :], turn[1][:, r * T:(r + 1) * T],
                                          par[:, 80 + r:81 + r], None, ALU.mult)
                ins.then_inc(sem("b_kvT"), 1)

            def kB(n):
                v.wait_ge(sem("b_kB"), 2 * n + 2)
                v.tensor_copy(b_kBT[:, 4 * n + 2:4 * n + 4, :], gview(turn[1][:, :], 2)).then_inc(sem("b_kB_v"), 1)

            def vB():
                for m in (1, 3):
                    v.wait_ge(sem("b_vB_mm"), m + 1)
                    v.tensor_copy(b_vB[:, m // 2, CB:2 * CB], (turn[1], sc[1])[m // 2][:, :])\
                        .then_inc(sem("b_vB_v"), 1)
            vec_blocks(v, B_B0 + 4, {0: [kadup, kvT], 1: [lambda: kB(0), lambda: topk(1)],
                                     2: [lambda: kB(1), lambda: topk(1)], 3: [vB, lambda: topk(1)]})

            for g in range(4):
                def start(g=g):
                    v.wait_ge(sem("b_q_turned"), 2 * g + 2)
                    v.tensor_copy(b_qT[:, 2:4, :], gview(turn[1][:, :], 2)).then_inc(sem("b_qT_v"), 1)
                    if g == 0:
                        v.wait_ge(sem("sink_in"), 16)
                        vec(v.tensor_scalar(b_nsink[:, :], b_sink[:, :], -1.0, None, ALU.mult))
                        topk(2)

                def steps(c, g=g):
                    if g == 3:
                        vec_scaled_sum(v, "b_scaled", c - 1, CH * (B_B0 + 8) + c, c - 1, pair[0], b_tmp, 0)
                    if g == 0 and c in (1, 2):
                        topk(1)
                    if g == 1 and c == 1:
                        topk(1)
                        select()
                    if c == 1 and 1 <= g <= 2:
                        vec_b_outT(v, g - 1)
                    for what in B_STEPS.get(c, []):
                        kind, h = what[0], int(what[1])
                        n = 8 * g + h
                        if kind != "s":
                            continue
                        if h == 0:
                            v.wait_ge(sem("bias_in"), 32 * (g + 1))
                            if g == 2:
                                v.wait_ge(sem("sel"), 1)
                        v.wait_ge(sem("b_score"), n + 1)
                        if n >= 4:
                            v.wait_ge(sem("b_p_turned"), n - 3)
                        s = b_s[:, h % 4, :]
                        v.tensor_tensor(s, sc[h % 2][:, 0:384], b_bias[:, h, :], ALU.add).then_inc(sem("b_read"), 1)
                        v.wait_ge(sem("b_read"), n + 1)
                        if g >= 2:
                            vec(v.tensor_tensor(s, s, b_sel[:, :], ALU.add))
                            vec_wait(v)
                        for t, w in ((0, slice(0, P)), (1, slice(P, 384))):
                            ins = v.tensor_reduce(b_nm[:, h, t:t + 1], s[:, w], AX, ALU.max, negate=True)
                        if g < 2:
                            vec(ins)
                            vec_wait(v)
                            ins = v.tensor_scalar(b_nm[:, h, :], b_nm[:, h, :], b_nsink[:, 8 * g + h:8 * g + h + 1],
                                                  None, ALU.min)
                        ins.then_inc(sem("b_max"), 1)
                    if c == 3:
                        finish(g)

                def finish(g):
                    if g < 2:
                        v.wait_ge(sem("b_max"), 8 * g + 8)
                        v.tensor_tensor(b_es[:, :, :], b_nm[:, :, :],
                                        b_sink[:, 8 * g:8 * g + 8].unsqueeze(2).to_broadcast([P, 8, NT]),
                                        ALU.add).then_inc(sem("b_esx"), 1)
                        v.wait_ge(sem("b_es"), g + 1)
                        vec(v.tensor_tensor(b_ri[:, :, :], b_sum[:, :, :], b_es[:, :, :], ALU.add))
                        vec_wait(v)
                        vec(v.reciprocal(b_ri[:, :, :], b_ri[:, :, :]))
                    else:
                        v.wait_ge(sem("b_prob"), 8 * g + 8)
                        vec(v.reciprocal(b_ri[:, :, :], b_sum[:, :, :]))
                    vec_wait(v)
                    v.wait_ge(sem("b_pv"), 8 * g + 8)
                    if 1 <= g <= 2:
                        v.wait_ge(sem("b_o_turned"), 2 * g)
                    if g == 3:
                        v.wait_ge(sem("b_q_turned"), 8)
                    for t in range(NT):
                        ins = v.tensor_tensor(gview(b_out(g)[:, t, :], 8), gview(pair[1][t][:, :], 8),
                                              b_ri[:, :, t].unsqueeze(2).to_broadcast([P, 8, HALF]), ALU.mult)
                    ins.then_inc(sem("b_og"), 1)
                vec_blocks(v, B_B0 + 5 + g, {0: [start], **{c: [lambda c=c, s=steps: s(c)] for c in (1, 2, 3)}})
            for g in range(1, 4):
                def slot(c, g=g):
                    if c == 0:
                        vec_scaled_sum(v, "b_scaled", 4 * g - 1, CH * (B_B0 + 7 + g) + 4, 3,
                                       pair[0] if g == 1 else pair[1], b_tmp, 0)
                        if g < 3:
                            vec_b_outT(v, g + 1)
                    else:
                        vec_scaled_sum(v, "b_scaled", 4 * g + c - 1, CH * (B_B0 + 8 + g) + c, c - 1,
                                       pair[(c - 1) % 2], b_tmp, 0)
                vec_blocks(v, B_B0 + 8 + g, {c: [lambda c=c, s=slot: s(c)] for c in range(CH)})
            vec_scaled_sum(v, "b_scaled", 15, CH * (B_B0 + 11) + 4, 3, pair[1], b_tmp, 0)
            v.sem_inc(sem("z_full"), NT)

        def vec_b_outT(v, g):
            for b in range(2):
                v.wait_ge(sem("b_oh"), 2 * g + b + 1)
                v.tensor_tensor(b_ol[:, g % 2, 2 * b:2 * b + 2, :], gview(turn[b][:, :], 2),
                                b_oh[:, g % 2, 2 * b:2 * b + 2, :].bitcast(F32), ALU.subtract)\
                    .then_inc(sem("b_ol"), 1)

        def vec_feed_forward(v, f):
            first = isinstance(f, int) and f == 0
            last = isinstance(f, int) and f == FG
            B = [f_block(f, 0), f_block(f, 1), f_block(f, 2)]
            nb = B[1] + 1 if first else B[2] + 1

            def low():
                v.wait_ge(sem("f_hh"), f)
                v.tensor_tensor(f_hl[:, :, :], f_h[:, :, :], f_hh[:, :, :].bitcast(F32), ALU.subtract)\
                    .then_inc(sem("f_hl"), 1)

            def sum_rows(b, c):
                vec_scaled_sum(v, "f_scaled", 1 + 4 * (f - 1) + c, CH * b + c + 1, c, pair[c % 2], f_y, 1)
            if last:
                split_lo(v, B[0], 3)
                low()
                for c in range(CH):
                    sum_rows(B[0], c)
                return
            ahead = [(B[0], 3), *((B[1], c) for c in range(4)), *([] if first else ((B[2], c) for c in range(4))),
                     (nb, 0), (nb, 1), (nb, 2)]

            def S_(count=1):
                for _ in range(count):
                    split_lo(v, *ahead.pop(0))
            S_()
            if not first:
                v.wait_ge(sem("f_conv"), f)
            v.tensor_copy(f_par[:, :, :], conv[:, bass.ds(4 * f, 4), :]).then_inc(sem("f_par"), 1)
            S_()
            if not first:
                low()
            S_(3)
            S_()
            v.wait_ge(sem("f_par"), f + 1)
            v.wait_ge(sem("f_tap"), f + 1)
            for tap in (1, 2):
                for k in range(4):
                    src = turn[k // 2][:, k % 2 * T:(k % 2 + 1) * T - tap]
                    ins = v.scalar_tensor_tensor(out=f_c[:, k, tap:], in0=src, scalar=f_par[:, k, 2 - tap:3 - tap],
                                                 in1=f_c[:, k, tap:], op0=ALU.mult, op1=ALU.add)
                    if tap == 1:
                        vec(ins)
                if tap == 1:
                    vec_wait(v)
            ins.then_inc(sem("f_conv"), 1)
            S_(2)
            if not first:
                S_()
                sum_rows(B[2], 0)
            v.wait_ge(sem("f_silu"), f + 1)
            if not first:
                v.wait_ge(sem("f_hh"), f)
                v.wait_ge(sem("f_hl"), f)
            for b in range(2):
                v.wait_ge(sem("f_g_turned"), 2 * f + b + 1)
                ins = v.tensor_tensor(f_h[:, 2 * b:2 * b + 2, :], gview(sc[b][:, :], 2),
                                      f_c[:, 2 * b:2 * b + 2, :], ALU.mult)
            ins.then_inc(sem("f_h"), 1)
            if not first:
                for c in range(1, CH):
                    S_()
                    sum_rows(B[2], c)
            assert not ahead

        def vec_second_block(v):
            vec_second_attention(v)
            v.scalar_tensor_tensor(out=aff[:, :], in0=modc[:, 4 * KC:5 * KC], scalar=1.0, in1=par[:, 64:80],
                                   op0=ALU.add, op1=ALU.mult).then_inc(sem("aff"), 1)
            vec_rms(v, 2)
            v.wait_ge(sem("aff"), 2)
            v.sem_inc(sem("f_scaled"), 1)
            turn_lo(v, 3, aff[:, :], modc[:, 3 * KC:4 * KC])
            vec_feed_forward(v, 0)
            with v.Fori(1, FG) as f:
                vs.enter(f, 1, VEC_F)
                vec_feed_forward(v, f)
            vs.leave(FG - 1)
            vec_feed_forward(v, FG)
            v.sem_inc(sem("z_full"), NT)
            vec_rms(v, 3)
            v.wait_ge(sem("final_in"), 16)
            for t in range(NT):
                v.scalar_tensor_tensor(out=z[:, t, :], in0=z[:, t, :], scalar=rstd[:, t:t + 1], in1=rows[:, 0, :],
                                       op0=ALU.mult, op1=ALU.mult).then_inc(sem("final"), 1)

        def sync_second_block(sp):
            for j in range(12):
                load(sp, B_B0 + j, b_blocks[j], b_width[j], halves=j == 3)
            for j in range(2):
                load(sp, f_block(0, j), f_blocks[j](0))
            with sp.Fori(1, FG) as f:
                for j in range(2):
                    load(sp, f_block(f, j), f_blocks[j](f))
                load(sp, f_block(f, 2), out_rows(w_f_out, f - 1))
            load(sp, f_block(FG, 0), out_rows(w_f_out, FG - 1))
            for t in range(NT):
                sp.wait_ge(sem("final"), t + 1)
                sp.dma_start(out[0][t * P:(t + 1) * P, :], z[:, t, :]).then_inc(sem("out"), 16)
            sp.wait_ge(sem("out"), 16 * NT)

        def pool_second_block(g):
            def get(to, src, name):
                g.dma_start(to, src).then_inc(sem(name), 16)

            def power(to, src, ready, value, done):
                g.wait_ge(sem(ready), value)
                g.tensor_tensor(to, src, minus_half[:, 0:NT], ALU.pow).then_inc(sem(done), 1)

            g.wait_ge(sem("r_turned"), 2 * R_HEADS)
            g.wait_ge(sem("r_ol"), 2 * R_HEADS)
            g.wait_ge(sem("products"), CH * B_B0)
            get(b_idx[:, :], causal_c, "causal_in")
            get(b_sink[:, :], broadcast_row(attn_sinks_2, 0, 16), "sink_in")
            for r in range(2):
                for to, src in ((b_wuk, w_uk_2), (b_wuv, w_uv_2)):
                    get(gview(to[:, r, :], W_HEADS),
                        bass.AP(tensor=src.tensor, offset=src.offset + r * P * W_HD,
                                ap=[[W_HD, P], [RANK * W_HD, W_HEADS], [1, W_HD]]), "b_w_in")
            power(rstd[:, :], var[:, :], "var", 3, "rsqrt")
            power(b_crs[:, :], b_cvar[:, :], "b_cvar", 1, "b_crsqrt")
            for grp in range(4):
                if grp:
                    g.wait_ge(sem("b_read"), 8 * grp)
                else:
                    g.wait_ge(sem("b_kv_turned"), 2)
                row = toep.offset + 8 * grp * P * TOEP + P - 1
                get(b_bias[:, :, 0:P], bass.AP(tensor=toep.tensor, offset=row + P,
                                               ap=[[TOEP - 1, P], [P * TOEP, 8], [1, P]]), "bias_in")
                get(b_bias[:, :, P:384], bass.AP(tensor=toep.tensor, offset=row,
                                                 ap=[[TOEP - 1, P], [P * TOEP, 8], [1, T]]), "bias_in")
            power(rstd[:, :], var[:, :], "var", 4, "rsqrt")
            power(rstd[:, :], var[:, :], "var", 5, "rsqrt")

        block = ctx.enter_context(nc.Block())

        @block.sync
        def _(sp):
            sync_first_block(sp)
            sync_second_block(sp)

        @block.gpsimd
        def _(g):
            pool_first_block(g)
            pool_second_block(g)

        @block.scalar
        def _(act):
            act_first_block(act)
            act_second_block(act)

        @block.vector
        def _(v):
            vec_first_block(v)
            vec_second_block(v)

        @block.tensor
        def _(pe):
            pe_first_block(pe)
            pe_second_block(pe)


NAMES = ["x", "attn_w_in", "attn_q_gain", "attn_k_gain", "attn_w_out", "ret_w_in", "ret_decay_exp",
         "ret_w_out", "ln_gain", "ln_bias", "c_2", "w_mod_2", "b_mod_2", "norm_attn_2", "w_in_2",
         "attn_sinks_2", "kv_norm_2", "w_uk_2", "w_uv_2", "rel_bias_2", "w_out_2", "norm_ffn_2",
         "w_up_2", "conv_w_2", "conv_b_2", "w_down_2", "norm_final_2"]
CONSTANTS = ["ident", "cos_a", "sin_a", "cos_r", "sin_r", "ahead", "behind", "onehot", "mask", "causal"]


def kernel(**inputs):
    import concourse.bacc as _bacc
    from concourse.bass_utils import run_bass_kernel_spmd as _run

    nc = _bacc.Bacc("TRN2", target_bir_lowering=False, num_devices=1)
    arrays, args = {}, []
    constants = shape_constants()
    for name in NAMES + CONSTANTS:
        a = np.ascontiguousarray(inputs[name] if name in inputs else constants[name])
        arrays[f"in_{name}_dram"] = a
        args.append(nc.dram_tensor(f"in_{name}_dram", a.shape, mybir.dt.from_np(a.dtype),
                                   kind="ExternalInput").ap())
    args.append(nc.dram_tensor("out_0_dram", (1, T, D), F32, kind="ExternalOutput").ap())
    build(nc, *args)
    r = _run(nc, [arrays], core_ids=[0])
    return r.results[0]["out_0_dram"]
```

```python
from contextlib import ExitStack

import numpy as np
import concourse.bass as bass
from concourse import mybir

F32 = mybir.dt.float32
F32R = mybir.dt.float32r
ALU = mybir.AluOpType
ACT = mybir.ActivationFunctionType
AX = mybir.AxisListType.X

P = 128
D = 2048
T = 256
NT = T // P
KC = D // P
CB = 512
CH = 4
NEG = -1e30

A_HD, A_KV = 128, 4
R_HEADS, R_DK, R_DV = 8, 256, 512
W_HD, W_HEADS = 64, 16
RANK, TOPK, WINDOW = 256, 64, 128
FF = 5632
FG = FF // CB
ALPHA = 4.0 ** 0.25
LN_EPS, RMS_EPS = 1e-5, 1e-6
MOD_BLOCKS = 6 * D // CB
TOEP = 384
COPIES = 32
VEC_A, VEC_R, VEC_F = 45, 37, 16

INDEX_HEADS = {1: range(0, 4), 2: range(4, 9), 3: range(9, 16)}
A_B0 = 0
R_B0 = A_B0 + 4 * A_KV
B_B0 = R_B0 + 4 * R_HEADS
F_B0 = B_B0 + 12


def rope_tables(head_dim):
    pos = np.arange(T)
    row, col = (pos // 64).astype(np.float32), (pos % 64).astype(np.float32)
    half = head_dim // 2
    inv = (np.float32(10000.0) ** (-np.arange(0, half, 2, dtype=np.float32) / np.float32(half))).astype(np.float32)
    ar, ac = row[:, None] * inv, col[:, None] * inv
    ang = np.concatenate([ar, ar, ac, ac], axis=-1)
    sign = np.repeat(np.array([-1, 1, -1, 1], np.float32), head_dim // 4)
    return np.cos(ang).astype(np.float32), (np.sin(ang) * sign).astype(np.float32)


def shape_constants():
    cos_a, sin_a = rope_tables(A_HD)
    cos_r, sin_r = rope_tables(R_DK)
    s, t = np.arange(T)[:, None], np.arange(T)[None, :]
    ahead = np.maximum(t - s, 0).astype(np.float32)
    behind = np.maximum(s - t, 0).astype(np.float32)
    dist = 255 - np.arange(TOEP)
    n = np.maximum(dist, 0)
    nf = np.maximum(n, 1).astype(np.float32)
    large = 16 + (np.log(nf / np.float32(16)) / np.float32(np.log(128 / 16)) * np.float32(16)).astype(np.int32)
    bucket = np.where(n < 16, n, np.minimum(large, 31))
    onehot = (np.arange(32)[:, None] == bucket[None, :]).astype(np.float32)
    ok = np.stack([(dist >= 0) & (dist < WINDOW)] * W_HEADS + [dist >= 0] * W_HEADS)
    onehot *= (dist >= 0)[None, :]
    mask = np.where(ok, 0.0, NEG).astype(np.float32)
    i = np.arange(P)[:, None]
    causal = np.concatenate([np.where(np.arange(P)[None, :] <= i, 0.0, NEG),
                             np.where(np.arange(T)[None, :] <= i + P, 0.0, NEG)], axis=1).astype(np.float32)
    return {"ident": np.eye(P, dtype=np.float32), "cos_a": cos_a, "sin_a": sin_a, "cos_r": cos_r,
            "sin_r": sin_r, "ahead": ahead, "behind": behind, "onehot": onehot, "mask": mask,
            "causal": causal}


class Count:

    def __init__(self):
        self.n, self.reg = 0, None

    def one(self):
        self.n += 1
        return 1

    def now(self):
        return self.n if self.reg is None else self.n + self.reg

    def enter(self, index, first, per):
        self.start, self.per, self.reg = self.n, per, per * (index - first)

    def leave(self, trips):
        assert self.n - self.start == self.per, (self.n - self.start, self.per)
        self.n, self.reg = self.start + self.per * trips, None


def build(nc, x, attn_w_in, attn_q_gain, attn_k_gain, attn_w_out, ret_w_in, ret_decay_exp,
          ret_w_out, ln_gain, ln_bias, c_2, w_mod_2, b_mod_2, norm_attn_2, w_in_2, attn_sinks_2,
          kv_norm_2, w_uk_2, w_uv_2, rel_bias_2, w_out_2, norm_ffn_2, w_up_2, conv_w_2, conv_b_2,
          w_down_2, norm_final_2, ident_c, cos_a_c, sin_a_c, cos_r_c, sin_r_c, ahead_c, behind_c,
          onehot_c, mask_c, causal_c, out):
    ctx = ExitStack()
    with ctx:
        at = {"byte": 16512}

        def take(name, shape, dtype=F32):
            t = nc.alloc_sbuf_tensor_at(name, [P, *shape], dtype, offset=at["byte"])
            at["byte"] += -(-4 * int(np.prod(shape)) // 32) * 32
            return t

        def over(name, base, shape, dtype):
            return nc.alloc_sbuf_tensor_at(name, [P, *shape], dtype, offset=base)

        raw_at = at["byte"]
        raw = take("raw", [CH, CH, CB])
        w_lo = over("w_lo", raw_at, [CH, CH, CB], F32R)
        w_hi = take("w_hi", [CH, CH, CB], F32R)
        x_hi = take("x_hi", [KC, T], F32R)
        x_lo_at = at["byte"]
        x_lo = take("x_lo", [KC, T], F32R)
        b_tmp = over("b_tmp", x_lo_at, [NT, CB], F32)
        x_mid = over("x_mid", x_lo_at, [KC, T], F32)
        z = take("z", [NT, D])
        rows = take("rows", [2, D])
        ident = take("ident", [P])
        ones = take("ones", [P])
        par = take("par", [82])
        bmod = take("bmod", [6 * KC])
        modc = take("modc", [6 * KC])
        csilu = take("csilu", [KC])
        aff = take("aff", [KC])
        stats = take("stats", [NT, 4, 6])
        mv = take("mv", [NT, 2])
        rstd = take("rstd", [NT])
        var = take("var", [NT])
        spare = take("spare", [1])
        minus_half = take("minus_half", [8])
        nmr = take("nmr", [NT])
        ssq = take("ssq", [NT, 4])
        diag = take("diag", [NT, P])
        conv = take("conv", [FF // P, 4])
        r_e, r_u = take("r_e", [16]), take("r_u", [16])
        r_lg, r_m, r_n = take("r_lg", [16]), take("r_m", [16]), take("r_n", [16])
        arena = at["byte"]

        cos_q, sin_q = take("cos_q", [NT, A_HD]), take("sin_q", [NT, A_HD])
        cos_k, sin_k = take("cos_k", [NT, A_HD]), take("sin_k", [NT, A_HD])
        ropet = take("ropet", [CB])
        a_sq = take("a_sq", [NT, CB])
        a_ss, a_rs = take("a_ss", [2, NT, 4]), take("a_rs", [2, NT, 4])
        a_q, a_k = take("a_q", [NT, CB]), take("a_k", [NT, A_HD])
        a_v = take("a_v", [NT, A_HD])
        a_qT, a_kT = take("a_qT", [4, T]), take("a_kT", [T])
        a_p_at = at["byte"]
        a_p = take("a_p", [4, NT, T])
        a_pT = take("a_pT", [2, NT, T])
        a_nmax, a_sum, a_rinv = take("a_nmax", [4, NT]), take("a_sum", [4, NT]), take("a_rinv", [4, NT])
        a_sg, a_og = take("a_sg", [NT, CB]), take("a_og", [NT, CB])
        a_oh, a_ol = take("a_oh", [4, T], F32R), take("a_ol", [4, T], F32R)
        a_end = at["byte"]

        at["byte"] = arena
        cos_r, sin_r = take("cos_r", [NT, R_DK]), take("sin_r", [NT, R_DK])
        r_decay = take("r_decay", [R_HEADS, NT, T])
        r_t = take("r_t", [CB])
        r_qk, r_v = take("r_qk", [NT, CB]), take("r_v", [NT, R_DV])
        r_sg = take("r_sg", [NT, R_DV])
        r_og_at = at["byte"]
        r_og = take("r_og", [NT, R_DV])
        r_qT, r_kT, r_s = take("r_qT", [2, T]), take("r_kT", [2, T]), take("r_s", [NT, T])
        r_oh_at = at["byte"]
        r_oh, r_ol = take("r_oh", [4, T], F32R), take("r_ol", [4, T], F32R)
        r_pos = over("r_pos", r_og_at, [2, NT, T], F32)
        r_back = over("r_back", r_oh_at, [2, NT, T], F32)
        r_st, r_mv, r_rs = take("r_st", [NT, 6]), take("r_mv", [NT, 2]), take("r_rs", [NT])
        r_var = take("r_var", [NT])
        r_end = at["byte"]
        at["byte"] = max(a_end, r_end)

        mod_at = at["byte"]
        m_raw = take("m_raw", [2, CH, CB])
        m_acc = take("m_acc", [2, CB])
        top = at["byte"]
        assert top <= 229344, top

        at["byte"] = arena
        b_kBT = take("b_kBT", [8, T])
        b_vB = take("b_vB", [NT, W_HEADS * W_HD])
        b_kaT = take("b_kaT", [2, T])
        b_va = take("b_va", [NT, P])
        b_bias = take("b_bias", [8, 384])
        b_q = take("b_q", [NT, CB])
        b_qT = take("b_qT", [4, T])
        b_s_at = at["byte"]
        b_s = take("b_s", [4, 384])
        junk2_at = at["byte"]
        b_pT = take("b_pT", [2, 384])
        b_o = take("b_o", [NT, CB])
        b_ckvT = take("b_ckvT", [2, T])
        b_idx, b_sel = take("b_idx", [384]), take("b_sel", [384])
        b_max8 = take("b_max8", [NT, 8])
        b_w = take("b_w", [NT, 16])
        b_sink, b_nsink = take("b_sink", [16]), take("b_nsink", [16])
        b_nm, b_sum, b_es, b_ri = (take(n, [8, NT]) for n in ("b_nm", "b_sum", "b_es", "b_ri"))
        oT_at = at["byte"]
        b_oh, b_ol = take("b_oh", [2, 4, T], F32R), take("b_ol", [2, 4, T], F32R)
        b_end = at["byte"]
        assert b_end <= 229344, b_end
        b_wuk = over("b_wuk", oT_at, [2, W_HEADS * W_HD], F32)
        b_wuv = over("b_wuv", oT_at + 8192, [2, W_HEADS * W_HD], F32)
        at["byte"] = arena
        i_qT = take("i_qT", [8, T])
        i_kdup, i_kT = take("i_kdup", [NT, P]), take("i_kT", [T])
        i_relu = take("i_relu", [2, 384])
        i_end = at["byte"]
        assert i_end <= arena + 16384
        at["byte"] = arena + 16384 + 2048 + 1024
        i_q = take("i_q", [NT, CB])
        b_kvc = take("b_kvc", [NT, CB])
        b_kadup = take("b_kadup", [NT, 2, P])

        b_cvar, b_crs = take("b_cvar", [NT]), take("b_crs", [NT])
        junk = over("junk", arena, [D], F32)
        junk2 = over("junk2", junk2_at, [T], F32)
        gate_diag = over("gate_diag", b_s_at, [2, 4, P], F32)

        at["byte"] = arena
        f_u, f_g = take("f_u", [NT, CB]), take("f_g", [NT, CB])
        f_c, f_h = take("f_c", [4, T]), take("f_h", [4, T])
        f_par = take("f_par", [4, 4])
        f_hh, f_hl = take("f_hh", [4, T], F32R), take("f_hl", [4, T], F32R)
        f_y = take("f_y", [NT, CB])
        f_zw = take("f_zw", [NT, D])
        par_rows, bmod_rows = over("par_rows", a_p_at, [P], F32), over("bmod_rows", a_p_at + 512, [P], F32)
        conv_rows = over("conv_rows", a_p_at + 1024, [2, P], F32)
        at["byte"] = mod_at
        t_hot = nc.alloc_sbuf_tensor_at("t_hot", [32, TOEP], F32, offset=mod_at + 16384)
        t_mask = nc.alloc_sbuf_tensor_at("t_mask", [32, TOEP], F32, offset=mod_at + 16384 + 1536)
        t_rel = nc.alloc_sbuf_tensor_at("t_rel", [32, 32], F32, offset=a_end - 4096)
        t_out = nc.alloc_sbuf_tensor_at("t_out", [32, TOEP], F32, offset=a_end - 8192)

        toep = nc.dram_tensor("toeplitz_rows", (32, COPIES, TOEP), F32, kind="Internal").ap()

        def bank(name):
            return ctx.enter_context(nc.psum_tensor(name, [P, CB], F32))

        pair = [[bank("pair0_t0"), bank("pair0_t1")], [bank("pair1_t0"), bank("pair1_t1")]]
        turn = [bank("turn0"), bank("turn1")]
        sc = [bank("sc0"), bank("sc1")]

        S = {}

        def sem(name):
            if name not in S:
                S[name] = ctx.enter_context(nc.semaphore(name))
            return S[name]

        def gview(ap, n):
            return ap.rearrange("p (n w) -> p n w", n=n)

        def swapped(ap, groups, width, part):
            v = ap.rearrange("p (g h s w) -> p g h s w", g=groups, h=2, s=2, w=width)
            return v[:, :, :, part, :]

        def cast(ap, groups):
            w = ap.shape[-1]
            return ap.unsqueeze(1).to_broadcast([P, groups, w])

        w_attn = attn_w_in[0].rearrange("(k p) n -> p k n", p=P)
        w_attn_out = attn_w_out[0].rearrange("(k p) n -> p k n", p=P)
        w_ret = ret_w_in[0].rearrange("(k p) n -> p k n", p=P)
        w_ret_out = ret_w_out[0].rearrange("(k p) n -> p k n", p=P)
        w_b = w_in_2[0].rearrange("(k p) n -> p k n", p=P)
        w_b_out = w_out_2[0].rearrange("(k p) n -> p k n", p=P)
        w_f = w_up_2[0].rearrange("(k p) n -> p k n", p=P)
        w_f_out = w_down_2[0].rearrange("(k p) n -> p k n", p=P)
        w_m = w_mod_2[0].rearrange("(k p) n -> p k n", p=P)

        def cols(w, first, width=CB):
            return lambda c: w[:, CH * c:CH * c + CH, bass.ds(first, width)]

        def two(w, lo, hi, step, first, width):
            v = w[:, :, lo:hi].rearrange("p k (s n) -> p k s n", n=step)
            return lambda c: v[:, CH * c:CH * c + CH, :, bass.ds(first, width)]

        def out_rows(w, g):
            return lambda c: w[:, bass.ds(CH * g, CH), c * CB:(c + 1) * CB]

        a_blocks = [lambda g: cols(w_attn, g * CB),
                    lambda g: two(w_attn, D, D + 2 * CB, CB, g * A_HD, A_HD),
                    lambda g: cols(w_attn, D + 2 * CB + g * CB)]
        r_blocks = [lambda g: two(w_ret, 0, 2 * D, D, g * R_DK, R_DK),
                    lambda g: cols(w_ret, 2 * D + g * CB),
                    lambda g: cols(w_ret, 4 * D + g * CB)]
        f_blocks = [lambda g: cols(w_f, g * CB), lambda g: cols(w_f, FF + g * CB)]
        b_blocks = [cols(w_b, 2560), cols(w_b, 3072), cols(w_b, 3584, 80),
                    two(w_b, 1024, 3584, 1280, 0, 256), cols(w_b, 0), cols(w_b, 512),
                    cols(w_b, 1280), cols(w_b, 1792), *(out_rows(w_b_out, g) for g in range(4))]
        b_width = [CB, CB, 80] + [CB] * 9

        def chunk(t, c, width=CB):
            return t[:, c, :, 0:width]

        def load(sp, b, source, width=CB, halves=False):
            for c in range(CH):
                if not isinstance(b, int) or b > 0:
                    sp.wait_ge(sem("products"), CH * b + c - CH + 1)
                for h in range(2):
                    if halves:
                        to = raw[:, c, :, h * width // 2:(h + 1) * width // 2]
                        src = source(c)[:, :, h, :]
                    else:
                        to = raw[:, c, 2 * h:2 * h + 2, 0:width]
                        src = source(c)[:, 2 * h:2 * h + 2, :]
                    sp.dma_start(to, src).then_inc(sem(f"chunk_in{c}"), 16)

        def round_hi(act, b, c, width=CB):
            act.wait_ge(sem(f"chunk_in{c}"), 32 * (b + 1))
            act.activation(chunk(w_hi, c, width), chunk(raw, c, width), ACT.Copy).then_inc(sem("hi"), 1)

        def split_lo(v, b, c, width=CB):
            v.wait_ge(sem("hi"), CH * b + c + 1)
            v.tensor_tensor(chunk(w_lo, c, width), chunk(raw, c, width),
                            chunk(w_hi, c, width).bitcast(F32), ALU.subtract).then_inc(sem("lo"), 1)

        def product(pe, to, xh, xl, c, k, width, start, stop):
            wh, wl = w_hi[:, c, k, 0:width], w_lo[:, c, k, 0:width]
            pe.matmul(to, xh, wh, start=start, stop=False)
            pe.matmul(to, xh, wl, start=False, stop=False)
            return pe.matmul(to, xl, wh, start=False, stop=stop)

        def project(pe, b, banks, width=CB, before=None, after=None):
            for c in range(CH):
                if before:
                    before(c)
                pe.wait_ge(sem("lo"), CH * b + c + 1)
                for k in range(CH):
                    kk = CH * c + k
                    for t in range(NT):
                        mm = product(pe, banks[t][:, 0:width], x_hi[:, kk, t * P:(t + 1) * P],
                                     x_lo[:, kk, t * P:(t + 1) * P], c, k, width,
                                     kk == 0, kk == KC - 1)
                mm.then_inc(sem("products"), 1)
                if after:
                    after(c)

        def output(pe, b, oh, ol, order, before, after=None):
            for c in range(CH):
                before(c)
                pe.wait_ge(sem("lo"), CH * b + c + 1)
                for t in range(NT):
                    for k in range(CH):
                        mm = product(pe, pair[order[c]][t][:, :], oh[:, k, t * P:(t + 1) * P],
                                     ol[:, k, t * P:(t + 1) * P], c, k, CB, k == 0, k == CH - 1)
                mm.then_inc(sem("products"), 1)
                if after:
                    after(c)

        turn_bank = [turn[0], turn[1], sc[0], sc[1], pair[1][0], pair[1][1]]

        def turn_groups(pe, n, ready, scaled):
            for j in range(KC // 2):
                ready(j)
                if j >= 6 and n == 0:
                    pe.wait_ge(sem("turn_lo"), j - 6 + 1)
                elif j >= 6:
                    pe.wait_ge(sem("turn_mid"), 8 * (n - 1) + j - 6 + 1)
                for k in range(2):
                    for t in range(NT):
                        to = turn_bank[j % 6][:, k * T + t * P:k * T + (t + 1) * P]
                        src = z[:, t, (2 * j + k) * P:(2 * j + k + 1) * P]
                        if scaled:
                            mm = pe.matmul(to, src, diag[:, t, :], start=True, stop=True)
                        else:
                            mm = pe.transpose(to, src, ident[:, :])
                mm.then_inc(sem("turned"), 1)

        def turn_hi(act, n, plain):
            for j in range(KC // 2):
                if plain:
                    act.wait_ge(sem("turned"), 8 * n + j + 1)
                    src = gview(turn_bank[j % 6][:, :], 2)
                else:
                    act.wait_ge(sem("turn_mid"), 8 * (n - 1) + j + 1)
                    src = x_mid[:, 2 * j:2 * j + 2, :]
                act.activation(x_hi[:, 2 * j:2 * j + 2, :], src, ACT.Copy).then_inc(sem("turn_hi"), 1)

        def turn_lo(v, n, gain=None, bias=None):
            def low(j, src):
                v.wait_ge(sem("turn_hi"), 8 * n + j + 1)
                ins = v.tensor_tensor(x_lo[:, 2 * j:2 * j + 2, :], src,
                                      x_hi[:, 2 * j:2 * j + 2, :].bitcast(F32), ALU.subtract)
                ins.then_inc(sem("turn_lo"), 1)
            if gain is None:
                for j in range(KC // 2):
                    v.wait_ge(sem("turned"), 8 * n + j + 1)
                    low(j, gview(turn_bank[j % 6][:, :], 2))
                return
            for j in range(KC // 2 + 2):
                if j < KC // 2:
                    v.wait_ge(sem("turned"), 8 * n + j + 1)
                    for k in range(2):
                        kk = 2 * j + k
                        ins = v.tensor_scalar(x_mid[:, kk, :], turn_bank[j % 6][:, k * T:(k + 1) * T],
                                              gain[:, kk:kk + 1], bias[:, kk:kk + 1], ALU.mult, ALU.add)
                    ins.then_inc(sem("turn_mid"), 1)
                if j >= 2:
                    low(j - 2, x_mid[:, 2 * (j - 2):2 * (j - 2) + 2, :])

        def pe_transposes(pe, to, src, tiles):
            for m in tiles:
                for t in range(NT):
                    i = (m - tiles[0]) * NT + t
                    mm = pe.transpose(to[:, i * P:(i + 1) * P], src[:, t, m * P:(m + 1) * P], ident[:, :])
            return mm

        def pe_mod(pe, step):
            pe.wait_ge(sem("mod_used"), 8 * step + 8)
            for m in range(2):
                for q in range(4):
                    mm = pe.matmul(turn[0][:, 4 * m + q:4 * m + q + 1], m_acc[:, m, q * P:(q + 1) * P],
                                   ones[:, 0:1], start=True, stop=True)
            mm.then_inc(sem("mod_cols"), 1)

        def a_block(i, j):
            return A_B0 + 4 * i - 1 + j if not isinstance(i, int) or i > 0 else A_B0 + j

        def pe_a_output(pe, i, after=None):
            last = isinstance(i, int) and i == A_KV

            def before(c):
                if c == 0:
                    pe.wait_ge(sem("a_ol"), 2 * i)
                    pe.wait_ge(sem("a_sg"), i if last else i + 1)
                elif c == 1:
                    if not last:
                        pe.wait_ge(sem("a_krot"), i + 1)
                else:
                    pe.wait_ge(sem("a_sum_z"), 2 + 4 * (i - 1) + c - 1)
            output(pe, a_block(i, 0) if last else a_block(i, 3), a_oh, a_ol, [0, 1, 0, 1], before, after)

        def pe_a_turn(pe, i):
            pe.wait_ge(sem("a_og"), i)
            if not (isinstance(i, int) and i == A_KV):
                pe.wait_ge(sem("mod_read"), i)
            for b in range(2):
                pe_transposes(pe, turn[b], a_og, [2 * b, 2 * b + 1]).then_inc(sem("a_turned"), 1)

        def pe_attention(pe, i):
            first = isinstance(i, int) and i == 0

            def arrived(c):
                if first:
                    pe.wait_ge(sem("turn_lo"), 2 * (c + 1))
                elif c == 0:
                    pe.wait_ge(sem("a_sg"), i)
                    pe.wait_ge(sem("a_sum_z"), 2 + 4 * (i - 1) - 1)

            def mod(c):
                if c == 1 and not first:
                    pe_mod(pe, i - 1)
            project(pe, a_block(i, 0), pair[0], before=arrived, after=mod)
            if first:
                pe_params(pe)
            else:
                pe_a_turn(pe, i)

            def kv_free(c):
                if c == 0 and not first:
                    pe.wait_ge(sem("a_krot"), i)
                    pe.wait_ge(sem("a_sum_z"), 2 + 4 * (i - 1))
            project(pe, a_block(i, 1), pair[1], width=2 * A_HD, before=kv_free)

            def q_read(c):
                if c == 0:
                    pe.wait_ge(sem("a_qrot"), i + 1)

            def turn_qk():
                if not first:
                    pe.wait_ge(sem("a_ol"), 2 * i)
                else:
                    pe.wait_ge(sem("par_read"), 2)
                pe_transposes(pe, turn[0], a_q, [0, 1]).then_inc(sem("a_qk_turned"), 1)
                pe_transposes(pe, turn[1], a_q, [2, 3]).then_inc(sem("a_qk_turned"), 1)
                pe.wait_ge(sem("a_krot"), i + 1)
                if not first:
                    pe.wait_ge(sem("a_og"), i)
                pe_transposes(pe, sc[0], a_k, [0]).then_inc(sem("a_qk_turned"), 1)

            def scores(h):
                if h >= 2:
                    pe.wait_ge(sem("a_prob"), 4 * i + h - 1)
                for t in range(NT):
                    mm = pe.matmul(sc[(h + 1) % 2][:, t * T:(t + 1) * T], a_qT[:, h, t * P:(t + 1) * P],
                                   a_kT[:, :], start=True, stop=True)
                mm.then_inc(sem("a_score"), 1)

            def turn_probs(h):
                pe.wait_ge(sem("a_prob"), 4 * i + h + 1)
                if h >= 2:
                    pe.wait_ge(sem(f"a_pT{h % 2}"), 2 * i + 1)
                for k in range(NT):
                    for t in range(NT):
                        mm = pe.transpose(turn[h % 2][:, k * T + t * P:k * T + (t + 1) * P],
                                          a_p[:, h, t, k * P:(k + 1) * P], ident[:, :])
                mm.then_inc(sem("a_p_turned"), 1)

            def values(h):
                pe.wait_ge(sem(f"a_pT{h % 2}"), 2 * i + h // 2 + 1)
                for t in range(NT):
                    for k in range(NT):
                        mm = pe.matmul(sc[t][:, h * A_HD:(h + 1) * A_HD], a_pT[:, h % 2, k, t * P:(t + 1) * P],
                                       a_v[:, k, :], start=k == 0, stop=k == NT - 1)
                mm.then_inc(sem("a_pv"), 1)

            def along_gate(c):
                if c == 1:
                    turn_qk()
                elif c == 2:
                    pe.wait_ge(sem("a_qT_act"), i + 1)
                    pe.wait_ge(sem("a_qkT_dve"), i + 1)
                    scores(0)
                    scores(1)
                elif c == 3:
                    scores(2)
                    scores(3)

            def between(c):
                if c == 1:
                    turn_probs(0)
                    turn_probs(1)
                elif c == 2:
                    pe.wait_ge(sem("a_prob"), 4 * i + 4)
                    values(0)
                    turn_probs(2)
                    values(1)
                    turn_probs(3)
                elif c == 3:
                    values(2)
                    values(3)
            project(pe, a_block(i, 2), pair[0], before=q_read, after=along_gate)
            if first:
                for c in range(CH):
                    between(c)
            else:
                pe_a_output(pe, i, between)

        def pe_params(pe):
            pe.wait_ge(sem("par_in"), 16 * 13)
            pe.transpose(sc[0][:, 0:82], par_rows[0:82, :], ident[0:82, 0:82])
            pe.transpose(sc[0][:, 128:224], bmod_rows[0:96, :], ident[0:96, 0:96])
            for m in range(2):
                mm = pe.transpose(sc[0][:, 256 + 128 * m:344 + 128 * m], conv_rows[0:88, m, :],
                                  ident[0:88, 0:88])
            mm.then_inc(sem("par_turned"), 1)
            pe.matmul(sc[1][0:32, 0:TOEP], t_rel[:, :], t_hot[:, :], start=True, stop=True)\
                .then_inc(sem("par_turned"), 1)

        def r_block(i, j):
            return R_B0 + 4 * i - 1 + j if not isinstance(i, int) or i > 0 else R_B0 + j

        def pe_r_output(pe, i, after=None):
            last = isinstance(i, int) and i == R_HEADS

            def before(c):
                if c == 0:
                    pe.wait_ge(sem("r_ol"), 2 * i)
                    pe.wait_ge(sem("r_sg"), i if last else i + 1)
                elif c == 1:
                    if not last:
                        pe.wait_ge(sem("r_v"), i + 1)
                else:
                    pe.wait_ge(sem("r_sum_z"), 2 + 4 * (i - 1) + c - 1)
            output(pe, r_block(i, 0) if last else r_block(i, 3), r_oh, r_ol, [0, 1, 0, 1], before, after)

        def pe_r_turn(pe, i):
            pe.wait_ge(sem("r_og"), i)
            if not (isinstance(i, int) and i == R_HEADS):
                pe.wait_ge(sem("mod_read"), A_KV + i)
            for b in range(2):
                pe_transposes(pe, turn[b], r_og, [2 * b, 2 * b + 1]).then_inc(sem("r_turned"), 1)

        def pe_retention(pe, i):
            first = isinstance(i, int) and i == 0

            def arrived(c):
                if first:
                    pe.wait_ge(sem("turn_lo"), 8 + 2 * (c + 1))
                elif c == 0:
                    pe.wait_ge(sem("r_sg"), i)
                    pe.wait_ge(sem("r_sum_z"), 2 + 4 * (i - 1) - 1)

            def mod(c):
                if c == 1 and not first:
                    pe_mod(pe, A_KV + i - 1)
            project(pe, r_block(i, 0), pair[0], before=arrived, after=mod)
            if not first:
                pe_r_turn(pe, i)

            def v_free(c):
                if c == 0 and not first:
                    pe.wait_ge(sem("r_v"), i)
                    pe.wait_ge(sem("r_sum_z"), 2 + 4 * (i - 1))
            project(pe, r_block(i, 1), pair[1], before=v_free)

            def qk_read(c):
                if c == 0:
                    pe.wait_ge(sem("r_rot"), i + 1)

            def along_gate(c):
                if c == 0:
                    if not first:
                        pe.wait_ge(sem("r_ol"), 2 * i)
                    pe_transposes(pe, turn[0], r_qk, [0, 1]).then_inc(sem("r_qk_turned"), 1)
                    pe_transposes(pe, turn[1], r_qk, [2, 3]).then_inc(sem("r_qk_turned"), 1)
                elif c == 2:
                    pe.wait_ge(sem("r_qT"), i + 1)
                    pe.wait_ge(sem("r_kT"), i + 1)
                    if not first:
                        pe.wait_ge(sem("r_og"), i)
                    for s in range(NT):
                        for k in range(2):
                            mm = pe.matmul(sc[0][:, s * T:(s + 1) * T], r_kT[:, k, s * P:(s + 1) * P],
                                           r_qT[:, k, :], start=k == 0, stop=k == 1)
                    mm.then_inc(sem("r_score"), 1)
                elif c == 3:
                    pe.wait_ge(sem("r_s"), i + 1)
                    pe.wait_ge(sem("r_v"), i + 1)
                    for t in range(NT):
                        for s in range(NT):
                            mm = pe.matmul(sc[t][:, :], r_s[:, s, t * P:(t + 1) * P], r_v[:, s, :],
                                           start=s == 0, stop=s == NT - 1)
                    mm.then_inc(sem("r_o"), 1)
            project(pe, r_block(i, 2), pair[0], before=qk_read, after=along_gate)
            if not first:
                pe_r_output(pe, i)

        def pe_first_block(pe):
            pe.wait_ge(sem("ident_in"), 16)
            turn_groups(pe, 0, lambda j: pe.wait_ge(sem(f"x_in{j // 2}"), 16), False)
            pe_attention(pe, 0)
            with pe.Fori(1, A_KV) as i:
                pe_attention(pe, i)
            pe_a_turn(pe, A_KV)
            pe_a_output(pe, A_KV, lambda c: pe_mod(pe, A_KV - 1) if c == 1 else None)
            pe.wait_ge(sem("mod_read"), A_KV)
            def normalized(j):
                if j % 4 == 0:
                    pe.wait_ge(sem("z_norm"), j // 4 + 1)
                    pe.wait_ge(sem("z_norm1"), j // 4 + 1)
            turn_groups(pe, 1, normalized, False)
            pe_retention(pe, 0)
            with pe.Fori(1, R_HEADS) as i:
                pe_retention(pe, i)
            pe_r_turn(pe, R_HEADS)
            pe_r_output(pe, R_HEADS, lambda c: pe_mod(pe, A_KV + R_HEADS - 1) if c == 1 else None)
            pe.wait_ge(sem("mod_read"), A_KV + R_HEADS)

        def act_attention(act, i, n, rest):
            first = isinstance(i, int) and i == 0
            H = lambda j, c: round_hi(act, a_block(i, j), c, 2 * A_HD if j == 1 else CB)
            H(0, 3)
            for c in range(3):
                H(1, c)
            act.wait_ge(sem("products"), CH * a_block(i, 0) + 4)
            for t in range(NT):
                act.activation(a_sq[:, t, :], pair[0][t][:, :], ACT.Square).then_inc(sem("a_square"), 1)
            if not first:
                act_a_turn(act, i)
            else:
                act_params(act)
            H(1, 3)
            H(2, 0)
            H(2, 1)
            H(2, 2)
            act.wait_ge(sem("products"), CH * a_block(i, 1) + 4)
            if not first:
                act.wait_ge(sem("a_pv"), 4 * i)
            for t in range(NT):
                act.activation(a_v[:, t, :], pair[1][t][:, A_HD:2 * A_HD], ACT.Copy).then_inc(sem("a_v"), 1)
            act.wait_ge(sem("a_qrot"), i + 1)
            for t in range(NT):
                act.activation(a_sq[:, t, 0:A_HD], pair[1][t][:, 0:A_HD], ACT.Square).then_inc(sem("a_square"), 1)
            H(2, 3)
            act.wait_ge(sem("a_qk_turned"), 3 * i + 1)
            act.activation(a_qT[:, 0:2, :], gview(turn[0][:, :], 2), ACT.Copy).then_inc(sem("a_qT_act"), 1)
            round_hi(act, n, 0)

            def probs(h):
                act.wait_ge(sem("a_max"), 4 * i + h + 1)
                for t in range(NT):
                    ins = act.activation(a_p[:, h, t, :], sc[(h + 1) % 2][:, t * T:(t + 1) * T], ACT.Exp,
                                         bias=a_nmax[:, h, t:t + 1], accum_out=a_sum[:, h, t:t + 1])
                ins.then_inc(sem("a_prob"), 1)
            probs(0)
            probs(1)
            round_hi(act, n, 1)
            act.wait_ge(sem("products"), CH * a_block(i, 2) + 4)
            if not first:
                act.wait_ge(sem("a_og"), i)
            for t in range(NT):
                ins = act.activation(a_sg[:, t, :], pair[0][t][:, :], ACT.Silu)
            ins.then_inc(sem("a_sg"), 1)
            round_hi(act, n, 2)

            def turned(h):
                act.wait_ge(sem("a_p_turned"), 4 * i + h + 1)
                act.activation(a_pT[:, 0, :, :], gview(turn[0][:, :], 2), ACT.Copy).then_inc(sem("a_pT0"), 1)
            probs(2)
            probs(3)
            if rest:
                rest[0](3)
            if rest:
                rest[1](0)
            turned(0)
            if rest:
                rest[1](1)
            turned(2)
            if rest:
                rest[1](2)

        def act_a_turn(act, i):
            for b in range(2):
                act.wait_ge(sem("a_turned"), 2 * (i - 1) + b + 1)
                if b == 0 and not (isinstance(i, int) and i == 1):
                    act.wait_ge(sem("a_sum_z"), 2 + 4 * (i - 1))
                act.activation(a_oh[:, 2 * b:2 * b + 2, :], gview(turn[b][:, :], 2), ACT.Copy)\
                    .then_inc(sem("a_oh"), 1)

        def act_params(act):
            act.wait_ge(sem("par_read"), 1)
            act.activation(csilu[:, :], par[:, 32:48], ACT.Silu).then_inc(sem("csilu"), 1)

        def act_retention(act, i, n, rest):
            first = isinstance(i, int) and i == 0
            H = lambda j, c: round_hi(act, r_block(i, j), c)
            H(0, 3)
            for c in range(3):
                H(1, c)
            if not first:
                act_r_turn(act, i)
            H(1, 3)
            H(2, 0)
            H(2, 1)
            H(2, 2)
            if first:
                act_decay_tables(act)
            act.wait_ge(sem("products"), CH * r_block(i, 1) + 4)
            if not first:
                act.wait_ge(sem("r_o"), i)
            for t in range(NT):
                ins = act.activation(r_v[:, t, :], pair[1][t][:, :], ACT.Copy)
            ins.then_inc(sem("r_v"), 1)
            H(2, 3)
            act.wait_ge(sem("r_qk_turned"), 2 * i + 1)
            act.activation(r_qT[:, :, :], gview(turn[0][:, :], 2), ACT.Copy).then_inc(sem("r_qT"), 1)
            round_hi(act, n, 0)
            round_hi(act, n, 1)
            act.wait_ge(sem("products"), CH * r_block(i, 2) + 4)
            if not first:
                act.wait_ge(sem("r_og"), i)
            for t in range(NT):
                ins = act.activation(r_sg[:, t, :], pair[0][t][:, :], ACT.Silu)
            ins.then_inc(sem("r_sg"), 1)
            round_hi(act, n, 2)
            if rest:
                rest[0](3)
                for c in range(3):
                    rest[1](c)

        def act_r_turn(act, i):
            for b in range(2):
                act.wait_ge(sem("r_turned"), 2 * (i - 1) + b + 1)
                if b == 0 and not (isinstance(i, int) and i == 1):
                    act.wait_ge(sem("r_sum_z"), 2 + 4 * (i - 1))
                act.activation(r_oh[:, 2 * b:2 * b + 2, :], gview(turn[b][:, :], 2), ACT.Copy)\
                    .then_inc(sem("r_oh"), 1)

        def act_normalize(act, n, value):
            act.wait_ge(sem("norm_stats"), n)
            for h in range(2):
                act.activation(z[:, 0, h * 1024:(h + 1) * 1024], z[:, 0, h * 1024:(h + 1) * 1024],
                               ACT.Identity, bias=nmr[:, 0:1], scale=rstd[:, 0:1]).then_inc(sem("z_norm"), 1)

        def act_first_block(act):
            act.dma_start(ident[:, :], ident_c).then_inc(sem("ident_in"), 16)
            turn_hi(act, 0, True)
            for c in range(3):
                round_hi(act, 0, c)
            act_decay(act)
            act_attention(act, 0, a_block(1, 0), None)
            act.wait_ge(sem("toep"), 16)
            with act.Fori(1, A_KV) as i:
                act_attention(act, i, a_block(i, 3),
                              [lambda c: round_hi(act, a_block(i, 3), c),
                               lambda c: round_hi(act, a_block(i + 1, 0), c)])
            act_a_turn(act, A_KV)
            round_hi(act, R_B0 - 1, 3)
            for c in range(3):
                round_hi(act, R_B0, c)
            act_normalize(act, 1, 1)
            turn_hi(act, 1, False)
            act_retention(act, 0, r_block(1, 0), None)
            act.wait_ge(sem("rows_used"), 1)
            act_rows(act, 1)
            with act.Fori(1, R_HEADS) as i:
                act_retention(act, i, r_block(i, 3),
                              [lambda c: round_hi(act, r_block(i, 3), c),
                               lambda c: round_hi(act, r_block(i + 1, 0), c)])
            act_r_turn(act, R_HEADS)
            round_hi(act, B_B0 - 1, 3)
            for c in range(3):
                round_hi(act, B_B0, c)

        def act_rows(act, layer):
            act.dma_start(rows[:, 0, :], broadcast_row(ln_gain, layer * D, D)).then_inc(sem("rows1_in"), 16)
            act.dma_start(rows[:, 1, :], broadcast_row(ln_bias, layer * D, D)).then_inc(sem("rows1_in"), 16)

        def act_decay(act):
            act.wait_ge(sem("decay_e_in"), 16)
            act.activation(r_e[:, :], r_e[:, :], ACT.Exp, scale=-float(np.log(2.0))).then_inc(sem("decay_e"), 1)
            act.wait_ge(sem("decay_u"), 1)
            act.activation(r_lg[:, :], r_u[:, :], ACT.Ln).then_inc(sem("decay_e"), 1)

        def act_decay_tables(act):
            for h in range(R_HEADS):
                if h == 0:
                    act.wait_ge(sem("decay_in"), 16 * 4)
                    act.wait_ge(sem("rates"), 1)
                    act.wait_ge(sem("products"), CH * R_B0)
                if h >= 2:
                    act.wait_ge(sem("decay"), h - 1)
                act.activation(r_decay[:, h, :, :], r_pos[:, 0, :, :], ACT.Exp, scale=r_lg[:, h:h + 1])
                act.activation(r_back[:, h % 2, :, :], r_pos[:, 1, :, :], ACT.Exp,
                               scale=r_lg[:, R_HEADS + h:R_HEADS + h + 1]).then_inc(sem("decay_x"), 1)

        vs = Count()

        def vec(ins):
            ins.then_inc(sem("vec"), vs.one())

        def vec_wait(v):
            v.wait_ge(sem("vec"), vs.now())

        def mod_quarter(v, step, m, c):
            n = 8 * step + 4 * m + c
            if c == 0 and not (isinstance(step, int) and step == 0):
                v.wait_ge(sem("mod_cols"), step)
            v.wait_ge(sem(f"mod_in{c % 2}"), 16 * (4 * step + 2 * m + c // 2 + 1))
            for k in range(CH):
                w, cc = m_raw[:, c % 2, k, :], csilu[:, CH * c + k:CH * c + k + 1]
                if c == 0 and k == 0:
                    ins = v.tensor_scalar(m_acc[:, m, :], w, cc, None, ALU.mult)
                else:
                    if k == 0:
                        v.wait_ge(sem("mod_used"), n)
                    else:
                        vec_wait(v)
                    ins = v.scalar_tensor_tensor(out=m_acc[:, m, :], in0=w, scalar=cc,
                                                 in1=m_acc[:, m, :], op0=ALU.mult, op1=ALU.add)
                if k < CH - 1:
                    vec(ins)
            ins.then_inc(sem("mod_used"), 1)

        def mod_read(v, step):
            v.wait_ge(sem("mod_cols"), step + 1)
            v.tensor_tensor(modc[:, bass.ds(8 * step, 8)], turn[0][:, 0:8],
                            bmod[:, bass.ds(8 * step, 8)], ALU.add).then_inc(sem("mod_read"), 1)

        def rotate(v, to, src, tmp, cos, sin, groups, width):
            vec(v.tensor_tensor(gview(to, groups), gview(src, groups), cast(cos, groups), ALU.mult))
            for part in range(2):
                sn = gview(sin, 2)[:, :, part * width:(part + 1) * width]
                vec(v.tensor_tensor(swapped(tmp, groups, width, part), swapped(src, groups, width, 1 - part),
                                    sn.unsqueeze(1).to_broadcast([P, groups, 2, width]), ALU.mult))
            vec_wait(v)
            return v.tensor_tensor(to, to, tmp, ALU.add)

        def vec_params(v):
            v.wait_ge(sem("par_turned"), 1)
            v.tensor_copy(par[:, :], sc[0][:, 0:82]).then_inc(sem("par_read"), 1)
            v.tensor_copy(bmod[:, :], sc[0][:, 128:224])
            for m in range(2):
                v.tensor_copy(conv.rearrange("p f j -> p j f")[:, 2 * m:2 * m + 2, :],
                              gview(sc[0][:, 256 + 128 * m:344 + 128 * m], 2))
            v.wait_ge(sem("par_in"), 16 * 13)
            v.wait_ge(sem("par_turned"), 2)
            v.tensor_tensor(t_out[:, :], sc[1][0:32, 0:TOEP], t_mask[:, :], ALU.add)\
                .then_inc(sem("par_read"), 1)

        def vec_rope_gains(v):
            v.wait_ge(sem("rope_in"), 16 * 6)
            vec(v.tensor_scalar(ropet[:, P:2 * P], ropet[:, P:2 * P], float(A_HD) ** 0.5, None, ALU.mult))
            vec_wait(v)
            q = A_HD // 4
            for m, (cos, sin) in enumerate(((cos_q, sin_q), (cos_k, sin_k))):
                gain = ropet[:, m * P:(m + 1) * P]
                v.tensor_tensor(cos[:, :, :], cos[:, :, :], cast(gain, NT), ALU.mult)
                for part in range(2):
                    sv = sin.rearrange("p t (h s w) -> p t h s w", h=2, s=2)[:, :, :, part, :]
                    gs = gain.rearrange("p (h s w) -> p h s w", h=2, s=2)[:, :, 1 - part, :]
                    vec(v.tensor_tensor(sv, sv, gs.unsqueeze(1).to_broadcast([P, NT, 2, q]), ALU.mult))
            vec_wait(v)

        def vec_attention(v, i, n, rest):
            first = isinstance(i, int) and i == 0
            todo = [(m, c) for m in range(2) for c in range(CH)]

            def M(count=1):
                for _ in range(count):
                    mod_quarter(v, i, *todo.pop(0))
            S_ = lambda j, c: split_lo(v, a_block(i, j), c, 2 * A_HD if j == 1 else CB)
            S_(0, 3)
            for c in range(3):
                S_(1, c)
                if not first:
                    if c == 0:
                        mod_read(v, i - 1)
                    if c < 2:
                        M()
            for kind in range(2):
                w = CB if kind == 0 else A_HD
                cos, sin, to = (cos_q, sin_q, a_q) if kind == 0 else (cos_k, sin_k, a_k)
                heads = w // A_HD
                ss, rs = a_ss[:, kind, :, 0:heads], a_rs[:, kind, :, 0:heads]
                for t in range(NT):
                    v.wait_ge(sem("a_square"), 4 * i + 2 * kind + t + 1)
                    vec(v.tensor_reduce(ss[:, t, :], gview(a_sq[:, t, 0:w], heads), AX, ALU.add))
                vec_wait(v)
                v.tensor_scalar(ss, ss, RMS_EPS * A_HD, None, ALU.add).then_inc(sem("a_var"), 1)
                for t in range(NT):
                    vec(rotate(v, to[:, t, :], pair[kind][t][:, 0:w], ropet[:, 0:w], cos[:, t, :], sin[:, t, :],
                               heads, A_HD // 4))
                    vec_wait(v)
                v.wait_ge(sem("a_rsqrt"), 2 * i + kind + 1)
                for t in range(NT):
                    ins = v.tensor_tensor(gview(to[:, t, :], heads), gview(to[:, t, :], heads),
                                          rs[:, t, :].unsqueeze(2).to_broadcast([P, heads, A_HD]), ALU.mult)
                ins.then_inc(sem("a_qrot" if kind == 0 else "a_krot"), 1)
                if kind == 0:
                    if first:
                        vec_params(v)
                    S_(1, 3)
                    if not first:
                        vec_a_turn(v, i)
                    for c in range(3):
                        S_(2, c)
                        if c == 0 and first:
                            v.wait_ge(sem("csilu"), 1)
                            v.wait_ge(sem("par_read"), 2)
                        if first or c < 2:
                            M()
            S_(2, 3)
            if not first:
                M()
            v.wait_ge(sem("a_qk_turned"), 3 * i + 2)
            v.tensor_copy(a_qT[:, 2:4, :], gview(turn[1][:, :], 2))
            v.wait_ge(sem("a_qk_turned"), 3 * i + 3)
            v.tensor_copy(a_kT[:, :], sc[0][:, 0:T]).then_inc(sem("a_qkT_dve"), 1)
            split_lo(v, n, 0)

            def score_max(h):
                v.wait_ge(sem("a_score"), 4 * i + h + 1)
                v.tensor_reduce(a_nmax[:, h, :], gview(sc[(h + 1) % 2][:, :], NT), AX, ALU.max,
                                negate=True).then_inc(sem("a_max"), 1)

            def turned(h):
                v.wait_ge(sem("a_p_turned"), 4 * i + h + 1)
                v.tensor_copy(a_pT[:, 1, :, :], gview(turn[1][:, :], 2)).then_inc(sem("a_pT1"), 1)
            score_max(0)
            score_max(1)
            split_lo(v, n, 1)
            score_max(2)
            score_max(3)
            split_lo(v, n, 2)
            if rest:
                rest[0](3)
            for c in range(CH):
                if rest:
                    vec_sum(v, "a", 2 + 4 * (i - 1) + c, CH * a_block(i, 3) + c + 1, c)
                    if c:
                        rest[1](c - 1)
                if c in (1, 2):
                    turned(2 * c - 1)
                if c < 3:
                    M()
                elif first:
                    M(2)
            assert not todo
            v.wait_ge(sem("a_prob"), 4 * i + 4)
            vec(v.reciprocal(a_rinv[:, :, :], a_sum[:, :, :]))
            vec_wait(v)
            v.wait_ge(sem("a_pv"), 4 * i + 4)
            v.wait_ge(sem("a_sg"), i + 1)
            for t in range(NT):
                for h in range(4):
                    w = slice(h * A_HD, (h + 1) * A_HD)
                    ins = v.scalar_tensor_tensor(out=a_og[:, t, w], in0=sc[t][:, w], scalar=a_rinv[:, h, t:t + 1],
                                                 in1=a_sg[:, t, w], op0=ALU.mult, op1=ALU.mult)
            ins.then_inc(sem("a_og"), 1)

        def vec_sum(v, which, before, done, c, order=(0, 1, 0, 1)):
            v.wait_ge(sem("products"), done)
            v.wait_ge(sem(which + "_sum_z"), before)
            for t in range(NT):
                ins = v.tensor_tensor(z[:, t, c * CB:(c + 1) * CB], z[:, t, c * CB:(c + 1) * CB],
                                      pair[order[c]][t][:, :], ALU.add)
            ins.then_inc(sem(which + "_sum_z"), 1)

        def vec_a_turn(v, i):
            for b in range(2):
                v.wait_ge(sem("a_oh"), 2 * (i - 1) + b + 1)
                v.tensor_tensor(a_ol[:, 2 * b:2 * b + 2, :], gview(turn[b][:, :], 2),
                                a_oh[:, 2 * b:2 * b + 2, :].bitcast(F32), ALU.subtract).then_inc(sem("a_ol"), 1)

        def vec_r_turn(v, i):
            for b in range(2):
                v.wait_ge(sem("r_oh"), 2 * (i - 1) + b + 1)
                v.tensor_tensor(r_ol[:, 2 * b:2 * b + 2, :], gview(turn[b][:, :], 2),
                                r_oh[:, 2 * b:2 * b + 2, :].bitcast(F32), ALU.subtract).then_inc(sem("r_ol"), 1)

        def vec_retention(v, i, n, rest, between=None):
            todo = [(m, c) for m in range(2) for c in range(CH)]

            def M():
                mod_quarter(v, A_KV + i, *todo.pop(0))
            first = isinstance(i, int) and i == 0
            S_ = lambda j, c: split_lo(v, r_block(i, j), c)
            S_(0, 3)
            for c in range(3):
                S_(1, c)
                if c == 0 and not first:
                    mod_read(v, A_KV + i - 1)
                if c < 2:
                    M()
            v.wait_ge(sem("products"), CH * r_block(i, 0) + 4)
            for t in range(NT):
                ins = rotate(v, r_qk[:, t, :], pair[0][t][:, :], r_t[:, :], cos_r[:, t, :], sin_r[:, t, :],
                             2, R_DK // 4)
                if t == 0:
                    vec(ins)
                    vec_wait(v)
            ins.then_inc(sem("r_rot"), 1)
            S_(1, 3)
            if not first:
                vec_r_turn(v, i)
            for c in range(3):
                S_(2, c)
                M()
            if between:
                between()
            S_(2, 3)
            v.wait_ge(sem("r_qk_turned"), 2 * i + 2)
            v.tensor_copy(r_kT[:, :, :], gview(turn[1][:, :], 2)).then_inc(sem("r_kT"), 1)
            split_lo(v, n, 0)
            v.wait_ge(sem("r_score"), i + 1)
            v.tensor_tensor(r_s[:, :, :], gview(sc[0][:, :], 2),
                            r_decay[:, bass.ds(i, 1), :, :].rearrange("p o t n -> p (o t) n"),
                            ALU.mult).then_inc(sem("r_s"), 1)
            split_lo(v, n, 1)
            M()
            split_lo(v, n, 2)

            def gated():
                v.wait_ge(sem("r_o"), i + 1)
                v.wait_ge(sem("r_sg"), i + 1)
                for t in range(NT):
                    vec(v.bn_stats(r_st[:, t, :], sc[t][:, :]))
                vec_wait(v)
                v.memset(spare[:, :], 0.0)
                for t in range(NT):
                    vec(v.bn_aggr(r_mv[:, t, :], r_st[:, t, :]))
                vec_wait(v)
                v.tensor_scalar(r_var[:, :], r_mv[:, :, 1], LN_EPS, None, ALU.add).then_inc(sem("r_var"), 1)
                v.wait_ge(sem("r_rsqrt"), i + 1)
                for t in range(NT):
                    vec(v.tensor_scalar(r_og[:, t, :], sc[t][:, :], r_mv[:, t, 0:1], r_rs[:, t:t + 1],
                                        ALU.subtract, ALU.mult))
                vec_wait(v)
                ins = v.tensor_tensor(r_og[:, :, :], r_og[:, :, :], r_sg[:, :, :], ALU.mult)
                ins.then_inc(sem("r_og"), 1)
            if rest:
                rest[0](3)
                for c in range(CH):
                    vec_sum(v, "r", 2 + 4 * (i - 1) + c, CH * r_block(i, 3) + c + 1, c)
                    if c:
                        rest[1](c - 1)
                    if c == 1:
                        gated()
                    elif c < 3:
                        M()
            else:
                M()
                gated()
                M()
            assert not todo

        def vec_layer_end(v, which, b, i, n):
            (vec_a_turn if which == "a" else vec_r_turn)(v, i)
            split_lo(v, b, 3)
            for c in range(CH):
                vec_sum(v, which, 2 + 4 * (i - 1) + c, CH * b + c + 1, c)
                v.wait_ge(sem(which + "_sum_z"), 2 + 4 * (i - 1) + c + 1)
                for t in range(NT):
                    ins = v.bn_stats(stats[:, t, c, :], z[:, t, c * CB:(c + 1) * CB])
                vec(ins)
                if c < 2:
                    split_lo(v, b + 1, c)
                if c == 1:
                    mod_read(v, A_KV - 1 if which == "a" else A_KV + R_HEADS - 1)
            vec_wait(v)
            for t in range(NT):
                vec(v.bn_aggr(mv[:, t, :], stats[:, t, :, :]))
            vec_wait(v)
            v.tensor_scalar(var[:, :], mv[:, :, 1], LN_EPS, None, ALU.add).then_inc(sem("var"), 1)
            if which == "r":
                return
            v.wait_ge(sem("rsqrt"), n)
            v.scalar_tensor_tensor(out=nmr[:, :], in0=mv[:, :, 0], scalar=-1.0, in1=rstd[:, :],
                                   op0=ALU.mult, op1=ALU.mult).then_inc(sem("norm_stats"), 1)
            for h in range(2):
                zz = z[:, 1, h * 1024:(h + 1) * 1024]
                v.tensor_scalar(zz, zz, mv[:, 1, 0:1], rstd[:, 1:2], ALU.subtract, ALU.mult)\
                    .then_inc(sem("z_norm1"), 1)

        def vec_decay(v):
            v.wait_ge(sem("decay_e"), 1)
            v.tensor_scalar(r_u[:, :], r_e[:, :], -1.0, 1.0, ALU.mult, ALU.add).then_inc(sem("decay_u"), 1)
            terms = 14
            vec(v.tensor_scalar(r_m[:, :], r_e[:, :], 1.0 / terms, 1.0 / (terms - 1), ALU.mult, ALU.add))
            for k in range(terms - 2, 0, -1):
                vec_wait(v)
                vec(v.tensor_tensor(r_m[:, :], r_m[:, :], r_e[:, :], ALU.mult))
                vec_wait(v)
                vec(v.tensor_scalar(r_m[:, :], r_m[:, :], 1.0 / k, None, ALU.add))
            vec_wait(v)
            vec(v.scalar_tensor_tensor(out=r_m[:, :], in0=r_m[:, :], scalar=-1.0, in1=r_e[:, :],
                                       op0=ALU.mult, op1=ALU.mult))
            v.wait_ge(sem("decay_u"), 1)
            v.wait_ge(sem("decay_e"), 2)
            vec(v.tensor_scalar(r_u[:, :], r_u[:, :], -1.0, 1.0, ALU.mult, ALU.add))
            vec_wait(v)
            vec(v.tensor_scalar(r_u[:, :], r_u[:, :], 1e-7, None, ALU.max))
            vec_wait(v)
            vec(v.reciprocal(r_u[:, :], r_u[:, :]))
            vec_wait(v)
            vec(v.tensor_tensor(r_lg[:, :], r_lg[:, :], r_u[:, :], ALU.mult))
            vec_wait(v)
            vec(v.tensor_tensor(r_lg[:, :], r_lg[:, :], r_e[:, :], ALU.mult))
            vec(v.tensor_scalar(r_n[:, :], r_e[:, :], 0.25, None, ALU.is_lt))
            vec_wait(v)
            vec(v.tensor_tensor(r_m[:, :], r_m[:, :], r_n[:, :], ALU.mult))
            vec(v.tensor_scalar(r_n[:, :], r_n[:, :], -1.0, 1.0, ALU.mult, ALU.add))
            vec_wait(v)
            vec(v.tensor_tensor(r_lg[:, :], r_lg[:, :], r_n[:, :], ALU.mult))
            vec_wait(v)
            v.tensor_tensor(r_lg[:, :], r_lg[:, :], r_m[:, :], ALU.add).then_inc(sem("rates"), 1)

        def vec_decay_tables(v):
            for h in range(R_HEADS):
                v.wait_ge(sem("decay_x"), h + 1)
                v.scalar_tensor_tensor(out=r_decay[:, h, :, :], in0=r_decay[:, h, :, :],
                                       scalar=float(R_DK) ** -0.5, in1=r_back[:, h % 2, :, :],
                                       op0=ALU.mult, op1=ALU.mult).then_inc(sem("decay"), 1)
            v.wait_ge(sem("decay"), R_HEADS)

        def vec_first_block(v):
            vec(v.memset(ones[:, :], 1.0))
            turn_lo(v, 0)
            for c in range(3):
                split_lo(v, 0, c)
            vec_rope_gains(v)
            vec_decay(v)
            vec_attention(v, 0, a_block(1, 0), None)
            with v.Fori(1, A_KV) as i:
                vs.enter(i, 1, VEC_A)
                vec_attention(v, i, a_block(i, 3),
                              [lambda c: split_lo(v, a_block(i, 3), c),
                               lambda c: split_lo(v, a_block(i + 1, 0), c)])
            vs.leave(A_KV - 1)
            vec_layer_end(v, "a", R_B0 - 1, A_KV, 1)
            turn_lo(v, 1, par[:, 0:KC], par[:, KC:2 * KC])
            split_lo(v, R_B0, 2)

            v.wait_ge(sem("decay_in"), 16 * 4)
            vec_retention(v, 0, r_block(1, 0), None, lambda: vec_decay_tables(v))
            with v.Fori(1, R_HEADS) as i:
                vs.enter(i, 1, VEC_R)
                vec_retention(v, i, r_block(i, 3),
                              [lambda c: split_lo(v, r_block(i, 3), c),
                               lambda c: split_lo(v, r_block(i + 1, 0), c)])
            vs.leave(R_HEADS - 1)
            vec_layer_end(v, "r", B_B0 - 1, R_HEADS, 2)

        def broadcast_row(ap, first, n):
            return bass.AP(tensor=ap.tensor, offset=ap.offset + first, ap=[[0, P], [1, n]])

        def by_row(ap, first, n):
            return bass.AP(tensor=ap.tensor, offset=ap.offset + first, ap=[[P, n], [1, P]])

        def by_token(ap):
            return ap.rearrange("(t p) d -> p t d", p=P)

        def sync_first_block(sp):
            for q in range(4):
                sp.dma_start(z[:, :, q * CB:(q + 1) * CB], by_token(x[0])[:, :, q * CB:(q + 1) * CB])\
                    .then_inc(sem(f"x_in{q}"), 16)
            widths = (CB, 2 * A_HD, CB)
            for j in range(3):
                load(sp, a_block(0, j), a_blocks[j](0), widths[j], halves=j == 1)
            with sp.Fori(1, A_KV) as i:
                for j in range(3):
                    load(sp, a_block(i, j), a_blocks[j](i), widths[j], halves=j == 1)
                load(sp, a_block(i, 3), out_rows(w_attn_out, i - 1))
            load(sp, R_B0 - 1, out_rows(w_attn_out, A_KV - 1))
            for j in range(3):
                load(sp, r_block(0, j), r_blocks[j](0), halves=j == 0)
            with sp.Fori(1, R_HEADS) as i:
                for j in range(3):
                    load(sp, r_block(i, j), r_blocks[j](i), halves=j == 0)
                load(sp, r_block(i, 3), out_rows(w_ret_out, i - 1))
            load(sp, B_B0 - 1, out_rows(w_ret_out, R_HEADS - 1))

        def pool_first_block(g):
            def get(to, src, name):
                g.dma_start(to, src).then_inc(sem(name), 16)
            for m in range(2):
                gain = (attn_q_gain, attn_k_gain)[m]
                get(ropet[:, m * P:(m + 1) * P], broadcast_row(gain, 0, P), "rope_in")
                get((cos_q, cos_k)[m][:, :, :], by_token(cos_a_c), "rope_in")
                get((sin_q, sin_k)[m][:, :, :], by_token(sin_a_c), "rope_in")
            get(r_e[:, :], broadcast_row(ret_decay_exp, 0, 16), "decay_e_in")
            get(par_rows[0:16, :], by_row(ln_gain, 0, 16), "par_in")
            get(par_rows[16:32, :], by_row(ln_bias, 0, 16), "par_in")
            get(par_rows[32:48, :], by_row(c_2, 0, 16), "par_in")
            get(par_rows[48:64, :], by_row(norm_attn_2, 0, 16), "par_in")
            get(par_rows[64:80, :], by_row(norm_ffn_2, 0, 16), "par_in")
            get(par_rows[80:82, :], by_row(kv_norm_2, 0, 2), "par_in")
            get(bmod_rows[0:96, :], by_row(b_mod_2, 0, 96), "par_in")
            get(conv_rows[0:88, 0, :], by_row(conv_w_2, 0, 88), "par_in")
            get(conv_rows[0:44, 1, :], by_row(conv_w_2, 2 * FF, 44), "par_in")
            get(conv_rows[44:88, 1, :], by_row(conv_b_2, 0, 44), "par_in")
            get(t_rel[:, :], rel_bias_2, "par_in")
            get(t_hot[:, :], onehot_c, "par_in")
            get(t_mask[:, :], mask_c, "par_in")
            get(rows[:, 0, :], broadcast_row(ln_gain, 0, D), "rows_in")
            get(rows[:, 1, :], broadcast_row(ln_bias, 0, D), "rows_in")

            def mod_load(step, m, c):
                n = 8 * step + 4 * m + c
                if not isinstance(n, int) or n >= 2:
                    g.wait_ge(sem("mod_used"), n - 1)
                g.dma_start(m_raw[:, c % 2, :, :],
                            w_m[:, CH * c:CH * c + CH, bass.ds((2 * step + m) * CB, CB)])\
                    .then_inc(sem(f"mod_in{c % 2}"), 16)

            def loads(step, first, last):
                for n in range(first, last):
                    mod_load(step, n // CH, n % CH)

            def power(to, src, ready, value, done):
                g.wait_ge(sem(ready), value)
                shape = list(src.shape)
                half = minus_half[:, 0:int(np.prod(shape[1:]))]
                if len(shape) == 3:
                    half = half.rearrange("p (a b) -> p a b", a=shape[1])
                g.tensor_tensor(to, src, half, ALU.pow).then_inc(sem(done), 1)

            def a_power(i, kind):
                h = 4 if kind == 0 else 1
                power(a_rs[:, kind, :, 0:h], a_ss[:, kind, :, 0:h], "a_var", 2 * i + kind + 1, "a_rsqrt")

            g.memset(minus_half[:, :], -0.5).then_inc(sem("half_set"), 1)
            g.wait_ge(sem("half_set"), 1)
            loads(0, 0, 2)
            for q in range(4):
                g.wait_ge(sem(f"x_in{q}"), 16)
            g.wait_ge(sem("turned"), 8)
            g.wait_ge(sem("turn_lo"), 8)
            g.tensor_scalar(z[:, :, :], z[:, :, :], ALPHA, None, ALU.mult).then_inc(sem("a_sum_z"), 2)
            a_power(0, 0)
            g.wait_ge(sem("par_read"), 2)
            loads(0, 2, 5)
            get(toep, t_out[:, :].unsqueeze(1).to_broadcast([32, COPIES, TOEP]), "toep")
            a_power(0, 1)
            loads(0, 5, 8)
            loads(1, 0, 2)
            with g.Fori(1, A_KV) as i:
                loads(i, 2, 4)
                a_power(i, 0)
                loads(i, 4, 6)
                a_power(i, 1)
                loads(i, 6, 8)
                loads(i + 1, 0, 2)
            g.wait_ge(sem("a_og"), A_KV)
            g.wait_ge(sem("a_turned"), 2 * A_KV)
            get(cos_r[:, :, :], by_token(cos_r_c), "decay_in")
            get(sin_r[:, :, :], by_token(sin_r_c), "decay_in")
            get(r_pos[:, 0, :, :], by_token(ahead_c), "decay_in")
            get(r_pos[:, 1, :, :], by_token(behind_c), "decay_in")
            power(rstd[:, :], var[:, :], "var", 1, "rsqrt")

            def affine(part):
                if part == 0:
                    g.wait_ge(sem("rows_in"), 32)
                    g.tensor_scalar(rows[:, :, :], rows[:, :, :], ALPHA, None, ALU.mult).then_inc(sem("affine"), 1)
                    return
                t = (part - 1) // 2
                if part == 1:
                    g.wait_ge(sem("turned"), 16)
                    g.wait_ge(sem("z_norm"), 2)
                    g.wait_ge(sem("z_norm1"), 2)
                g.wait_ge(sem("affine"), part)
                ins = g.tensor_tensor(z[:, t, :], z[:, t, :], rows[:, 1 - part % 2, :],
                                      ALU.mult if part % 2 else ALU.add)
                ins.then_inc(sem("affine"), 1)

            def r_step(i, last):
                if isinstance(i, int) and i == 0:
                    for part in range(5):
                        affine(part)
                        loads(A_KV, 2 + part, 3 + part)
                    g.wait_ge(sem("affine"), 5)
                    g.sem_inc(sem("r_sum_z"), 2)
                    g.sem_inc(sem("rows_used"), 1)
                    loads(A_KV, 7, 8)
                else:
                    loads(A_KV + i, 2, 8)
                power(r_rs[:, :], r_var[:, :], "r_var", i + 1, "r_rsqrt")
                if not last:
                    loads(A_KV + i + 1, 0, 2)
            r_step(0, False)
            with g.Fori(1, R_HEADS - 1) as i:
                r_step(i, False)
            r_step(R_HEADS - 1, True)
            power(rstd[:, :], var[:, :], "var", 2, "rsqrt")

        B_STEPS = {1: ["s0", "s1", "s2"], 2: ["t0", "s3", "t1", "s4", "v0"],
                   3: ["s5", "t2", "v1", "s6", "t3", "v2", "s7", "t4", "v3", "t5", "v4", "t6", "v5", "t7",
                       "v6", "v7"]}
        B_ACT_STEPS = {1: ["s0", "s1", "s2"], 2: ["t0", "s3", "t1", "s4"],
                       3: ["t2", "s5", "t3", "s6", "t4", "s7", "t5", "t6", "t7"]}
        HALF = W_HD

        def half(h):
            return slice((h % 2) * HALF, (h % 2 + 1) * HALF)

        def b_out(g):
            return b_q if g == 3 else b_o

        def three(to, fn):
            fn(to[:, 0:P], 0, P)
            return fn(to[:, P:P + T], 1, T)

        def pe_b_step(pe, g, what):
            kind, h = what[0], int(what[1])
            n = 8 * g + h
            if kind == "s":
                pe.wait_ge(sem("b_qT_b"), g + 1)
                pe.wait_ge(sem("b_qT_a"), g + 1)
                if n >= 2:
                    pe.wait_ge(sem("b_read"), n - 1)
                keys = (lambda w: b_kaT[half(h), g, 0:w]) if g < 2 else \
                       (lambda w: b_kBT[half(h), 4 * (g - 2) + h // 2, 0:w])
                mm = three(sc[h % 2], lambda to, t, w: pe.matmul(
                    to, b_qT[half(h), h // 2, t * P:(t + 1) * P], keys(w), start=True, stop=True))
                mm.then_inc(sem("b_score"), 1)
            elif kind == "t":
                pe.wait_ge(sem("b_prob"), n + 1)
                if h < 2 and g > 0:
                    pe.wait_ge(sem("b_ol"), 4 if g == 3 else 2 * g)
                if n >= 2:
                    pe.wait_ge(sem("b_pT"), n - 1)
                for m in range(3):
                    mm = pe.transpose(turn[h % 2][:, m * P:(m + 1) * P], b_s[:, h % 4, m * P:(m + 1) * P],
                                      ident[:, :])
                mm.then_inc(sem("b_p_turned"), 1)
            else:
                pe.wait_ge(sem("b_pT"), n + 1)
                if h == 0 and g > 0:
                    pe.wait_ge(sem("b_og"), g)
                val = (lambda k: b_va[:, k, g * HALF:(g + 1) * HALF]) if g < 2 else \
                      (lambda k: b_vB[:, k, (8 * (g - 2) + h) * HALF:(8 * (g - 2) + h + 1) * HALF])
                col = slice(h * HALF, (h + 1) * HALF)
                pe.matmul(pair[1][0][:, col], b_pT[:, h % 2, 0:P], val(0), start=True, stop=True)
                pe.matmul(pair[1][1][:, col], b_pT[:, h % 2, P:2 * P], val(0), start=True, stop=False)
                pe.matmul(pair[1][1][:, col], b_pT[:, h % 2, 2 * P:3 * P], val(1), start=False, stop=True)\
                    .then_inc(sem("b_pv"), 1)

        def pe_turn_pairs(pe, src, done):
            for b in range(2):
                pe_transposes(pe, turn[b], src, [2 * b, 2 * b + 1]).then_inc(sem(done), 1)

        def pe_b_outT(pe, g):
            pe.wait_ge(sem("b_og"), g + 1)
            if g < 2:
                pe.wait_ge(sem("b_qT_a"), g + 2)
                pe.wait_ge(sem("b_qT_b"), g + 2)
            elif g == 2:
                pe.wait_ge(sem("b_pT"), 32)
            else:
                pe.wait_ge(sem("b_ol"), 6)
            pe_turn_pairs(pe, b_out(g), "b_o_turned")

        def pe_second_attention(pe):
            pe.wait_ge(sem("diag"), 1)
            turn_groups(pe, 2, lambda j: None, True)

            project(pe, B_B0, pair[0], before=lambda c: pe.wait_ge(sem("turn_lo"), 16 + 2 * (c + 1)))

            def gates(c):
                for b in range(2):
                    n = 2 * c + b
                    pe.wait_ge(sem("gate_diag"), n + 1)
                    if n >= 2:
                        pe.wait_ge(sem("gate_row"), n - 1)
                    for m in range(4):
                        mm = pe.matmul(sc[b][:, m * P:(m + 1) * P], ones[:, :], gate_diag[:, b, m, :],
                                       start=True, stop=True)
                    mm.then_inc(sem("gate_mm"), 1)
            def turn_qi0(c):
                if c == 0:
                    pe.wait_ge(sem("i_q"), 1)
                    pe_turn_pairs(pe, i_q, "i_q_turned")
                gates(c)
            project(pe, B_B0 + 1, pair[1], after=turn_qi0)
            project(pe, B_B0 + 2, pair[0], width=80)
            pe.wait_ge(sem("i_q"), 2)
            pe.wait_ge(sem("i_qT_a"), 1)
            pe.wait_ge(sem("i_qT_v"), 1)
            pe_turn_pairs(pe, i_q, "i_q_turned")

            def index(c):
                if c == 0:
                    pe.wait_ge(sem("i_kdup"), 1)
                    pe.wait_ge(sem("gate_row"), 8)
                    pe_transposes(pe, sc[0], i_kdup, [0]).then_inc(sem("i_k_turned"), 1)
                    return
                if c == 1:
                    pe.wait_ge(sem("i_kT"), 1)
                    pe.wait_ge(sem("i_qT_a"), 2)
                    pe.wait_ge(sem("i_qT_v"), 2)
                for h in INDEX_HEADS[c]:
                    if h >= 2:
                        pe.wait_ge(sem("i_relu"), h - 1)
                    three(sc[h % 2], lambda to, t, w: pe.matmul(
                        to, i_qT[half(h), h // 2, t * P:(t + 1) * P], i_kT[half(h), 0:w],
                        start=True, stop=True)).then_inc(sem("i_dot"), 1)
            project(pe, B_B0 + 3, pair[1], after=index)

            def build(c):
                if c == 0:
                    pe.wait_ge(sem("b_kadup"), 1)
                    for kv in range(2):
                        for t in range(NT):
                            mm = pe.transpose(turn[0][:, kv * T + t * P:kv * T + (t + 1) * P],
                                              b_kadup[:, t, kv, :], ident[:, :])
                    mm.then_inc(sem("b_kv_turned"), 1)
                    pe.wait_ge(sem("b_cdiag"), 1)
                    for r in range(2):
                        for t in range(NT):
                            mm = pe.matmul(turn[1][:, r * T + t * P:r * T + (t + 1) * P],
                                           b_kvc[:, t, (2 + r) * P:(3 + r) * P], diag[:, t, :],
                                           start=True, stop=True)
                    mm.then_inc(sem("b_kv_turned"), 1)
                elif c < 3:
                    pe.wait_ge(sem("b_kvT"), 1)
                    pe.wait_ge(sem("b_w_in"), 16 * 4)
                    if c == 2:
                        pe.wait_ge(sem("b_kB_a"), 1)
                        pe.wait_ge(sem("b_kB_v"), 1)
                    for b in range(2):
                        for m in range(2):
                            n = 4 * (c - 1) + 2 * b + m
                            for r in range(2):
                                mm = pe.matmul(turn[b][:, m * T:(m + 1) * T], b_wuk[:, r, n * P:(n + 1) * P],
                                               b_ckvT[:, r, :], start=r == 0, stop=r == 1)
                        mm.then_inc(sem("b_kB"), 1)
                else:
                    pe.wait_ge(sem("b_kB_a"), 2)
                    pe.wait_ge(sem("b_kB_v"), 2)
                    pe.wait_ge(sem("i_relu"), 16)
                    for m in range(4):
                        to = (turn[0], turn[1], sc[0], sc[1])[m]
                        for r in range(2):
                            mm = pe.matmul(to[:, :], b_ckvT[:, r, m // 2 * P:(m // 2 + 1) * P],
                                           b_wuv[:, r, m % 2 * CB:(m % 2 + 1) * CB], start=r == 0, stop=r == 1)
                        mm.then_inc(sem("b_vB_mm"), 1)
            project(pe, B_B0 + 4, pair[0], after=build)

            for g in range(4):
                def steps(c, g=g):
                    if c == 0:
                        pe.wait_ge(sem("b_q"), g + 1)
                        if g == 0:
                            pe.wait_ge(sem("b_vB_a"), 2)
                            pe.wait_ge(sem("b_vB_v"), 2)
                        else:
                            pe.wait_ge(sem("b_pT"), 8 * g)
                        pe_turn_pairs(pe, b_q, "b_q_turned")
                    if c == 1 and 1 <= g <= 2:
                        pe_b_outT(pe, g - 1)
                    for what in B_STEPS.get(c, []):
                        pe_b_step(pe, g, what)
                if g < 3:
                    def q_read(c, g=g):
                        if c == 0:
                            pe.wait_ge(sem("b_q"), g + 1)
                    project(pe, B_B0 + 5 + g, pair[0], before=q_read, after=steps)
                else:
                    def z_read(c):
                        if c == 0:
                            pe.wait_ge(sem("b_ol"), 4)
                            pe.wait_ge(sem("b_q"), 4)
                        else:
                            pe.wait_ge(sem("b_scaled"), c)
                    output(pe, B_B0 + 8, b_oh[:, 0], b_ol[:, 0], [0, 0, 0, 0], z_read, steps)
            for g in range(1, 4):
                def z_read(c, g=g):
                    if c == 0:
                        pe.wait_ge(sem("b_og"), 4)
                        pe.wait_ge(sem("b_ol"), 2 * g + 2)
                    pe.wait_ge(sem("b_scaled"), max(4, 4 * g + c - 1))

                def after(c, g=g):
                    if c == 0 and g < 3:
                        pe_b_outT(pe, g + 1)
                output(pe, B_B0 + 8 + g, b_oh[:, g % 2], b_ol[:, g % 2], [0, 1, 0, 1], z_read, after)

        def f_block(f, j):
            return F_B0 + j if isinstance(f, int) and f == 0 else F_B0 - 1 + 3 * f + j

        def pe_f_output(pe, f, after=None):
            last = isinstance(f, int) and f == FG

            def before(c):
                if c == 0:
                    pe.wait_ge(sem("f_hl"), f)
                    pe.wait_ge(sem("f_u"), f if last else f + 1)
                if c == 1:
                    pe.wait_ge(sem("f_g"), f if last else f + 1)
                if c >= 2:
                    pe.wait_ge(sem("f_scaled"), 2 + 4 * (f - 1) + c - 1)
            output(pe, f_block(f, 0) if last else f_block(f, 2), f_hh, f_hl, [0, 1, 0, 1], before, after)

        def pe_feed_forward(pe, f):
            first = isinstance(f, int) and f == 0

            def u_before(c):
                if first:
                    pe.wait_ge(sem("turn_lo"), 24 + 2 * (c + 1))
                elif c == 0:
                    pe.wait_ge(sem("f_u"), f)
                    pe.wait_ge(sem("f_scaled"), 2 + 4 * (f - 1) - 1)
            project(pe, f_block(f, 0), pair[0], before=u_before)

            def g_before(c):
                if c == 0 and not first:
                    pe.wait_ge(sem("f_g"), f)
                    pe.wait_ge(sem("f_scaled"), 2 + 4 * (f - 1))

            def turn_u(c):
                if c == 0:
                    pe.wait_ge(sem("f_u"), f + 1)
                    if not first:
                        pe.wait_ge(sem("f_conv"), f)
                    pe_turn_pairs(pe, f_u, "f_u_turned")
            project(pe, f_block(f, 1), pair[1], before=g_before, after=turn_u)

            def turn_g(c):
                if c == 0:
                    pe.wait_ge(sem("f_g"), f + 1)
                    if not first:
                        pe.wait_ge(sem("f_h"), f)
                    for b in range(2):
                        pe_transposes(pe, sc[b], f_g, [2 * b, 2 * b + 1]).then_inc(sem("f_g_turned"), 1)
            if first:
                turn_g(0)
            else:
                pe_f_output(pe, f, turn_g)

        def pe_second_block(pe):
            pe_second_attention(pe)
            pe.wait_ge(sem("diag"), 2)
            turn_groups(pe, 3, lambda j: None, True)
            pe_feed_forward(pe, 0)
            with pe.Fori(1, FG) as f:
                pe_feed_forward(pe, f)
            pe_f_output(pe, FG)

        def act_rms(act, n):
            if n == 1:
                for t in range(NT):
                    act.wait_ge(sem("z_full"), t + 1)
                    if t:
                        act.wait_ge(sem("ssq"), t)
                    act.activation(junk[:, :], z[:, t, :], ACT.Square, accum_out=ssq[:, t, 0:1])\
                        .then_inc(sem("ssq"), 1)
                return
            for c in range(CH):
                act.wait_ge(sem("z_full"), NT + CH * (n - 2) + c + 1)
                for t in range(NT):
                    act.activation(junk[:, (2 * c + t) % 4 * CB:((2 * c + t) % 4 + 1) * CB],
                                   z[:, t, c * CB:(c + 1) * CB], ACT.Square, accum_out=ssq[:, t, c:c + 1])\
                        .then_inc(sem("ssq"), 1)
                act.wait_ge(sem("ssq"), NT + NT * CH * (n - 2) + NT * c + NT)

        def act_blocks(act, b, slots, first=None):
            for c in range(CH):
                if first:
                    first(c)
                bb, cc = (b, 3) if c == 0 else (b + 1, c - 1)
                round_hi(act, bb, cc, b_width[bb - B_B0] if bb < F_B0 else CB)
                for task in slots.get(c, []):
                    task()

        def act_second_attention(act):
            act_rms(act, 1)
            turn_hi(act, 2, False)

            def done(b):
                act.wait_ge(sem("products"), CH * (B_B0 + b) + 4)

            def gates(c):
                for b in range(2):
                    n = 2 * c + b
                    act.wait_ge(sem("gate_mm"), n + 1)
                    act.activation(rows[:, n // 4, n % 4 * CB:(n % 4 + 1) * CB], sc[b][:, :], ACT.Copy)\
                        .then_inc(sem("gate_row"), 1)
            act_blocks(act, B_B0, {})

            def qi(n):
                done(n)
                if n == 1:
                    act.wait_ge(sem("i_q_turned"), 2)
                for t in range(NT):
                    ins = act.activation(i_q[:, t, :], pair[n][t][:, :], ACT.Copy)
                ins.then_inc(sem("i_q"), 1)

            def qiT(n):
                act.wait_ge(sem("i_q_turned"), 2 * n + 1)
                act.activation(i_qT[:, 4 * n:4 * n + 2, :], gview(turn[0][:, :], 2), ACT.Copy)\
                    .then_inc(sem("i_qT_a"), 1)
            act_blocks(act, B_B0 + 1, {0: [lambda: qi(0), lambda: qiT(0), lambda: gates(0)],
                                       **{c: [lambda c=c: gates(c)] for c in (1, 2, 3)}})
            act_blocks(act, B_B0 + 2, {0: [lambda: qi(1)]})

            def kiT():
                act.wait_ge(sem("i_k_turned"), 1)
                act.activation(i_kT[:, :], sc[0][:, 0:T], ACT.Copy).then_inc(sem("i_kT"), 1)

            def relu(heads):
                for h in heads:
                    act.wait_ge(sem("i_dot"), h + 1)
                    if h >= 2:
                        act.wait_ge(sem("i_added"), h - 1)
                    act.activation(i_relu[:, h % 2, :], sc[h % 2][:, 0:384], ACT.Relu).then_inc(sem("i_relu"), 1)
            act_blocks(act, B_B0 + 3, {0: [lambda: qiT(1), kiT], 1: [lambda: relu(INDEX_HEADS[1])],
                                       2: [lambda: relu(INDEX_HEADS[2])], 3: [lambda: relu(INDEX_HEADS[3])]})

            def kvc():
                done(3)
                for t in range(NT):
                    act.activation(b_kvc[:, t, :], pair[1][t][:, :], ACT.Copy).then_inc(sem("b_kvc"), 1)
                act.wait_ge(sem("b_kvc"), 2)
                for t in range(NT):
                    act.activation(junk2[:, :], b_kvc[:, t, T:2 * T], ACT.Square, accum_out=ssq[:, t, 1:2])\
                        .then_inc(sem("b_cssq"), 1)
                    act.wait_ge(sem("b_cssq"), t + 1)

            def kB(n):
                act.wait_ge(sem("b_kB"), 2 * n + 1)
                act.activation(b_kBT[:, 4 * n:4 * n + 2, :], gview(turn[0][:, :], 2), ACT.Copy)\
                    .then_inc(sem("b_kB_a"), 1)

            def vB():
                act.wait_ge(sem("i_added"), 16)
                for m in (0, 2):
                    act.wait_ge(sem("b_vB_mm"), m + 1)
                    act.activation(b_vB[:, m // 2, 0:CB], (turn[0], sc[0])[m // 2][:, :], ACT.Copy)\
                        .then_inc(sem("b_vB_a"), 1)
            act_blocks(act, B_B0 + 4, {0: [kvc], 1: [lambda: kB(0)], 2: [lambda: kB(1)], 3: [vB]})
            def queries(g):
                done(4 + g)
                if g == 0:
                    act.wait_ge(sem("b_kadup"), 1)
                    act.wait_ge(sem("b_kv_turned"), 2)
                else:
                    act.wait_ge(sem("b_q_turned"), 2 * g)
                for t in range(NT):
                    ins = act.activation(b_q[:, t, :], pair[0][t][:, :], ACT.Copy, scale=float(W_HD) ** -0.5)
                ins.then_inc(sem("b_q"), 1)
            for g in range(4):
                def start(g=g):
                    if g == 0:
                        queries(0)
                    act.wait_ge(sem("b_q_turned"), 2 * g + 1)
                    act.activation(b_qT[:, 0:2, :], gview(turn[0][:, :], 2), ACT.Copy).then_inc(sem("b_qT_a"), 1)
                    act.wait_ge(sem("b_q_turned"), 2 * g + 2)
                    act.activation(b_qT[:, 2:4, :], gview(turn[1][:, :], 2), ACT.Copy).then_inc(sem("b_qT_b"), 1)

                def turned(h, g=g):
                    act.wait_ge(sem("b_p_turned"), 8 * g + h + 1)
                    act.activation(b_pT[:, h % 2, :], turn[h % 2][:, 0:384], ACT.Copy).then_inc(sem("b_pT"), 1)

                def steps(c, g=g):
                    if c == 3 and g < 3:
                        queries(g + 1)
                    if c == 1 and 1 <= g <= 2:
                        act_b_outT(act, g - 1)
                    for what in B_ACT_STEPS.get(c, []):
                        kind, h = what[0], int(what[1])
                        n = 8 * g + h
                        if kind == "s":
                            act.wait_ge(sem("b_max"), n + 1)
                            for t, w in ((0, slice(0, P)), (1, slice(P, 384))):
                                ins = act.activation(b_s[:, h % 4, w], b_s[:, h % 4, w], ACT.Exp,
                                                     bias=b_nm[:, h, t:t + 1], accum_out=b_sum[:, h, t:t + 1])
                            ins.then_inc(sem("b_prob"), 1)
                        else:
                            turned(h)
                    if c == 3 and g < 2:
                        act.wait_ge(sem("b_esx"), g + 1)
                        act.activation(b_es[:, :, :], b_es[:, :, :], ACT.Exp).then_inc(sem("b_es"), 1)
                act_blocks(act, B_B0 + 5 + g, {0: [start]}, steps)
            for g in range(1, 4):
                act_blocks(act, B_B0 + 8 + g, {0: [lambda g=g: act_b_outT(act, g + 1)]} if g < 3 else {})

        def act_b_outT(act, g):
            if g >= 2:
                act.wait_ge(sem("products"), CH * (B_B0 + 8 + g - 2) + 4)
            for b in range(2):
                act.wait_ge(sem("b_o_turned"), 2 * g + b + 1)
                act.activation(b_oh[:, g % 2, 2 * b:2 * b + 2, :], gview(turn[b][:, :], 2), ACT.Copy)\
                    .then_inc(sem("b_oh"), 1)

        def act_feed_forward(act, f):
            first = isinstance(f, int) and f == 0
            last = isinstance(f, int) and f == FG
            B = [f_block(f, 0), f_block(f, 1), f_block(f, 2)]
            nb = B[1] + 1 if first else B[2] + 1
            if last:
                act_f_hi(act, f)
                round_hi(act, B[0], 3)
                return
            ahead = [(B[0], 3), *((B[1], c) for c in range(4)), *([] if first else ((B[2], c) for c in range(4))),
                     (nb, 0), (nb, 1), (nb, 2)]

            def H(count):
                for _ in range(count):
                    round_hi(act, *ahead.pop(0))
            H(2)
            if not first:
                act_f_hi(act, f)
            H(2)
            act.wait_ge(sem("products"), CH * B[0] + 4)
            if not first:
                act.wait_ge(sem("f_u_turned"), 2 * f)
            for t in range(NT):
                ins = act.activation(f_u[:, t, :], pair[0][t][:, :], ACT.Copy)
            ins.then_inc(sem("f_u"), 1)
            H(2)
            act.wait_ge(sem("f_par"), f + 1)
            if not first:
                act.wait_ge(sem("f_h"), f)
            for k in range(4):
                if k % 2 == 0:
                    act.wait_ge(sem("f_u_turned"), 2 * f + k // 2 + 1)
                ins = act.activation(f_c[:, k, :], turn[k // 2][:, k % 2 * T:(k % 2 + 1) * T], ACT.Identity,
                                     bias=f_par[:, k, 3:4], scale=f_par[:, k, 2:3])
            ins.then_inc(sem("f_tap"), 1)
            H(2)
            act.wait_ge(sem("products"), CH * B[1] + 4)
            if not first:
                act.wait_ge(sem("f_g_turned"), 2 * f)
            for t in range(NT):
                ins = act.activation(f_g[:, t, :], pair[1][t][:, :], ACT.Copy)
            ins.then_inc(sem("f_g"), 1)
            act.wait_ge(sem("f_conv"), f + 1)
            act.activation(f_c[:, :, :], f_c[:, :, :], ACT.Silu).then_inc(sem("f_silu"), 1)
            H(len(ahead))

        def act_f_hi(act, f):
            act.wait_ge(sem("f_h"), f)
            if not (isinstance(f, int) and f == 1):
                act.wait_ge(sem("products"), CH * f_block(f, 0))
            act.activation(f_hh[:, :, :], f_h[:, :, :], ACT.Copy).then_inc(sem("f_hh"), 1)

        def act_second_block(act):
            act_second_attention(act)
            act.wait_ge(sem("b_scaled"), 16)
            act.dma_start(rows[:, 0, :], broadcast_row(norm_final_2, 0, D)).then_inc(sem("final_in"), 16)
            act_rms(act, 2)
            turn_hi(act, 3, False)
            act_feed_forward(act, 0)
            with act.Fori(1, FG) as f:
                act_feed_forward(act, f)
            act_feed_forward(act, FG)
            act_rms(act, 3)
            act.wait_ge(sem("rsqrt"), 5)
            act.wait_ge(sem("zw"), CH)
            for h in range(2):
                w = slice(h * D // 2, (h + 1) * D // 2)
                act.activation(z[:, 0, w], f_zw[:, 0, w], ACT.Copy, scale=rstd[:, 0:1])\
                    .then_inc(sem("final0"), 1)

        def vec_rms(v, n):
            v.wait_ge(sem("ssq"), NT + NT * CH * (n - 1))
            total = ssq[:, :, 0]
            if n > 1:
                vec(v.tensor_reduce(mv[:, :, 0], ssq[:, :, :], AX, ALU.add))
                vec_wait(v)
                total = mv[:, :, 0]
            v.tensor_scalar(var[:, :], total, 1.0 / D, RMS_EPS, ALU.mult, ALU.add).then_inc(sem("var"), 1)
            v.wait_ge(sem("rsqrt"), 2 + n)
            if n < 3:
                for t in range(NT):
                    ins = v.tensor_scalar(diag[:, t, :], ident[:, :], rstd[:, t:t + 1], None, ALU.mult)
                ins.then_inc(sem("diag"), 1)

        def vec_blocks(v, b, slots, first=None):
            for c in range(CH):
                if first:
                    first(c)
                bb, cc = (b, 3) if c == 0 else (b + 1, c - 1)
                split_lo(v, bb, cc, b_width[bb - B_B0] if bb < F_B0 else CB)
                for task in slots.get(c, []):
                    task()

        def vec_scaled_sum(v, which, n, done, c, banks, tmp, row, full=0):
            v.wait_ge(sem("products"), done)
            for t in range(NT):
                ins = v.tensor_tensor(tmp[:, t, :], banks[t][:, :], rows[:, row, c * CB:(c + 1) * CB], ALU.mult)
                if t == 0:
                    vec(ins)
            ins.then_inc(sem(which), 1)
            v.wait_ge(sem(which), n + 1)
            for t in range(NT):
                ins = v.tensor_tensor(z[:, t, c * CB:(c + 1) * CB], z[:, t, c * CB:(c + 1) * CB],
                                      tmp[:, t, :], ALU.add)
                if full and t == NT - 1:
                    ins.then_inc(sem("z_full"), 1)
                    v.wait_ge(sem("z_full"), full)
                else:
                    vec(ins)
            vec_wait(v)

        def vec_second_attention(v):
            v.wait_ge(sem("rows1_in"), 32)
            for t in range(NT):
                vec(v.scalar_tensor_tensor(out=z[:, t, :], in0=z[:, t, :], scalar=mv[:, t, 0:1],
                                           in1=rows[:, 0, :], op0=ALU.subtract, op1=ALU.mult))
                vec_wait(v)
                v.wait_ge(sem("rsqrt"), 2)
                v.scalar_tensor_tensor(out=z[:, t, :], in0=z[:, t, :], scalar=rstd[:, t:t + 1],
                                       in1=rows[:, 1, :], op0=ALU.mult, op1=ALU.add).then_inc(sem("z_full"), 1)
            v.scalar_tensor_tensor(out=aff[:, :], in0=modc[:, KC:2 * KC], scalar=1.0, in1=par[:, 48:64],
                                   op0=ALU.add, op1=ALU.mult).then_inc(sem("aff"), 1)
            vec_rms(v, 1)
            v.wait_ge(sem("aff"), 1)
            turn_lo(v, 2, aff[:, :], modc[:, 0:KC])
            split_lo(v, B_B0, 2)

            def gates(c):
                for b in range(2):
                    n = 2 * c + b
                    first = 2 * KC if n < 4 else 5 * KC
                    if n >= 2:
                        v.wait_ge(sem("gate_mm"), n - 1)
                    v.tensor_tensor(gate_diag[:, b, :, :], cast(ident[:, :], 4),
                                    modc[:, first + n % 4 * 4:first + n % 4 * 4 + 4].unsqueeze(2)
                                    .to_broadcast([P, 4, P]), ALU.mult).then_inc(sem("gate_diag"), 1)
            vec_blocks(v, B_B0, {})

            def qiT(n):
                v.wait_ge(sem("i_q_turned"), 2 * n + 2)
                v.tensor_copy(i_qT[:, 4 * n + 2:4 * n + 4, :], gview(turn[1][:, :], 2)).then_inc(sem("i_qT_v"), 1)
            vec_blocks(v, B_B0 + 1, {0: [lambda: gates(0)], 1: [lambda: qiT(0), lambda: gates(1)],
                                     2: [lambda: gates(2)], 3: [lambda: gates(3)]})
            vec_blocks(v, B_B0 + 2, {})

            def kiwi():
                v.wait_ge(sem("products"), CH * (B_B0 + 2) + 4)
                for t in range(NT):
                    v.tensor_copy(gview(i_kdup[:, t, :], 2), cast(pair[0][t][:, 0:HALF], 2))
                    ins = v.tensor_scalar(b_w[:, t, :], pair[0][t][:, HALF:HALF + 16],
                                          float(W_HD * W_HEADS) ** -0.5, None, ALU.mult)
                ins.then_inc(sem("i_kdup"), 1)

            def added(heads):
                v.wait_ge(sem("i_kdup"), 1)
                v.wait_ge(sem("causal_in"), 16)
                for h in heads:
                    v.wait_ge(sem("i_relu"), h + 1)
                    if h:
                        v.wait_ge(sem("i_added"), h)
                    for t, w in ((0, slice(0, P)), (1, slice(P, 384))):
                        ins = v.scalar_tensor_tensor(out=b_idx[:, w], in0=i_relu[:, h % 2, w],
                                                     scalar=b_w[:, t, h:h + 1], in1=b_idx[:, w],
                                                     op0=ALU.mult, op1=ALU.add)
                    ins.then_inc(sem("i_added"), 1)
            vec_blocks(v, B_B0 + 3, {0: [kiwi, lambda: qiT(1)], 1: [lambda: added(INDEX_HEADS[1])],
                                     2: [lambda: added(INDEX_HEADS[2])], 3: [lambda: added(INDEX_HEADS[3])]})

            def topk(rounds):
                v.wait_ge(sem("i_added"), 16)
                for _ in range(rounds):
                    for t, w in ((0, slice(0, P)), (1, slice(P, 384))):
                        vec(v.max(b_max8[:, t, :], b_idx[:, w]))
                    vec_wait(v)
                    for t, w in ((0, slice(0, P)), (1, slice(P, 384))):
                        vec(v.match_replace(b_idx[:, w], b_max8[:, t, :], b_idx[:, w], -3e38))
                    vec_wait(v)

            def select():
                v.tensor_scalar(b_sel[:, :], b_idx[:, :], -2e38, NEG, ALU.is_gt, ALU.mult).then_inc(sem("sel"), 1)

            def kadup():
                v.wait_ge(sem("b_kvc"), 2)
                for t in range(NT):
                    for kv in range(2):
                        v.tensor_copy(gview(b_kadup[:, t, kv, :], 2),
                                      cast(b_kvc[:, t, kv * HALF:(kv + 1) * HALF], 2))
                v.tensor_copy(b_va[:, :, :], b_kvc[:, :, P:2 * P]).then_inc(sem("b_kadup"), 1)
                v.wait_ge(sem("b_cssq"), 2)
                v.tensor_scalar(b_cvar[:, :], ssq[:, :, 1], 1.0 / RANK, RMS_EPS, ALU.mult, ALU.add)\
                    .then_inc(sem("b_cvar"), 1)
                v.wait_ge(sem("b_crsqrt"), 1)
                for t in range(NT):
                    ins = v.tensor_scalar(diag[:, t, :], ident[:, :], b_crs[:, t:t + 1], None, ALU.mult)
                ins.then_inc(sem("b_cdiag"), 1)

            def kvT():
                v.wait_ge(sem("b_kv_turned"), 2)
                v.tensor_copy(b_kaT[:, :, :], gview(turn[0][:, :], 2))
                for r in range(2):
                    ins = v.tensor_scalar(b_ckvT[:, r, :], turn[1][:, r * T:(r + 1) * T],
                                          par[:, 80 + r:81 + r], None, ALU.mult)
                ins.then_inc(sem("b_kvT"), 1)

            def kB(n):
                v.wait_ge(sem("b_kB"), 2 * n + 2)
                v.tensor_copy(b_kBT[:, 4 * n + 2:4 * n + 4, :], gview(turn[1][:, :], 2)).then_inc(sem("b_kB_v"), 1)

            def vB():
                for m in (1, 3):
                    v.wait_ge(sem("b_vB_mm"), m + 1)
                    v.tensor_copy(b_vB[:, m // 2, CB:2 * CB], (turn[1], sc[1])[m // 2][:, :])\
                        .then_inc(sem("b_vB_v"), 1)
            vec_blocks(v, B_B0 + 4, {0: [kadup, kvT], 1: [lambda: kB(0), lambda: topk(1)],
                                     2: [lambda: kB(1), lambda: topk(1)], 3: [vB, lambda: topk(1)]})

            for g in range(4):
                def start(g=g):
                    if g == 0:
                        v.wait_ge(sem("sink_in"), 16)
                        vec(v.tensor_scalar(b_nsink[:, :], b_sink[:, :], -1.0, None, ALU.mult))
                        topk(2)

                def head(h, g=g):
                    n = 8 * g + h
                    if h == 0:
                        v.wait_ge(sem("bias_in"), 16 * 2 * (P // COPIES) * (g + 1))
                        if g == 2:
                            v.wait_ge(sem("sel"), 1)
                    v.wait_ge(sem("b_score"), n + 1)
                    if n >= 4:
                        v.wait_ge(sem("b_p_turned"), n - 3)
                    s = b_s[:, h % 4, :]
                    v.tensor_tensor(s, sc[h % 2][:, 0:384], b_bias[:, h, :], ALU.add).then_inc(sem("b_read"), 1)
                    v.wait_ge(sem("b_read"), n + 1)
                    if g >= 2:
                        vec(v.tensor_tensor(s, s, b_sel[:, :], ALU.add))
                        vec_wait(v)
                    for t, w in ((0, slice(0, P)), (1, slice(P, 384))):
                        ins = v.tensor_reduce(b_nm[:, h, t:t + 1], s[:, w], AX, ALU.max, negate=True)
                    if g < 2:
                        vec(ins)
                        vec_wait(v)
                        ins = v.tensor_scalar(b_nm[:, h, :], b_nm[:, h, :], b_nsink[:, 8 * g + h:8 * g + h + 1],
                                              None, ALU.min)
                    ins.then_inc(sem("b_max"), 1)

                def steps(c, g=g):
                    if g == 0 and c in (1, 2):
                        topk(1)
                    if g == 1 and c == 1:
                        topk(1)
                        select()
                def finish(g):
                    if g < 2:
                        v.wait_ge(sem("b_max"), 8 * g + 8)
                        v.tensor_tensor(b_es[:, :, :], b_nm[:, :, :],
                                        b_sink[:, 8 * g:8 * g + 8].unsqueeze(2).to_broadcast([P, 8, NT]),
                                        ALU.add).then_inc(sem("b_esx"), 1)
                        v.wait_ge(sem("b_es"), g + 1)
                        vec(v.tensor_tensor(b_ri[:, :, :], b_sum[:, :, :], b_es[:, :, :], ALU.add))
                        vec_wait(v)
                        vec(v.reciprocal(b_ri[:, :, :], b_ri[:, :, :]))
                    else:
                        v.wait_ge(sem("b_prob"), 8 * g + 8)
                        vec(v.reciprocal(b_ri[:, :, :], b_sum[:, :, :]))
                    vec_wait(v)
                    v.wait_ge(sem("b_pv"), 8 * g + 8)
                    if 1 <= g <= 2:
                        v.wait_ge(sem("b_o_turned"), 2 * g)
                    if g == 3:
                        v.wait_ge(sem("b_q_turned"), 8)
                    for t in range(NT):
                        ins = v.tensor_tensor(gview(b_out(g)[:, t, :], 8), gview(pair[1][t][:, :], 8),
                                              b_ri[:, :, t].unsqueeze(2).to_broadcast([P, 8, HALF]), ALU.mult)
                    ins.then_inc(sem("b_og"), 1)

                def before(c, g=g):
                    if g == 3:
                        vec_scaled_sum(v, "b_scaled", c, CH * (B_B0 + 8) + c + 1, c, pair[0], b_tmp, 0)
                    for h in {1: (0, 1, 2), 2: (3, 4), 3: (5, 6, 7)}.get(c, ()):
                        head(h)
                        if h == 0 and 1 <= g <= 2:
                            vec_b_outT(v, g - 1)
                    if c == 3:
                        finish(g)
                vec_blocks(v, B_B0 + 5 + g, {0: [start], **{c: [lambda c=c, s=steps: s(c)] for c in (1, 2, 3)}}, before)
            for g in range(1, 4):
                def slot(c, g=g):
                    vec_scaled_sum(v, "b_scaled", 4 * g + c, CH * (B_B0 + 8 + g) + c + 1, c, pair[c % 2],
                                   b_tmp, 0, NT + c + 1 if g == 3 else 0)
                vec_blocks(v, B_B0 + 8 + g, {0: [lambda g=g: vec_b_outT(v, g + 1)]} if g < 3 else {}, slot)

        def vec_b_outT(v, g):
            for b in range(2):
                v.wait_ge(sem("b_oh"), 2 * g + b + 1)
                v.tensor_tensor(b_ol[:, g % 2, 2 * b:2 * b + 2, :], gview(turn[b][:, :], 2),
                                b_oh[:, g % 2, 2 * b:2 * b + 2, :].bitcast(F32), ALU.subtract)\
                    .then_inc(sem("b_ol"), 1)

        def vec_feed_forward(v, f):
            first = isinstance(f, int) and f == 0
            last = isinstance(f, int) and f == FG
            B = [f_block(f, 0), f_block(f, 1), f_block(f, 2)]
            nb = B[1] + 1 if first else B[2] + 1

            def low():
                v.wait_ge(sem("f_hh"), f)
                v.tensor_tensor(f_hl[:, :, :], f_h[:, :, :], f_hh[:, :, :].bitcast(F32), ALU.subtract)\
                    .then_inc(sem("f_hl"), 1)

            def sum_rows(b, c):
                vec_scaled_sum(v, "f_scaled", 2 + 4 * (f - 1) + c, CH * b + c + 1, c, pair[c % 2], f_y, 1,
                               NT + CH + c + 1 if last else 0)
            if last:
                low()
                split_lo(v, B[0], 3)
                v.wait_ge(sem("final_in"), 16)
                for c in range(CH):
                    sum_rows(B[0], c)
                    for t in range(NT):
                        w = slice(c * CB, (c + 1) * CB)
                        ins = v.tensor_tensor(f_zw[:, t, w], z[:, t, w], rows[:, 0, w], ALU.mult)
                    ins.then_inc(sem("zw"), 1)
                return
            ahead = [(B[0], 3), *((B[1], c) for c in range(4)), *([] if first else ((B[2], c) for c in range(4))),
                     (nb, 0), (nb, 1), (nb, 2)]

            def S_(count=1):
                for _ in range(count):
                    split_lo(v, *ahead.pop(0))
            S_()
            if not first:
                v.wait_ge(sem("f_conv"), f)
            v.tensor_copy(f_par[:, :, :], conv[:, bass.ds(4 * f, 4), :]).then_inc(sem("f_par"), 1)
            S_()
            if not first:
                low()
            S_(3)
            S_()
            v.wait_ge(sem("f_par"), f + 1)
            v.wait_ge(sem("f_tap"), f + 1)
            for tap in (1, 2):
                for k in range(4):
                    src = turn[k // 2][:, k % 2 * T:(k % 2 + 1) * T - tap]
                    ins = v.scalar_tensor_tensor(out=f_c[:, k, tap:], in0=src, scalar=f_par[:, k, 2 - tap:3 - tap],
                                                 in1=f_c[:, k, tap:], op0=ALU.mult, op1=ALU.add)
                    if tap == 1:
                        vec(ins)
                if tap == 1:
                    vec_wait(v)
            ins.then_inc(sem("f_conv"), 1)
            S_(2)
            if not first:
                S_()
                sum_rows(B[2], 0)
            v.wait_ge(sem("f_silu"), f + 1)
            if not first:
                v.wait_ge(sem("f_hh"), f)
                v.wait_ge(sem("f_hl"), f)
            for b in range(2):
                v.wait_ge(sem("f_g_turned"), 2 * f + b + 1)
                ins = v.tensor_tensor(f_h[:, 2 * b:2 * b + 2, :], gview(sc[b][:, :], 2),
                                      f_c[:, 2 * b:2 * b + 2, :], ALU.mult)
            ins.then_inc(sem("f_h"), 1)
            if not first:
                for c in range(1, CH):
                    sum_rows(B[2], c)
                    S_()
            assert not ahead

        def vec_second_block(v):
            vec_second_attention(v)
            v.scalar_tensor_tensor(out=aff[:, :], in0=modc[:, 4 * KC:5 * KC], scalar=1.0, in1=par[:, 64:80],
                                   op0=ALU.add, op1=ALU.mult).then_inc(sem("aff"), 1)
            vec_rms(v, 2)
            v.wait_ge(sem("aff"), 2)
            v.sem_inc(sem("f_scaled"), 2)
            turn_lo(v, 3, aff[:, :], modc[:, 3 * KC:4 * KC])
            vec_feed_forward(v, 0)
            with v.Fori(1, FG) as f:
                vs.enter(f, 1, VEC_F)
                vec_feed_forward(v, f)
            vs.leave(FG - 1)
            vec_feed_forward(v, FG)
            vec_rms(v, 3)
            v.wait_ge(sem("zw"), CH)
            for h in range(2):
                w = slice(h * D // 2, (h + 1) * D // 2)
                v.tensor_scalar(z[:, 1, w], f_zw[:, 1, w], rstd[:, 1:2], None, ALU.mult)\
                    .then_inc(sem("final1"), 1)

        def sync_second_block(sp):
            for j in range(12):
                load(sp, B_B0 + j, b_blocks[j], b_width[j], halves=j == 3)
            for j in range(2):
                load(sp, f_block(0, j), f_blocks[j](0))
            with sp.Fori(1, FG) as f:
                for j in range(2):
                    load(sp, f_block(f, j), f_blocks[j](f))
                load(sp, f_block(f, 2), out_rows(w_f_out, f - 1))
            load(sp, f_block(FG, 0), out_rows(w_f_out, FG - 1))
            for h in range(2):
                for t in range(NT):
                    w = slice(h * D // 2, (h + 1) * D // 2)
                    sp.wait_ge(sem(f"final{t}"), h + 1)
                    sp.dma_start(out[0][t * P:(t + 1) * P, w], z[:, t, w]).then_inc(sem("out"), 16)
            sp.wait_ge(sem("out"), 16 * NT * 2)

        def pool_second_block(g):
            def get(to, src, name):
                g.dma_start(to, src).then_inc(sem(name), 16)

            def power(to, src, ready, value, done):
                g.wait_ge(sem(ready), value)
                g.tensor_tensor(to, src, minus_half[:, 0:NT], ALU.pow).then_inc(sem(done), 1)

            g.wait_ge(sem("r_turned"), 2 * R_HEADS)
            g.wait_ge(sem("r_ol"), 2 * R_HEADS)
            g.wait_ge(sem("products"), CH * B_B0)
            get(b_idx[:, :], causal_c, "causal_in")
            get(b_sink[:, :], broadcast_row(attn_sinks_2, 0, 16), "sink_in")
            for r in range(2):
                for to, src in ((b_wuk, w_uk_2), (b_wuv, w_uv_2)):
                    get(gview(to[:, r, :], W_HEADS),
                        bass.AP(tensor=src.tensor, offset=src.offset + r * P * W_HD,
                                ap=[[W_HD, P], [RANK * W_HD, W_HEADS], [1, W_HD]]), "b_w_in")
            power(rstd[:, :], var[:, :], "var", 3, "rsqrt")
            power(b_crs[:, :], b_cvar[:, :], "b_cvar", 1, "b_crsqrt")
            for grp in range(4):
                if grp:
                    g.wait_ge(sem("b_read"), 8 * grp)
                else:
                    g.wait_ge(sem("b_kv_turned"), 2)
                for band in range(P // COPIES):
                    row = toep.offset + 8 * grp * COPIES * TOEP + P - 1 - band * COPIES
                    rows_of = slice(band * COPIES, (band + 1) * COPIES)
                    get(b_bias[rows_of, :, 0:P],
                        bass.AP(tensor=toep.tensor, offset=row + P,
                                ap=[[TOEP - 1, COPIES], [COPIES * TOEP, 8], [1, P]]), "bias_in")
                    get(b_bias[rows_of, :, P:384],
                        bass.AP(tensor=toep.tensor, offset=row,
                                ap=[[TOEP - 1, COPIES], [COPIES * TOEP, 8], [1, T]]), "bias_in")
            power(rstd[:, :], var[:, :], "var", 4, "rsqrt")
            power(rstd[:, :], var[:, :], "var", 5, "rsqrt")

        block = ctx.enter_context(nc.Block())

        @block.sync
        def _(sp):
            sync_first_block(sp)
            sync_second_block(sp)

        @block.gpsimd
        def _(g):
            pool_first_block(g)
            pool_second_block(g)

        @block.scalar
        def _(act):
            act_first_block(act)
            act_second_block(act)

        @block.vector
        def _(v):
            vec_first_block(v)
            vec_second_block(v)

        @block.tensor
        def _(pe):
            pe_first_block(pe)
            pe_second_block(pe)


NAMES = ["x", "attn_w_in", "attn_q_gain", "attn_k_gain", "attn_w_out", "ret_w_in", "ret_decay_exp",
         "ret_w_out", "ln_gain", "ln_bias", "c_2", "w_mod_2", "b_mod_2", "norm_attn_2", "w_in_2",
         "attn_sinks_2", "kv_norm_2", "w_uk_2", "w_uv_2", "rel_bias_2", "w_out_2", "norm_ffn_2",
         "w_up_2", "conv_w_2", "conv_b_2", "w_down_2", "norm_final_2"]
CONSTANTS = ["ident", "cos_a", "sin_a", "cos_r", "sin_r", "ahead", "behind", "onehot", "mask", "causal"]


def kernel(**inputs):
    import concourse.bacc as _bacc
    from concourse.bass_utils import run_bass_kernel_spmd as _run

    nc = _bacc.Bacc("TRN2", target_bir_lowering=False, num_devices=1)
    arrays, args = {}, []
    constants = shape_constants()
    for name in NAMES + CONSTANTS:
        a = np.ascontiguousarray(inputs[name] if name in inputs else constants[name])
        arrays[f"in_{name}_dram"] = a
        args.append(nc.dram_tensor(f"in_{name}_dram", a.shape, mybir.dt.from_np(a.dtype),
                                   kind="ExternalInput").ap())
    args.append(nc.dram_tensor("out_0_dram", (1, T, D), F32, kind="ExternalOutput").ap())
    build(nc, *args)
    r = _run(nc, [arrays], core_ids=[0])
    return r.results[0]["out_0_dram"]
```
